# Optimizing a Trainium2 kernel written in Bass

```python
import jax, jax.numpy as jnp
from jax import lax
import numpy as np
import math

D_MODEL = 1024
BATCH = 1
SEQ = 256
DEPTH = 1

ATT_Q_HEADS = 8
ATT_KV_HEADS = 2
ATT_HEAD_DIM = 64
WINDOW = 128
ATT_BLOCK = 128
GLA_HEADS = 4
GLA_DK = 64
GLA_DV = 128
GLA_GATE_RANK = 16
GLA_GATE_NORMALIZER = 16.0
GLA_CHUNK = 64
N_EXPERTS = 32
TOP_K = 4
D_EXPERT = 1024
SWIGLU_LIMIT = 7.0
SWIGLU_ALPHA = 1.702
MOE_BLOCK = 128
NORM_EPS = 1e-6

ATT_WIDTH = ATT_Q_HEADS * ATT_HEAD_DIM
ATT_KV_WIDTH = ATT_KV_HEADS * ATT_HEAD_DIM
GLA_K_WIDTH = GLA_HEADS * GLA_DK
GLA_V_WIDTH = GLA_HEADS * GLA_DV
MIX_WIDTH = ATT_WIDTH + GLA_V_WIDTH
IN_SPLITS = (ATT_WIDTH, ATT_KV_WIDTH, ATT_KV_WIDTH, GLA_K_WIDTH, GLA_K_WIDTH, GLA_V_WIDTH, GLA_V_WIDTH, GLA_GATE_RANK)
IN_WIDTH = 2 * ATT_WIDTH + 2 * ATT_KV_WIDTH + 2 * GLA_K_WIDTH + 2 * GLA_V_WIDTH + GLA_GATE_RANK - ATT_WIDTH


def rms_norm(t, g):
    tf = t.astype(jnp.float32)
    tf = tf * lax.rsqrt(jnp.mean(tf * tf, axis=-1, keepdims=True) + NORM_EPS)
    return (tf * g.astype(jnp.float32)).astype(t.dtype)

def split_cols(t, sizes):
    idx = np.cumsum(sizes)[:-1].tolist()
    return jnp.split(t, idx, axis=-1)

def sliding_window_sink_attention(q, k, v, sinks):
    B, S = q.shape[0], q.shape[1]
    nb = S // ATT_BLOCK
    G = ATT_Q_HEADS // ATT_KV_HEADS
    qb = q.reshape(B, nb, ATT_BLOCK, ATT_KV_HEADS, G, ATT_HEAD_DIM)

    def with_prev(t):
        tb = t.reshape(B, nb, ATT_BLOCK, ATT_KV_HEADS, ATT_HEAD_DIM)
        prev = jnp.pad(tb[:, :-1], ((0, 0), (1, 0), (0, 0), (0, 0), (0, 0)))
        return jnp.concatenate([prev, tb], axis=2)

    kb, vb = with_prev(k), with_prev(v)
    scale = ATT_HEAD_DIM ** -0.5
    s = jnp.einsum('bnqhgd,bnkhd->bnhgqk', qb, kb).astype(jnp.float32) * scale
    qi = jnp.arange(ATT_BLOCK)[:, None]
    kj = jnp.arange(2 * ATT_BLOCK)[None, :]
    rel = qi + ATT_BLOCK - kj
    blk = jnp.arange(nb)[:, None, None]
    valid = (rel >= 0) & (rel < WINDOW) & ((blk > 0) | (kj >= ATT_BLOCK))
    s = jnp.where(valid[None, :, None, None], s, -jnp.inf)
    sink = sinks.astype(jnp.float32).reshape(ATT_KV_HEADS, G)[None, None, :, :, None, None]
    m = jnp.maximum(jnp.max(s, axis=-1, keepdims=True), sink)
    p = jnp.exp(s - m)
    p = p / (jnp.sum(p, axis=-1, keepdims=True) + jnp.exp(sink - m))
    o = jnp.einsum('bnhgqk,bnkhd->bnqhgd', p.astype(v.dtype), vb)
    return o.reshape(B, S, ATT_WIDTH)

def gla_chunked(q, k, v, g):
    B, S, H, dk = q.shape
    dv = v.shape[-1]
    C = GLA_CHUNK
    n = S // C
    r = lambda t: t.astype(jnp.float32).reshape(B, n, C, H, t.shape[-1])
    q, k, v, g = r(q), r(k), r(v), r(g)
    b = jnp.cumsum(g, axis=2)
    b_last = b[:, :, -1:]
    b_mid = b[:, :, C // 2 - 1:C // 2]
    A = jnp.einsum('bnihd,bnjhd->bnhij', q * jnp.exp(b - b_mid), k * jnp.exp(b_mid - b))
    causal = jnp.tril(jnp.ones((C, C), dtype=bool))
    A = jnp.where(causal, A, 0.0)
    o = jnp.einsum('bnhij,bnjhv->bnihv', A, v)
    kv = jnp.einsum('bnjhd,bnjhv->bnhdv', k * jnp.exp(b_last - b), v)
    decay = jnp.exp(b_last[:, :, 0])

    def step(state, inp):
        d, u = inp
        return d[..., None] * state + u, state

    _, states = lax.scan(step, jnp.zeros((B, H, dk, dv), jnp.float32),
                         (jnp.moveaxis(decay, 1, 0), jnp.moveaxis(kv, 1, 0)))
    states = jnp.moveaxis(states, 0, 1)
    o = o + jnp.einsum('bnihd,bnhdv->bnihv', q * jnp.exp(b), states)
    return o.reshape(B, S, H, dv)

def hybrid_mixer(h, w_in, w_gla_gate_up, b_gla_gate, g_gla_norm, sinks, w_out):
    B, S, _ = h.shape
    proj = h @ w_in
    aq, ak, av, gq, gk, gv, gg, ga = split_cols(proj, IN_SPLITS)
    att = sliding_window_sink_attention(
        aq.reshape(B, S, ATT_Q_HEADS, ATT_HEAD_DIM),
        ak.reshape(B, S, ATT_KV_HEADS, ATT_HEAD_DIM),
        av.reshape(B, S, ATT_KV_HEADS, ATT_HEAD_DIM), sinks)
    glog = jax.nn.log_sigmoid((ga @ w_gla_gate_up + b_gla_gate).astype(jnp.float32)) / GLA_GATE_NORMALIZER
    o = gla_chunked(gq.reshape(B, S, GLA_HEADS, GLA_DK) * (GLA_DK ** -0.5),
                    gk.reshape(B, S, GLA_HEADS, GLA_DK),
                    gv.reshape(B, S, GLA_HEADS, GLA_DV),
                    glog.reshape(B, S, GLA_HEADS, GLA_DK))
    o = rms_norm(o, g_gla_norm).reshape(B, S, GLA_V_WIDTH).astype(h.dtype) * jax.nn.silu(gg)
    return jnp.concatenate([att.astype(h.dtype), o], axis=-1) @ w_out

def moe_ffn(h, w_router, b_router, w_mlp1, b_mlp1, w_mlp2, b_mlp2):
    T, D = h.shape
    logits = (h @ w_router).astype(jnp.float32) + b_router.astype(jnp.float32)
    top_v, top_i = lax.top_k(logits, TOP_K)
    gates = jax.nn.softmax(top_v, axis=-1)
    n_assign = T * TOP_K
    flat_e = top_i.reshape(-1)
    order = jnp.argsort(flat_e)
    sorted_e = flat_e[order]
    counts = jnp.bincount(flat_e, length=N_EXPERTS)
    padded = (counts + MOE_BLOCK - 1) // MOE_BLOCK * MOE_BLOCK
    start = jnp.cumsum(counts) - counts
    pstart = jnp.cumsum(padded) - padded
    dest = pstart[sorted_e] + jnp.arange(n_assign) - start[sorted_e]
    n_slots = n_assign + N_EXPERTS * MOE_BLOCK
    n_blocks = n_slots // MOE_BLOCK
    slot_assign = jnp.full((n_slots,), n_assign, jnp.int32).at[dest].set(order.astype(jnp.int32))
    slot_tok = slot_assign // TOP_K
    slot_gate = jnp.concatenate([gates.reshape(-1), jnp.zeros((1,), jnp.float32)])[slot_assign]
    block_e = jnp.minimum(jnp.searchsorted(jnp.cumsum(padded), jnp.arange(n_blocks) * MOE_BLOCK, side='right'),
                          N_EXPERTS - 1)
    h_pad = jnp.concatenate([h, jnp.zeros((1, D), h.dtype)], axis=0)
    xs = h_pad[slot_tok].reshape(n_blocks, MOE_BLOCK, D)

    def expert_block(args):
        xb, e = args
        u = xb @ w_mlp1[e] + b_mlp1[e]
        x_glu = jnp.minimum(u[..., ::2], SWIGLU_LIMIT)
        x_lin = jnp.clip(u[..., 1::2], -SWIGLU_LIMIT, SWIGLU_LIMIT)
        a = x_glu * jax.nn.sigmoid(SWIGLU_ALPHA * x_glu) * (x_lin + 1)
        return a @ w_mlp2[e] + b_mlp2[e]

    ys = lax.map(expert_block, (xs, block_e)).reshape(n_slots, D)
    out = jnp.zeros((T + 1, D), jnp.float32).at[slot_tok].add(ys.astype(jnp.float32) * slot_gate[:, None])
    return out[:T].astype(h.dtype)

def first_inputs(seed: int = 0) -> dict:
    key = jax.random.key(seed)
    ks = jax.random.split(key, 24)
    nrm = lambda k, shape, s: jax.random.normal(k, shape, jnp.float32) * s
    L, D, E, F = DEPTH, D_MODEL, N_EXPERTS, D_EXPERT
    return {
        "x": nrm(ks[0], (BATCH, SEQ, D), 1.0),
        "c": nrm(ks[1], (BATCH, D), 1.0),
        "w_ada": nrm(ks[2], (L, D, 6 * D), 0.5 * D ** -0.5),
        "b_ada": nrm(ks[3], (L, 6 * D), 0.02),
        "g_pre_mix": 1.0 + nrm(ks[4], (L, D), 0.02),
        "g_post_mix": 1.0 + nrm(ks[5], (L, D), 0.02),
        "g_pre_ffn": 1.0 + nrm(ks[6], (L, D), 0.02),
        "g_post_ffn": 1.0 + nrm(ks[7], (L, D), 0.02),
        "w_in": nrm(ks[8], (L, D, IN_WIDTH), D ** -0.5),
        "w_gla_gate_up": nrm(ks[9], (L, GLA_GATE_RANK, GLA_K_WIDTH), GLA_GATE_RANK ** -0.5),
        "b_gla_gate": nrm(ks[10], (L, GLA_K_WIDTH), 0.1),
        "g_gla_norm": 1.0 + nrm(ks[11], (L, GLA_DV), 0.02),
        "sinks": nrm(ks[12], (L, ATT_Q_HEADS), 1.0),
        "w_out": nrm(ks[13], (L, MIX_WIDTH, D), MIX_WIDTH ** -0.5),
        "w_router": nrm(ks[14], (L, D, E), D ** -0.5),
        "b_router": nrm(ks[15], (L, E), 0.01),
        "w_mlp1": nrm(ks[16], (L, E, D, 2 * F), D ** -0.5),
        "b_mlp1": nrm(ks[17], (L, E, 2 * F), 0.02),
        "w_mlp2": nrm(ks[18], (L, E, F, D), F ** -0.5),
        "b_mlp2": nrm(ks[19], (L, E, D), 0.02),
    }

def first_block(x, c, w_ada, b_ada, g_pre_mix, g_post_mix, g_pre_ffn, g_post_ffn, w_in, w_gla_gate_up,
              b_gla_gate, g_gla_norm, sinks, w_out, w_router, b_router, w_mlp1, b_mlp1, w_mlp2, b_mlp2):
    B, S, D = x.shape
    for l in range(DEPTH):
        mod = jax.nn.silu(c) @ w_ada[l] + b_ada[l]
        sh1, sc1, gt1, sh2, sc2, gt2 = [m[:, None, :] for m in jnp.split(mod, 6, axis=-1)]
        h = rms_norm(x, g_pre_mix[l]) * (1 + sc1) + sh1
        y = hybrid_mixer(h, w_in[l], w_gla_gate_up[l], b_gla_gate[l], g_gla_norm[l], sinks[l], w_out[l])
        x = x + gt1 * rms_norm(y, g_post_mix[l])
        h = rms_norm(x, g_pre_ffn[l]) * (1 + sc2) + sh2
        y = moe_ffn(h.reshape(B * S, D), w_router[l], b_router[l], w_mlp1[l], b_mlp1[l],
                    w_mlp2[l], b_mlp2[l]).reshape(B, S, D)
        x = x + gt2 * rms_norm(y, g_post_ffn[l])
    return x


HEAD_DIM = 64
NSA_HEADS = 4
NSA_W = NSA_HEADS * HEAD_DIM
NSA_CMP_LEN = 32
NSA_CMP_STRIDE = 16
NSA_CMP_HIDDEN = 256
NSA_SEL_BLOCK = 64
NSA_TOPN = 16
NSA_WINDOW = 512
MOBA_HEADS = 4
MOBA_W = MOBA_HEADS * HEAD_DIM
MOBA_BLOCK = 256
MOBA_TOPK = 3
CONV_CH = 256
CONV_WIDTH = 31
HGRN_HEADS = 4
HGRN_KDIM = 64
HGRN_VDIM = 64
HGRN_W = HGRN_HEADS * HGRN_VDIM
HGRN_CHUNK = 64
MIX_WIDTH_2 = NSA_W + MOBA_W + CONV_CH + HGRN_W
IN_WIDTHS = (NSA_W, HEAD_DIM, HEAD_DIM, HEAD_DIM, HEAD_DIM, HEAD_DIM, HEAD_DIM, 3 * NSA_HEADS,
             MOBA_W, MOBA_W, MOBA_W, 2 * CONV_CH, HGRN_W, HGRN_W, HGRN_W, HGRN_W)
IN_COLS = NSA_W + 6 * HEAD_DIM + 3 * NSA_HEADS + 3 * MOBA_W + 2 * CONV_CH + 4 * HGRN_W
D_FF = 4 * D_MODEL
REL_BUCKETS = 32
REL_MAX_EXACT = 16
REL_MAX_DIST = 128
N_ATTN_HEADS = NSA_HEADS + MOBA_HEADS
Q_BLOCK = 128
LN_EPS = 1e-5
RMS_EPS = 1e-6
BIG = 1e9
DEEPNORM_ALPHA = (2 * DEPTH) ** 0.25
DEEPNORM_BETA = (8 * DEPTH) ** -0.25


def layer_norm(x, g, b):
    xf = x.astype(jnp.float32)
    mu = jnp.mean(xf, -1, keepdims=True)
    var = jnp.mean(jnp.square(xf - mu), -1, keepdims=True)
    return ((xf - mu) * lax.rsqrt(var + LN_EPS)).astype(x.dtype) * g + b

def masked_softmax(s, mask):
    s = jnp.where(mask, s.astype(jnp.float32), -jnp.inf)
    m = jnp.max(s, -1, keepdims=True)
    m = jnp.where(jnp.isfinite(m), m, 0.0)
    p = jnp.where(mask, jnp.exp(s - m), 0.0)
    return p / jnp.maximum(jnp.sum(p, -1, keepdims=True), 1e-30)

def rel_bucket(dist):
    n = jnp.maximum(dist, 0)
    nf = jnp.maximum(n, 1).astype(jnp.float32)
    large = REL_MAX_EXACT + (jnp.log(nf / REL_MAX_EXACT) / math.log(REL_MAX_DIST / REL_MAX_EXACT)
                             * (REL_BUCKETS - REL_MAX_EXACT)).astype(jnp.int32)
    return jnp.where(n < REL_MAX_EXACT, n, jnp.minimum(large, REL_BUCKETS - 1))

def nsa_compress(k, pe, w1, b1, w2):
    B, S, dh = k.shape
    n_cmp = (S - NSA_CMP_LEN) // NSA_CMP_STRIDE + 1
    idx = jnp.arange(n_cmp)[:, None] * NSA_CMP_STRIDE + jnp.arange(NSA_CMP_LEN)[None, :]
    blocks = (k[:, idx] + pe).reshape(B, n_cmp, NSA_CMP_LEN * dh)
    return jax.nn.gelu(blocks @ w1 + b1) @ w2

def nsa_attention(q, kc, vc, ks, vs, kw, vw, gates, tab):
    B, S, H, dh = q.shape
    n_cmp = kc.shape[1]
    n_sel = S // NSA_SEL_BLOCK
    topn = min(NSA_TOPN, n_sel)
    scale = dh ** -0.5
    cmp_start = jnp.arange(n_cmp) * NSA_CMP_STRIDE
    cmp_end = cmp_start + NSA_CMP_LEN - 1
    sel_start = jnp.arange(n_sel) * NSA_SEL_BLOCK
    overlap = jnp.clip(jnp.minimum(cmp_end[:, None] + 1, sel_start[None, :] + NSA_SEL_BLOCK)
                       - jnp.maximum(cmp_start[:, None], sel_start[None, :]), 0, None).astype(jnp.float32) / NSA_CMP_LEN
    kw_pad = jnp.pad(kw, ((0, 0), (NSA_WINDOW, 0), (0, 0)))
    vw_pad = jnp.pad(vw, ((0, 0), (NSA_WINDOW, 0), (0, 0)))
    bi = jnp.arange(B)[:, None, None]
    jsel = jnp.arange(n_sel)

    def block(c):
        s0 = c * Q_BLOCK
        qb = lax.dynamic_slice_in_dim(q, s0, Q_BLOCK, axis=1) * scale
        gb = lax.dynamic_slice_in_dim(gates, s0, Q_BLOCK, axis=1)
        t = s0 + jnp.arange(Q_BLOCK)
        dist_c = t[:, None] - cmp_end[None, :]
        s_c = jnp.einsum('bthd,bnd->bhtn', qb, kc) + tab[:, rel_bucket(dist_c)][None]
        p_c = masked_softmax(s_c, dist_c >= 0)
        o_c = jnp.einsum('bhtn,bnd->bthd', p_c.astype(vc.dtype), vc)
        imp = jnp.einsum('bhtn,nj->btj', p_c, overlap)
        blk_t = t // NSA_SEL_BLOCK
        forced = (jsel[None, :] == 0) | (jsel[None, :] == blk_t[:, None]) | (jsel[None, :] == blk_t[:, None] - 1)
        valid = jsel[None, :] <= blk_t[:, None]
        imp = jnp.where(forced, BIG, jnp.where(valid, imp, -BIG))
        _, sel = lax.top_k(imp, topn)
        pos = (sel[..., None] * NSA_SEL_BLOCK + jnp.arange(NSA_SEL_BLOCK)).reshape(B, Q_BLOCK, topn * NSA_SEL_BLOCK)
        k_sel = ks[bi, pos]
        v_sel = vs[bi, pos]
        dist_s = t[None, :, None] - pos
        s_s = jnp.einsum('bthd,btkd->bhtk', qb, k_sel) + jnp.moveaxis(tab[:, rel_bucket(dist_s)], 0, 1)
        p_s = masked_softmax(s_s, (dist_s >= 0)[:, None])
        o_s = jnp.einsum('bhtk,btkd->bthd', p_s.astype(v_sel.dtype), v_sel)
        kwb = lax.dynamic_slice_in_dim(kw_pad, s0, Q_BLOCK + NSA_WINDOW, axis=1)
        vwb = lax.dynamic_slice_in_dim(vw_pad, s0, Q_BLOCK + NSA_WINDOW, axis=1)
        kpos = s0 - NSA_WINDOW + jnp.arange(Q_BLOCK + NSA_WINDOW)
        dist_w = t[:, None] - kpos[None, :]
        mask_w = (dist_w >= 0) & (dist_w < NSA_WINDOW) & (kpos[None, :] >= 0)
        s_w = jnp.einsum('bthd,bkd->bhtk', qb, kwb) + tab[:, rel_bucket(dist_w)][None]
        p_w = masked_softmax(s_w, mask_w)
        o_w = jnp.einsum('bhtk,bkd->bthd', p_w.astype(vwb.dtype), vwb)
        return gb[..., 0:1] * o_c + gb[..., 1:2] * o_s + gb[..., 2:3] * o_w

    out = lax.map(block, jnp.arange(S // Q_BLOCK))
    return jnp.moveaxis(out, 0, 1).reshape(B, S, H * dh)

def moba_attention(q, k, v, tab):
    B, S, H, dh = q.shape
    s_pad = -(-S // MOBA_BLOCK) * MOBA_BLOCK
    nb = s_pad // MOBA_BLOCK
    ktop = min(MOBA_TOPK, nb)
    scale = dh ** -0.5
    padw = ((0, 0), (0, s_pad - S), (0, 0), (0, 0))
    kbh = jnp.pad(k, padw).reshape(B, nb, MOBA_BLOCK, H, dh).transpose(0, 3, 1, 2, 4)
    vbh = jnp.pad(v, padw).reshape(B, nb, MOBA_BLOCK, H, dh).transpose(0, 3, 1, 2, 4)
    k_mean = jnp.mean(kbh, axis=3)
    bi = jnp.arange(B)[:, None, None, None]
    hi = jnp.arange(H)[None, :, None, None]
    jblk = jnp.arange(nb)

    def block(c):
        s0 = c * Q_BLOCK
        qb = lax.dynamic_slice_in_dim(q, s0, Q_BLOCK, axis=1) * scale
        t = s0 + jnp.arange(Q_BLOCK)
        own = s0 // MOBA_BLOCK
        gate = jnp.einsum('bthd,bhnd->bhtn', qb, k_mean).astype(jnp.float32)
        gate = jnp.where((jblk < own)[None, None, None, :], gate, -BIG)
        gv, sel = lax.top_k(gate, ktop)
        sel_ok = gv > -0.5 * BIG
        k_sel = kbh[bi, hi, sel].reshape(B, H, Q_BLOCK, ktop * MOBA_BLOCK, dh)
        v_sel = vbh[bi, hi, sel].reshape(B, H, Q_BLOCK, ktop * MOBA_BLOCK, dh)
        pos_sel = (sel[..., None] * MOBA_BLOCK + jnp.arange(MOBA_BLOCK)).reshape(B, H, Q_BLOCK, ktop * MOBA_BLOCK)
        bias_sel = tab[hi, rel_bucket(t[None, None, :, None] - pos_sel)]
        s_sel = jnp.einsum('bthd,bhtkd->bhtk', qb, k_sel) + bias_sel
        mask_sel = jnp.repeat(sel_ok, MOBA_BLOCK, axis=-1)
        k_own = lax.dynamic_slice_in_dim(kbh, own, 1, axis=2)[:, :, 0]
        v_own = lax.dynamic_slice_in_dim(vbh, own, 1, axis=2)[:, :, 0]
        pos_own = own * MOBA_BLOCK + jnp.arange(MOBA_BLOCK)
        dist_own = t[:, None] - pos_own[None, :]
        s_own = jnp.einsum('bthd,bhkd->bhtk', qb, k_own) + tab[:, rel_bucket(dist_own)][None]
        mask_own = jnp.broadcast_to(dist_own >= 0, (B, H, Q_BLOCK, MOBA_BLOCK))
        p = masked_softmax(jnp.concatenate([s_sel, s_own], -1), jnp.concatenate([mask_sel, mask_own], -1))
        p_sel = p[..., :ktop * MOBA_BLOCK].astype(v.dtype)
        p_own = p[..., ktop * MOBA_BLOCK:].astype(v.dtype)
        return jnp.einsum('bhtk,bhtkd->bthd', p_sel, v_sel) + jnp.einsum('bhtk,bhkd->bthd', p_own, v_own)

    out = lax.map(block, jnp.arange(S // Q_BLOCK))
    return jnp.moveaxis(out, 0, 1).reshape(B, S, H * dh)

def conformer_conv(u, w_dw, b_dw, ln_g, ln_b, w_pw):
    a, g = jnp.split(u, 2, axis=-1)
    h = a * jax.nn.sigmoid(g)
    h = lax.conv_general_dilated(h, w_dw[:, None, :], window_strides=(1,),
                                 padding=[(CONV_WIDTH - 1, 0)],
                                 dimension_numbers=('NWC', 'WIO', 'NWC'),
                                 feature_group_count=CONV_CH) + b_dw
    h = jax.nn.silu(layer_norm(h, ln_g, ln_b))
    return h @ w_pw

def hgrn2_mixer(q, f_logit, i, g, lb, norm_g):
    B, S, _ = q.shape
    H, dk, dv, C = HGRN_HEADS, HGRN_KDIM, HGRN_VDIM, HGRN_CHUNK
    nc = S // C
    f = lb + (1.0 - lb) * jax.nn.sigmoid(f_logit.astype(jnp.float32))
    log_f = jnp.log(f)
    k = 1.0 - f

    def chunks(a, d):
        return a.astype(jnp.float32).reshape(B, nc, C, H, d).transpose(1, 0, 3, 2, 4)

    causal = jnp.tril(jnp.ones((C, C), dtype=bool))[:, :, None]

    def step(state, inp):
        qc, kc, vc, gc = inp
        cum = jnp.cumsum(gc, axis=2)
        diff = cum[:, :, :, None, :] - cum[:, :, None, :, :]
        decay = jnp.where(causal, jnp.exp(jnp.where(causal, diff, 0.0)), 0.0)
        attn = jnp.einsum('bhtk,bhsk,bhtsk->bhts', qc, kc, decay)
        o = jnp.einsum('bhtk,bhkv->bhtv', qc * jnp.exp(cum), state) + jnp.einsum('bhts,bhsv->bhtv', attn, vc)
        last = cum[:, :, -1:, :]
        state = jnp.exp(last[:, :, 0, :])[..., None] * state + jnp.einsum('bhsk,bhsv->bhkv', kc * jnp.exp(last - cum), vc)
        return state, o

    s_init = jnp.zeros((B, H, dk, dv), jnp.float32)
    _, o = lax.scan(step, s_init, (chunks(q, dk), chunks(k, dk), chunks(i, dv), chunks(log_f, dk)))
    o = o.transpose(1, 0, 3, 2, 4).reshape(B, S, H, dv)
    o = o * lax.rsqrt(jnp.mean(o * o, -1, keepdims=True) + RMS_EPS)
    return o.reshape(B, S, H * dv).astype(q.dtype) * norm_g * jax.nn.sigmoid(g)

def hybrid_layer(x, w_in, cmp_pe, cmp_w1, cmp_b1, cmp_w2, dw_w, dw_b, cln_g, cln_b, pw_w,
                 lb, hn_g, w_out, ln1_g, ln1_b, w_ff1, w_ff2, ln2_g, ln2_b, rel_tab):
    B, S, _ = x.shape
    split_points = [int(v) for v in np.cumsum(IN_WIDTHS)[:-1]]
    h = x @ w_in
    (q_n, kc, vc, ks, vs, kw, vw, g_n, q_m, k_m, v_m, conv_in,
     q_h, f_h, i_h, g_h) = jnp.split(h, split_points, axis=-1)
    kc = nsa_compress(kc, cmp_pe[0], cmp_w1[0], cmp_b1[0], cmp_w2[0])
    vc = nsa_compress(vc, cmp_pe[1], cmp_w1[1], cmp_b1[1], cmp_w2[1])
    gates = jax.nn.sigmoid(g_n.reshape(B, S, NSA_HEADS, 3))
    o_nsa = nsa_attention(q_n.reshape(B, S, NSA_HEADS, HEAD_DIM), kc, vc, ks, vs, kw, vw, gates,
                          rel_tab[:NSA_HEADS])
    o_moba = moba_attention(q_m.reshape(B, S, MOBA_HEADS, HEAD_DIM), k_m.reshape(B, S, MOBA_HEADS, HEAD_DIM),
                            v_m.reshape(B, S, MOBA_HEADS, HEAD_DIM), rel_tab[NSA_HEADS:])
    o_conv = conformer_conv(conv_in, dw_w, dw_b, cln_g, cln_b, pw_w)
    o_hgrn = hgrn2_mixer(q_h, f_h, i_h, g_h, lb, hn_g)
    mixed = jnp.concatenate([o_nsa, o_moba, o_conv, o_hgrn], axis=-1) @ w_out
    x = layer_norm(DEEPNORM_ALPHA * x + mixed, ln1_g, ln1_b)
    ff = jnp.square(jax.nn.relu(x @ w_ff1)) @ w_ff2
    return layer_norm(DEEPNORM_ALPHA * x + ff, ln2_g, ln2_b)

def second_inputs(seed: int = 0) -> dict:
    key = jax.random.key(seed)
    ks = jax.random.split(key, 24)

    def nrm(k, shape, scale):
        return jax.random.normal(k, shape, jnp.float32) * scale

    return {
        'x': nrm(ks[0], (BATCH, SEQ, D_MODEL), 1.0),
        'w_in': nrm(ks[1], (DEPTH, D_MODEL, IN_COLS), D_MODEL ** -0.5),
        'nsa_cmp_pe': nrm(ks[2], (DEPTH, 2, NSA_CMP_LEN, HEAD_DIM), 0.1),
        'nsa_cmp_w1': nrm(ks[3], (DEPTH, 2, NSA_CMP_LEN * HEAD_DIM, NSA_CMP_HIDDEN), (NSA_CMP_LEN * HEAD_DIM) ** -0.5),
        'nsa_cmp_b1': nrm(ks[4], (DEPTH, 2, NSA_CMP_HIDDEN), 0.02),
        'nsa_cmp_w2': nrm(ks[5], (DEPTH, 2, NSA_CMP_HIDDEN, HEAD_DIM), NSA_CMP_HIDDEN ** -0.5),
        'conv_dw_w': nrm(ks[6], (DEPTH, CONV_WIDTH, CONV_CH), CONV_WIDTH ** -0.5),
        'conv_dw_b': nrm(ks[7], (DEPTH, CONV_CH), 0.02),
        'conv_ln_g': 1.0 + nrm(ks[8], (DEPTH, CONV_CH), 0.02),
        'conv_ln_b': nrm(ks[9], (DEPTH, CONV_CH), 0.02),
        'conv_pw_w': nrm(ks[10], (DEPTH, CONV_CH, CONV_CH), CONV_CH ** -0.5),
        'hgrn_lb_logits': nrm(ks[11], (DEPTH, HGRN_HEADS * HGRN_KDIM), 0.5),
        'hgrn_norm_g': 1.0 + nrm(ks[12], (DEPTH, HGRN_W), 0.02),
        'w_out': nrm(ks[13], (DEPTH, MIX_WIDTH_2, D_MODEL), MIX_WIDTH_2 ** -0.5 * DEEPNORM_BETA),
        'ln1_g': 1.0 + nrm(ks[14], (DEPTH, D_MODEL), 0.02),
        'ln1_b': nrm(ks[15], (DEPTH, D_MODEL), 0.02),
        'w_ff1': nrm(ks[16], (DEPTH, D_MODEL, D_FF), D_MODEL ** -0.5),
        'w_ff2': nrm(ks[17], (DEPTH, D_FF, D_MODEL), D_FF ** -0.5 * DEEPNORM_BETA),
        'ln2_g': 1.0 + nrm(ks[18], (DEPTH, D_MODEL), 0.02),
        'ln2_b': nrm(ks[19], (DEPTH, D_MODEL), 0.02),
        'rel_bias': nrm(ks[20], (N_ATTN_HEADS, REL_BUCKETS), 0.5),
    }

def second_block(x, w_in, nsa_cmp_pe, nsa_cmp_w1, nsa_cmp_b1, nsa_cmp_w2, conv_dw_w, conv_dw_b,
              conv_ln_g, conv_ln_b, conv_pw_w, hgrn_lb_logits, hgrn_norm_g, w_out, ln1_g, ln1_b,
              w_ff1, w_ff2, ln2_g, ln2_b, rel_bias):
    lb_sm = jax.nn.softmax(hgrn_lb_logits.astype(jnp.float32), axis=0)
    lbs = (jnp.cumsum(lb_sm, axis=0) - lb_sm[0]).astype(x.dtype)
    for l in range(DEPTH):
        x = hybrid_layer(x, w_in[l], nsa_cmp_pe[l], nsa_cmp_w1[l], nsa_cmp_b1[l], nsa_cmp_w2[l],
                         conv_dw_w[l], conv_dw_b[l], conv_ln_g[l], conv_ln_b[l], conv_pw_w[l],
                         lbs[l], hgrn_norm_g[l], w_out[l], ln1_g[l], ln1_b[l], w_ff1[l], w_ff2[l],
                         ln2_g[l], ln2_b[l], rel_bias)
    return x


_first_inputs = second_inputs


def second_inputs(seed=0):
    import zlib

    import numpy as np

    out = dict(_first_inputs(seed))
    spreads = {}
    factors = {'nsa_cmp_pe': 44.131,
     'nsa_cmp_b1': 200.0,
     'conv_dw_b': 8.0,
     'conv_ln_g': 120.871,
     'conv_ln_b': 108.114,
     'hgrn_norm_g': 155.275,
     'ln1_g': 2.756,
     'ln1_b': 2.761,
     'ln2_g': 24.959,
     'ln2_b': 24.232,
     'rel_bias': 15.267,
     'nsa_cmp_w1': 4.902,
     'nsa_cmp_w2': 2.754}
    for name, (base, spread) in spreads.items():
        noise = np.random.default_rng([zlib.crc32(name.encode()), seed]).standard_normal(out[name].shape)
        drawn = base * np.exp(spread * noise) if base else spread * noise
        out[name] = __import__('jax').numpy.asarray(drawn.astype(out[name].dtype))
    for name, factor in factors.items():
        out[name] = (out[name] * factor).astype(out[name].dtype)
    return out


_narrow_inputs = second_inputs


def second_inputs(seed=0):

    out = dict(_narrow_inputs(seed))
    wider = {'conv_ln_g': 4.4, 'conv_ln_b': 4.41, 'hgrn_norm_g': 4.39, 'ln2_g': 3.3, 'ln2_b': 3.29}
    for name, times in wider.items():
        mean = out[name].mean()
        out[name] = (mean + times * (out[name] - mean)).astype(out[name].dtype)
    return out


RET_HEADS = 4
RET_DK = 256
RET_DV = 256
RET_CHUNK = 128
MLA_HEADS = 8
MLA_NOPE = 128
MLA_ROPE = 64
MLA_V = 128
MLA_Q_LORA = 384
MLA_KV_LORA = 256
ATTN_BLOCK = 128
ROPE_THETA = 10000.0
N_GROUPS = 4
EXPERTS_PER_GROUP = 8
TOP_K_3 = 2
D_EXPERT_3 = 256
EPS = 1e-6

RET_QK_W = RET_HEADS * RET_DK
RET_V_W = RET_HEADS * RET_DV
MLA_V_W = MLA_HEADS * MLA_V
SPLITS = [RET_QK_W, RET_QK_W, RET_V_W, RET_V_W, MLA_Q_LORA, MLA_KV_LORA, MLA_ROPE, D_MODEL, D_MODEL]
IN_W = sum(SPLITS)


def rmsnorm(x, g):
    xf = x.astype(jnp.float32)
    y = xf * lax.rsqrt(jnp.mean(xf * xf, axis=-1, keepdims=True) + EPS)
    return (y * g.astype(jnp.float32)).astype(x.dtype)

def modulate(x, shift, scale):
    return x * (1.0 + scale) + shift

def rope_tables(pos, dim):
    inv = ROPE_THETA ** (-jnp.arange(0, dim, 2, dtype=jnp.float32) / dim)
    ang = pos[:, None] * inv[None, :]
    return jnp.cos(ang), jnp.sin(ang)

def apply_rope(x, cos, sin):
    x1, x2 = jnp.split(x.astype(jnp.float32), 2, axis=-1)
    cos = cos[None, :, None, :]
    sin = sin[None, :, None, :]
    return jnp.concatenate([x1 * cos - x2 * sin, x2 * cos + x1 * sin], axis=-1).astype(x.dtype)

def retention(q, k, v):
    b, s, h, dk = q.shape
    dv = v.shape[-1]
    c = RET_CHUNK
    n = s // c
    log_gamma = jnp.log1p(-jnp.exp2(-5.0 - jnp.arange(h, dtype=jnp.float32)))
    idx = jnp.arange(c, dtype=jnp.float32)
    rel = idx[:, None] - idx[None, :]
    decay_in = jnp.where(rel[None] >= 0, jnp.exp(log_gamma[:, None, None] * jnp.maximum(rel, 0.0)[None]), 0.0)
    xi = jnp.exp(log_gamma[:, None] * (idx[None, :] + 1.0))
    zeta = jnp.exp(log_gamma[:, None] * (c - 1.0 - idx[None, :]))
    chunk_decay = jnp.exp(log_gamma * c)

    def to_chunks(t):
        return t.astype(jnp.float32).reshape(b, n, c, h, t.shape[-1]).transpose(1, 0, 2, 3, 4)

    qc = to_chunks(q)
    kc = to_chunks(k) * (dk ** -0.5)
    vc = to_chunks(v)

    def step(state, inp):
        qi, ki, vi = inp
        scores = jnp.einsum('bihd,bjhd->bhij', qi, ki) * decay_in[None]
        y = jnp.einsum('bhij,bjhe->bihe', scores, vi) + jnp.einsum('bihd,hi,bhde->bihe', qi, xi, state)
        state = state * chunk_decay[None, :, None, None] + jnp.einsum('bjhd,hj,bjhe->bhde', ki, zeta, vi)
        return state, y

    state0 = jnp.zeros((b, h, dk, dv), jnp.float32)
    _, ys = lax.scan(step, state0, (qc, kc, vc))
    return ys.transpose(1, 0, 2, 3, 4).reshape(b, s, h, dv)

def head_norm(y):
    mu = jnp.mean(y, axis=-1, keepdims=True)
    var = jnp.mean(jnp.square(y - mu), axis=-1, keepdims=True)
    return (y - mu) * lax.rsqrt(var + EPS)

def mla(c_q, c_kv, k_pe, q_norm, kv_norm, w_uq, w_ukv, cos, sin):
    b, s, _ = c_q.shape
    q = (rmsnorm(c_q, q_norm) @ w_uq).reshape(b, s, MLA_HEADS, MLA_NOPE + MLA_ROPE)
    q_nope, q_pe = q[..., :MLA_NOPE], q[..., MLA_NOPE:]
    q_pe = apply_rope(q_pe, cos, sin)
    kv = (rmsnorm(c_kv, kv_norm) @ w_ukv).reshape(b, s, MLA_HEADS, MLA_NOPE + MLA_V)
    k_nope, v = kv[..., :MLA_NOPE], kv[..., MLA_NOPE:]
    k_pe = apply_rope(k_pe[:, :, None, :], cos, sin)[:, :, 0, :]
    scale = (MLA_NOPE + MLA_ROPE) ** -0.5
    outs = []
    for blk in range(s // ATTN_BLOCK):
        lo = blk * ATTN_BLOCK
        hi = lo + ATTN_BLOCK
        scores = (jnp.einsum('bqhd,bkhd->bhqk', q_nope[:, lo:hi], k_nope[:, :hi])
                  + jnp.einsum('bqhr,bkr->bhqk', q_pe[:, lo:hi], k_pe[:, :hi])).astype(jnp.float32) * scale
        mask = (lo + jnp.arange(ATTN_BLOCK))[:, None] >= jnp.arange(hi)[None, :]
        p = jax.nn.softmax(jnp.where(mask, scores, -jnp.inf), axis=-1).astype(v.dtype)
        outs.append(jnp.einsum('bhqk,bkhd->bqhd', p, v[:, :hi]))
    return jnp.concatenate(outs, axis=1).reshape(b, s, MLA_V_W)

def token_mixer(u, w_in, w_ret_o, q_norm, kv_norm, w_uq, w_ukv, w_mla_o, w_out, ret_rope, mla_rope):
    b, s, _ = u.shape
    proj = u @ w_in
    offs = np.cumsum(SPLITS)[:-1].tolist()
    rq, rk, rv, rg, c_q, c_kv, k_pe, gate_ret, gate_mla = jnp.split(proj, offs, axis=-1)
    rq = apply_rope(rq.reshape(b, s, RET_HEADS, RET_DK), *ret_rope)
    rk = apply_rope(rk.reshape(b, s, RET_HEADS, RET_DK), *ret_rope)
    rv = rv.reshape(b, s, RET_HEADS, RET_DV)
    y_ret = head_norm(retention(rq, rk, rv)).reshape(b, s, RET_V_W).astype(u.dtype)
    y_ret = (jax.nn.silu(rg) * y_ret) @ w_ret_o
    y_mla = mla(c_q, c_kv, k_pe, q_norm, kv_norm, w_uq, w_ukv, *mla_rope) @ w_mla_o
    merged = jax.nn.sigmoid(gate_ret) * y_ret + jax.nn.sigmoid(gate_mla) * y_mla
    return merged @ w_out

def hier_moe(u, w_grp, b_grp, w_exp, b_exp, w1, w3, w2):
    b, s, d = u.shape
    t = u.reshape(-1, d)
    n_tok = t.shape[0]
    grp_logits = (t @ w_grp).astype(jnp.float32) + b_grp.astype(jnp.float32)
    grp_prob = jax.nn.softmax(grp_logits, axis=-1)
    _, g_sel = lax.top_k(grp_logits, 1)
    p_grp = jnp.take_along_axis(grp_prob, g_sel, axis=-1)
    exp_logits = ((t @ w_exp).astype(jnp.float32) + b_exp.astype(jnp.float32)).reshape(n_tok, N_GROUPS, EXPERTS_PER_GROUP)
    in_grp = jnp.take_along_axis(exp_logits, g_sel[:, :, None], axis=1)[:, 0]
    top_val, top_idx = lax.top_k(in_grp, TOP_K_3)
    top_w = jax.nn.softmax(top_val, axis=-1) * p_grp
    exp_w = jnp.sum(jax.nn.one_hot(top_idx, EXPERTS_PER_GROUP, dtype=jnp.float32) * top_w[..., None], axis=1)
    gate = jax.nn.one_hot(g_sel[:, 0], N_GROUPS, dtype=jnp.float32)[:, :, None] * exp_w[:, None, :]
    out = jnp.zeros_like(t)
    for gi in range(N_GROUPS):
        hid = jax.nn.silu(jnp.einsum('td,edf->tef', t, w1[gi])) * jnp.einsum('td,edf->tef', t, w3[gi])
        hid = hid * gate[:, gi, :, None].astype(hid.dtype)
        out = out + jnp.einsum('tef,efd->td', hid, w2[gi])
    return out.reshape(b, s, d)

def third_inputs(seed: int = 0) -> dict:
    key = jax.random.key(seed)
    ks = jax.random.split(key, 24)
    L = DEPTH
    G, E, F = N_GROUPS, EXPERTS_PER_GROUP, D_EXPERT_3

    def nrm(k, shape, fan_in, scale=1.0):
        return jax.random.normal(k, shape, jnp.float32) * (scale * fan_in ** -0.5)

    def gain(k, shape):
        return 1.0 + 0.02 * jax.random.normal(k, shape, jnp.float32)

    return {
        "x": jax.random.normal(ks[0], (BATCH, SEQ, D_MODEL), jnp.float32),
        "c": jax.random.normal(ks[1], (BATCH, D_MODEL), jnp.float32),
        "w_ada": nrm(ks[2], (L, D_MODEL, 6 * D_MODEL), D_MODEL, 0.5),
        "b_ada": 0.02 * jax.random.normal(ks[3], (L, 6 * D_MODEL), jnp.float32),
        "norm1": gain(ks[4], (L, D_MODEL)),
        "norm2": gain(ks[5], (L, D_MODEL)),
        "w_in": nrm(ks[6], (L, D_MODEL, IN_W), D_MODEL),
        "w_ret_o": nrm(ks[7], (L, RET_V_W, D_MODEL), RET_V_W),
        "q_norm": gain(ks[8], (L, MLA_Q_LORA)),
        "kv_norm": gain(ks[9], (L, MLA_KV_LORA)),
        "w_uq": nrm(ks[10], (L, MLA_Q_LORA, MLA_HEADS * (MLA_NOPE + MLA_ROPE)), MLA_Q_LORA),
        "w_ukv": nrm(ks[11], (L, MLA_KV_LORA, MLA_HEADS * (MLA_NOPE + MLA_V)), MLA_KV_LORA),
        "w_mla_o": nrm(ks[12], (L, MLA_V_W, D_MODEL), MLA_V_W),
        "w_out": nrm(ks[13], (L, D_MODEL, D_MODEL), D_MODEL),
        "w_grp": nrm(ks[14], (L, D_MODEL, G), D_MODEL),
        "b_grp": 0.01 * jax.random.normal(ks[15], (L, G), jnp.float32),
        "w_exp": nrm(ks[16], (L, D_MODEL, G * E), D_MODEL),
        "b_exp": 0.01 * jax.random.normal(ks[17], (L, G * E), jnp.float32),
        "w1": nrm(ks[18], (L, G, E, D_MODEL, F), D_MODEL),
        "w3": nrm(ks[19], (L, G, E, D_MODEL, F), D_MODEL),
        "w2": nrm(ks[20], (L, G, E, F, D_MODEL), F),
        "final_norm": gain(ks[21], (D_MODEL,)),
    }

def third_block(x, c, w_ada, b_ada, norm1, norm2, w_in, w_ret_o, q_norm, kv_norm, w_uq, w_ukv, w_mla_o, w_out,
              w_grp, b_grp, w_exp, b_exp, w1, w3, w2, final_norm):
    s = x.shape[1]
    pos = jnp.arange(s, dtype=jnp.float32)
    ret_rope = rope_tables(pos, RET_DK)
    mla_rope = rope_tables(pos, MLA_ROPE)
    c_act = jax.nn.silu(c)
    h = x
    for l in range(DEPTH):
        mod = (c_act @ w_ada[l] + b_ada[l])[:, None, :]
        sh1, sc1, g1, sh2, sc2, g2 = jnp.split(mod, 6, axis=-1)
        u = modulate(rmsnorm(h, norm1[l]), sh1, sc1)
        h = h + g1 * token_mixer(u, w_in[l], w_ret_o[l], q_norm[l], kv_norm[l], w_uq[l], w_ukv[l],
                                 w_mla_o[l], w_out[l], ret_rope, mla_rope)
        u = modulate(rmsnorm(h, norm2[l]), sh2, sc2)
        h = h + g2 * hier_moe(u, w_grp[l], b_grp[l], w_exp[l], b_exp[l], w1[l], w3[l], w2[l])
    return rmsnorm(h, final_norm)


def setup_inputs(seed=0):
    out = dict(first_inputs(seed))
    for name, value in second_inputs(seed + 1).items():
        if name != "x":
            out[name + "_2"] = value
    for name, value in third_inputs(seed + 2).items():
        if name != "x":
            out[name + "_3"] = value
    return out


def reference(
    x, c, w_ada, b_ada, g_pre_mix, g_post_mix, g_pre_ffn, g_post_ffn, w_in, w_gla_gate_up,
    b_gla_gate, g_gla_norm, sinks, w_out, w_router, b_router, w_mlp1, b_mlp1, w_mlp2, b_mlp2,
    w_in_2, nsa_cmp_pe_2, nsa_cmp_w1_2, nsa_cmp_b1_2, nsa_cmp_w2_2, conv_dw_w_2, conv_dw_b_2,
    conv_ln_g_2, conv_ln_b_2, conv_pw_w_2, hgrn_lb_logits_2, hgrn_norm_g_2, w_out_2, ln1_g_2,
    ln1_b_2, w_ff1_2, w_ff2_2, ln2_g_2, ln2_b_2, rel_bias_2, c_3, w_ada_3, b_ada_3, norm1_3,
    norm2_3, w_in_3, w_ret_o_3, q_norm_3, kv_norm_3, w_uq_3, w_ukv_3, w_mla_o_3, w_out_3,
    w_grp_3, b_grp_3, w_exp_3, b_exp_3, w1_3, w3_3, w2_3, final_norm_3,
):
    x = first_block(
        x, c, w_ada, b_ada, g_pre_mix, g_post_mix, g_pre_ffn, g_post_ffn, w_in, w_gla_gate_up,
        b_gla_gate, g_gla_norm, sinks, w_out, w_router, b_router, w_mlp1, b_mlp1, w_mlp2,
        b_mlp2,
    )
    x = second_block(
        x, w_in_2, nsa_cmp_pe_2, nsa_cmp_w1_2, nsa_cmp_b1_2, nsa_cmp_w2_2, conv_dw_w_2,
        conv_dw_b_2, conv_ln_g_2, conv_ln_b_2, conv_pw_w_2, hgrn_lb_logits_2, hgrn_norm_g_2,
        w_out_2, ln1_g_2, ln1_b_2, w_ff1_2, w_ff2_2, ln2_g_2, ln2_b_2, rel_bias_2,
    )
    return third_block(
        x, c_3, w_ada_3, b_ada_3, norm1_3, norm2_3, w_in_3, w_ret_o_3, q_norm_3, kv_norm_3,
        w_uq_3, w_ukv_3, w_mla_o_3, w_out_3, w_grp_3, b_grp_3, w_exp_3, b_exp_3, w1_3, w3_3,
        w2_3, final_norm_3,
    )


_drawn_inputs = setup_inputs


def setup_inputs(seed=0):
    import zlib

    import numpy as np

    out = dict(_drawn_inputs(seed))
    spreads = {}
    factors = {'g_post_mix': 2.821,
     'g_post_ffn': 5.619,
     'sinks': 3.042,
     'b_mlp1': 4.62,
     'b_mlp2': 5.574,
     'c_3': 8.0,
     'w_ada_3': 8.0,
     'b_ada_3': 8.0,
     'norm1_3': 8.0,
     'norm2_3': 8.0,
     'w_in_3': 8.0,
     'w_ret_o_3': 8.0,
     'q_norm_3': 8.0,
     'kv_norm_3': 8.0,
     'w_uq_3': 8.0,
     'w_ukv_3': 8.0,
     'w_mla_o_3': 8.0,
     'w_out_3': 8.0,
     'w_grp_3': 8.0,
     'b_grp_3': 64.0,
     'w_exp_3': 8.0,
     'b_exp_3': 64.0,
     'w1_3': 8.0,
     'w3_3': 8.0,
     'w2_3': 8.0,
     'final_norm_3': 7.933}
    for name, (base, spread) in spreads.items():
        noise = np.random.default_rng([zlib.crc32(name.encode()), seed]).standard_normal(out[name].shape)
        drawn = base * np.exp(spread * noise) if base else spread * noise
        out[name] = __import__('jax').numpy.asarray(drawn.astype(out[name].dtype))
    for name, factor in factors.items():
        out[name] = (out[name] * factor).astype(out[name].dtype)
    return out
```

```python
from contextlib import ExitStack

import numpy as np

import concourse.bass as bass
from concourse import mybir

F32 = mybir.dt.float32
ALU = mybir.AluOpType
ACT = mybir.ActivationFunctionType
AX = mybir.AxisListType

P = 128
S = 256
NT = S // P
D = 1024
KT = D // P
E1, F1 = 32, 1024
TOP1 = 4
E3, F3, G3, PG3 = 32, 256, 4, 8
TOP3 = 2
NCMP = 15
CONVW = 31
FF2 = 4096
SLOTS = 3
SLAB = 4096
BANK = 512
PBANKS = 3
NEG = -1.0e30
FLOOR = -1.0e20
EXPERT_STEPS = 18
BLK = 16
NBLK = S // BLK

STAGES = [
    ("rel", [], 1), ("ada1", [1] * 12, 0), ("flip", [], 5), ("h1T", [], 4), ("in1", [2, 3, 2, 2, 2], 0), ("gate1", [], 1),
    ("mix1T", [], 4), ("out1", [2, 2], 0), ("h2T", [], 4), ("route1", [], 1), ("gates1T", [], 2), ("bacc1", [], 4),
    ("moe1", None, 0),
    ("x1T", [], 4), ("convw", [], 1), ("in2", [4, 3, 2, 2, 2, 2], 0), ("cmp2", [1, 1], 2), ("convT", [], 1),
    ("convback", [], 1), ("pw2", [], 1), ("mix2T", [], 4), ("out2", [2, 2], 0), ("y2T", [], 4), ("ff1", [2] * 8, 0),
    ("ff2", [1] * 8, 0),
    ("ada3", [1] * 12, 0), ("u1T", [], 4), ("in3", [2] * 10, 0), ("gates3", [2] * 4, 0),
    ("retT", [], 4), ("reto", [2, 2], 0), ("cqT", [], 3), ("uq", [4, 4], 0), ("ukv", [8], 0),
    ("mlaT", [], 4), ("mlao", [2, 2], 0), ("mergeT", [], 4), ("out3", [2, 2], 0),
    ("u2T", [], 4), ("route3", [], 1), ("moe3", None, 0),
]
MOE_PRODUCTS = {"moe1": 12 * E1, "moe3": 6 * E3}
MOE_SLABS = {"moe1": 6 * E1, "moe3": 3 * E3 // 2}


def product_plan():
    first, end, first_slab, release, product, slab = {}, {}, {}, [], 0, 0
    for name, per_slab, extra in STAGES:
        first[name], first_slab[name] = product, slab
        if per_slab is None:
            slab += MOE_SLABS[name]
            release += [name] * MOE_SLABS[name]
        else:
            for n in per_slab:
                product += n
                release.append(product)
                slab += 1
            product += extra
        end[name] = product
    return first, end, first_slab, release


def constants():
    p, j = np.arange(P)[:, None], np.arange(2 * P)[None, :]
    rel = p + P - j
    window = np.where((rel >= 0) & (rel < P), 0.0, NEG)
    causal = np.where(rel >= 0, 0.0, NEG)
    dist = 255 - np.arange(BANK)
    nf = np.maximum(dist, 1).astype(np.float32)
    large = 16 + (np.log(nf / np.float32(16)) / np.float32(np.log(8.0)) * 16).astype(np.int32)
    n = np.maximum(dist, 0)
    bucket = np.where(n < 16, n, np.minimum(large, 31))
    onehot = np.zeros((33, BANK))
    onehot[bucket, np.arange(BANK)] = (dist >= 0)
    onehot[32] = np.where(dist >= 0, 0.0, NEG)
    s = np.arange(P)[:, None, None]
    b = np.arange(P // BLK)[None, :, None]
    i = np.arange(BLK)[None, None, :]
    diag = ((s // BLK == b) & (i >= s % BLK)).reshape(P, P)
    heads2 = np.stack([np.arange(P) < 64, np.arange(P) >= 64], 1)
    e = np.arange(32)
    before = np.broadcast_to((e[None, :] < e[:, None]).reshape(1, -1), (P, 1024))
    log_gamma = np.log1p(-np.exp2(-5.0 - np.arange(4)))
    relT = np.arange(2 * P)[None, :] - np.arange(P)[:, None]
    decay = np.where(relT[:, None, :] >= 0, np.exp(log_gamma[None, :, None] * np.maximum(relT, 0)[:, None, :]), 0.0) / 16.0

    def rope(dim):
        inv = np.float32(10000.0) ** (-np.arange(0, dim, 2, dtype=np.float32) / np.float32(dim))
        ang = inv[:, None].astype(np.float32) * np.arange(S, dtype=np.float32)[None, :]
        return np.cos(ang), np.sin(ang)

    cr, sr = rope(256)
    cm, sm = rope(64)
    ropes = np.stack([cr, sr, np.concatenate([cm, cm, cm, cm]), np.concatenate([-sm, sm, -sm, sm])], 1)
    c = {
        "c_ident": np.eye(P), "c_flip": np.eye(P)[::-1], "c_window": window, "c_causal": causal, "c_onehot": onehot, "c_diag": diag,
        "c_heads2": heads2, "c_before": before, "c_decay": decay.reshape(P, -1), "c_ropes": ropes.reshape(P, -1),
    }
    return {k: np.ascontiguousarray(v, dtype=np.float32) for k, v in c.items()}


PARTS = {("in3", 9): 3, ("uq", 0): 7, ("uq", 1): 7}
VECTORS = ["g_pre_mix", "g_post_mix", "g_pre_ffn", "g_post_ffn", "ln1_g_2", "ln1_b_2", "ln2_g_2", "ln2_b_2",
           "norm1_3", "norm2_3", "final_norm_3"]
GVSLOTS = 3


def landed_plan():
    at, out = [0] * SLOTS, []
    for name, per_slab, _ in STAGES:
        n = MOE_SLABS[name] if per_slab is None else len(per_slab)
        for i in range(n):
            parts = PARTS.get((name, i), 1)
            if name == "moe3" and i % 3 < 2:
                parts = 2
            at[len(out) % SLOTS] += 16 * parts
            out.append(at[len(out) % SLOTS])
    return out


def build(nc, I, out, rel_scratch, dbg=None):
    first, end, first_slab, release = product_plan()
    landed = landed_plan()
    with ExitStack() as ctx:
        def sb(name, shape):
            return ctx.enter_context(nc.sbuf_tensor(name, shape, F32))

        def sem(name):
            return ctx.enter_context(nc.semaphore(name))

        ring = sb("ring", [P, SLOTS, SLAB])
        X = sb("X", [P, NT, D])
        H = sb("H", [P, NT, D])
        HT = sb("HT", [P, KT, S])
        Y = sb("Y", [P, NT, D])
        MOD = sb("MOD", [P, 6, D])
        GV = sb("GV", [P, GVSLOTS, D])
        BD = sb("BD", [P, 4, 2, S])
        QD = sb("QD", [P, 2, NBLK, 2, BLK])
        KC = sb("KC", [P, 2, NCMP])
        BIAS = sb("BIAS", [P, 8, S])
        BIASC = sb("BIASC", [P, NT, 4, NCMP])
        decay = BIAS[:, 0:4, :]
        ropes = BIAS[:, 4:8, :]
        ident = sb("ident", [P, P])
        window = sb("window", [P, S])
        causal = sb("causal", [P, S])
        diag = sb("diag", [P, P])
        heads2 = sb("heads2", [P, 2])
        ones = sb("ones", [P, S])
        wr1 = sb("wr1", [P, KT, E1])
        wr3 = sb("wr3", [P, KT, G3 + E3])
        wgu = sb("wgu", [16, S])
        rows = sb("rows", [P, 1920])
        cols = sb("cols", [P, 128])
        stat = sb("stat", [P, 256])
        scr = sb("scr", [P, 13312])
        ps = ctx.enter_context(nc.psum_tensor("ps", [P, 8, BANK], F32))

        def shaped(v, shape):
            names = "abcd"[:len(shape)]
            if len(shape) == 1:
                return v
            return v.rearrange(f"p ({' '.join(names)}) -> p {' '.join(names)}",
                               **{k: s for k, s in zip(names, shape)})

        def carve(base, *shape):
            n = int(np.prod(shape))
            assert base + n <= 13312, (base, shape)
            return shaped(scr[:, base:base + n], shape)

        b_router, b_route3 = rows[:, 0:32], rows[:, 32:68]
        qn_row, kvn_row = rows[:, 128:512], rows[:, 512:768]
        gla_norm, sinks = rows[:, 768:896], rows[:, 896:904]
        conv_g, conv_b, hgrn_g = rows[:, 1024:1280], rows[:, 1280:1536], rows[:, 1536:1792]
        cvec = shaped(cols[:, 0:16], (2, KT))
        b_gate = cols[:, 16:18]
        conv_bias = cols[:, 18:20]
        cmp_b1 = shaped(cols[:, 20:24], (2, 2))
        tab = cols[0:33, 24:32]
        cmp_pe = shaped(cols[:, 32:64], (2, 16))
        csil = shaped(cols[:, 64:80], (2, KT))
        var, std, rstd = stat[:, 64:80], stat[:, 80:96], stat[:, 96:112]
        moment = stat[:, 0:64]
        bnst = stat[:, 128:140]
        att_stat = [{n: stat[:, 144 + 32 * b + 4 * i:148 + 32 * b + 4 * i]
                     for i, n in enumerate(("max", "shift", "sum", "inv", "sink"))} for b in range(2)]
        ada_rows = [Y[0:12, 0, 0:BANK], Y[0:12, 0, 0:BANK]]
        relv = Y[0:8, 1, 0:BANK]
        onehot = Y[0:33, 1, BANK:2 * BANK]

        slab_landed = [sem(f"slab_landed{i}") for i in range(SLOTS)]
        product_ready, product_free = sem("product_ready"), sem("product_free")
        consts_landed = sem("consts_landed")
        vec_landed = [sem(f"vec_landed{i}") for i in range(GVSLOTS)]
        vec_used = sem("vec_used")
        zeros_ready = sem("zeros_ready")
        rel_stored, rel_landed = sem("rel_stored"), sem("rel_landed")
        ada3_landed, moe1_params_landed = sem("ada3_landed"), sem("moe1_params_landed")
        block2_params_landed, tables_landed, before_landed = sem("block2_params"), sem("tables"), sem("before_landed")
        x_landed, stored = sem("x_landed"), sem("stored")
        dve_step, act_step = sem("dve_step"), sem("act_step")
        var_ready, std_ready = sem("var_ready"), sem("std_ready")
        cond_ready, h1_ready, abs_ready, glog_ready, loglog_ready = (sem(n) for n in (
            "cond_ready", "h1_ready", "abs_ready", "glog_ready", "loglog_ready"))
        mix_ready, h2_ready, route_shift, route_exp, gates_ready = (sem(n) for n in (
            "mix_ready", "h2_ready", "route_shift", "route_exp", "gates_ready"))
        moe_product_ready, moe_product_free, glu_ready, sig_ready, hidden_ready = (sem(n) for n in (
            "moe_product_ready", "moe_product_free", "glu_ready", "sig_ready", "hidden_ready"))
        x1_ready, blocks_ready, conv_ready, convln_ready, keep_ready, log_ready = (sem(n) for n in (
            "x1_ready", "blocks_ready", "conv_ready", "convln_ready", "keep_ready", "log_ready"))
        y2_ready, relu_ready, x2_ready, u1_ready, cq_ready, rope_ready = (sem(n) for n in (
            "y2_ready", "relu_ready", "x2_ready", "u1_ready", "cq_ready", "rope_ready"))
        ret_scores, ret_decayed, ret_out, ret_copied, ret_ready, mlarope_ready = (sem(n) for n in (
            "ret_scores", "ret_decayed", "ret_out", "ret_copied", "ret_ready", "mlarope_ready"))
        ret_gated, merge_ready, u2_ready, final_ready, mla_ready, convsilu_ready = (sem(n) for n in (
            "ret_gated", "merge_ready", "u2_ready", "final_ready", "mla_ready", "convsilu_ready"))
        att = {n: sem("att_" + n) for n in (
            "scores", "scores_read", "shift", "probs", "turned", "turned_copied", "out", "out_read", "sink")}
        lin = {n: sem("lin_" + n) for n in (
            "cum", "qdiff", "qexp", "queries", "kexp", "keys", "keys_used", "ddiff", "dexp", "diag", "diag_used", "tiles",
            "merged", "out", "read")}

        sS, sP, sPT = carve(6400, 4, S), carve(7424, 4, S), carve(8448, 2, 4, P)
        BIASR, BIASCR, flip = carve(0, 8, S), carve(2048, NT, 4, NCMP), carve(2304, P)
        Q1, AV = carve(0, 4, S), carve(1024, NT, P)
        GQ, GK = carve(1280, 2, S), carve(1792, 2, S)
        GVV, GG = carve(2304, NT, BANK), carve(3328, NT, BANK)
        GA, GZ, GL, CUM = carve(4352, S), carve(4608, 2, S), carve(5120, 2, S), carve(5632, 2, S)
        b1row, b2row = scr[0:E1, 0:2 * F1], scr[0:E1, 2560:3584]
        b1T = carve(2048, 16, E1)
        LG, GT, LX = carve(3584, NT, E1), carve(3648, NT, E1), carve(3712, NT, E1)
        gatesT = scr[0:E1, 3776:4032]
        aT = carve(4032, KT, S)
        glu, lnr, sig = carve(8128, 2, S), carve(8640, 2, S), carve(9152, 2, S)
        cmp1, cmp2, before = carve(9664, 32, 32), carve(10688, 32, 32), carve(11776, 32, 32)
        b1cur, gcur = carve(11712, 16), carve(11728, NT)
        GLA_KD, GLA_LD = carve(10496, 2, 2, S), carve(6400, BLK, S)
        LQ = carve(11520, 2, NBLK, BLK)
        GLA_AT, NCUM1 = (carve(12032, 4, S), carve(4608, 4, P)), carve(5120, 2, S)
        Q2, QM = carve(0, 2, S), carve(512, 2, S)
        VS, VW, VM = carve(1024, NT, 64), carve(1152, NT, 64), carve(1280, NT, S)
        GN = carve(1792, NT, 12)
        KCT, BLOCKS, CHID = carve(1824, 2, S), carve(2336, 2, 16, NCMP), carve(2816, 2, 2, NCMP)
        VC = carve(2880, 64)
        cw2 = shaped(MOD[:, 0, 0:256], (2, 2, 64))
        pww = shaped(MOD[:, 0, 256:768], (2, S))
        convrow = MOD[0:CONVW, 0, 768:1024]
        convw = carve(2944, 2, 32)
        CA, CG, CACC = carve(3520, 2, CONVW - 1 + S), carve(4096, 2, S), carve(4608, 2, S)
        CTOK, CSIL = carve(5120, NT, S), carve(5632, 2, S)
        QH, FH, IH, GH = carve(9472, 2, S), carve(9984, 2, S), carve(10496, NT, S), carve(11008, NT, S)
        HCUM, HLOG = carve(11520, 2, S), carve(4096, 2, S)
        ONSA = carve(12032, 4, 64)
        HG_KD, HG_LD, LQ2 = carve(0, 2, 2, S), carve(5120, BLK, S), carve(1024, 2, NBLK, BLK)
        HG_AT, NCUM2 = (carve(1824, 4, S), carve(3520, 4, P)), carve(12032, 2, S)
        FFT = carve(0, 32, S)
        RQ, RK = carve(0, 8, S), carve(2048, 8, S)
        RV, RG = carve(4096, NT, D), carve(6144, NT, D)
        RTMP = carve(8192, 2, 4, S)
        RT = carve(8192, 4, 2, S)
        CQ, CKV, KPE = carve(10240, NT, 384), carve(11008, NT, S), carve(11520, 2, S)
        CQT, CKVT = carve(12032, 3, S), carve(12800, 2, S)
        MG1, MG2 = carve(0, NT, D), MOD[:, 0:2, :]
        QNT, QPE, KNT, VV = carve(0, 8, S), carve(2048, 2, 4, S), carve(4096, 8, S), carve(9472, NT, D)
        YM = carve(0, NT, D)
        LR, GE, LE = carve(0, NT, 36), carve(128, NT, E3), carve(256, NT, G3 + E3)
        cmp3, cmp4 = carve(512, 4, 8, 8), carve(768, 4, 8, 8)
        aT3, sil3 = carve(1024, 4, 1, S), carve(3072, 2, S)
        gcur3 = carve(3600, NT, 2)
        before3 = carve(4096, 32, 32)

        units = []

        def unit(kind, tile, group, nk, width):
            units.append((kind, tile, group, nk, width))

        for t in range(NT):
            for grp in range(2):
                unit("window", t, grp, P * (t + 1), 64)
        for t in range(NT):
            for kind in ("cmp", "sel", "win", "moba"):
                unit(kind, t, 0, NCMP if kind == "cmp" else P * (t + 1), 64)
        for t in range(NT):
            for grp in range(2):
                unit("mla", t, grp, P * (t + 1), P)
        n_window, n_nsa = 4, 8

        def bias_of(u, pair):
            kind, t, grp, nk, _ = units[u]
            if kind == "cmp":
                return BIASC[:, t, 2 * pair:2 * pair + 2, :]
            k0 = S - nk
            if kind in ("sel", "win", "moba"):
                h = (4 if kind == "moba" else 0) + 2 * pair
                return BIAS[:, h:h + 2, k0:S]
            m = window if kind == "window" else causal
            return m[:, k0:S].unsqueeze(1).to_broadcast([P, 2, nk])

        def values_of(u, kt, h):
            kind, _, grp, _, _ = units[u]
            if kind == "window":
                return AV[:, kt, 64 * grp:64 * grp + 64]
            if kind == "cmp":
                return VC[0:NCMP, :]
            if kind == "sel":
                return VS[:, kt, :]
            if kind == "win":
                return VW[:, kt, :]
            if kind == "moba":
                return VM[:, kt, 64 * h:64 * h + 64]
            return VV[:, kt, (4 * grp + h) * P:(4 * grp + h + 1) * P]

        block = ctx.enter_context(nc.Block())

        def kpn(ap):
            return ap.rearrange("(k p) n -> p k n", p=P)

        def slot(s, k, n, off=0):
            return shaped(ring[:, s % SLOTS, off:off + k * n], (k, n))

        n_consts = 29

        @block.sync
        def _(sp):
            at = [0]

            def slab():
                s = at[0]
                at[0] += 1
                if s >= SLOTS:
                    r = release[s - SLOTS]
                    if r in MOE_PRODUCTS:
                        done = MOE_PRODUCTS["moe1"] + (MOE_PRODUCTS["moe3"] if r == "moe3" else 0)
                        sp.wait_ge(moe_product_ready, done)
                    else:
                        sp.wait_ge(product_ready, r)
                return s

            def load(s, dst, src):
                sp.dma_start(dst, src).then_inc(slab_landed[s % SLOTS], 16)

            def column_slabs(w, bounds, view=kpn):
                for lo, hi in zip(bounds, bounds[1:]):
                    s = slab()
                    load(s, slot(s, KT, hi - lo), view(w[:, lo:hi]))

            sp.dma_start(X[:, :, :], I["x"][0].rearrange("(a p) n -> p a n", p=P)).then_inc(x_landed, 16)

            def ada_view(ap):
                return ap.rearrange("(p k) n -> p k n", k=KT)

            wide = list(range(0, 6 * D + 1, BANK))
            column_slabs(I["w_ada"][0], wide, ada_view)
            column_slabs(I["w_in"][0], [0, 512, 1024, 1536, 2048, 2320])
            column_slabs(I["w_out"][0], [0, 512, 1024])
            s0 = first_slab["moe1"]

            def moe1_slab(e, j):
                w = I["w_mlp1"][0][e][:, BANK * j:BANK * (j + 1)] if j < 4 else \
                    I["w_mlp2"][0][e][:, BANK * (j - 4):BANK * (j - 3)]
                load(s0 + j, slot(s0 + j, KT, BANK), kpn(w))

            for j in range(SLOTS):
                slab()
                moe1_slab(0, j)
            freed1 = [2, 4, 6, 8, 10, 12]
            with sp.Fori(0, E1 - 1) as e:
                for j in range(6):
                    sp.wait_ge(moe_product_ready, 12 * e + freed1[j])
                    moe1_slab(e if j + SLOTS < 6 else e + 1, (j + SLOTS) % 6)
            for j in range(SLOTS):
                sp.wait_ge(moe_product_ready, 12 * (E1 - 1) + freed1[j])
                moe1_slab(E1 - 1, j + SLOTS)
            at[0] = s0 + MOE_SLABS["moe1"]
            column_slabs(I["w_in_2"][0], [0, 512, 908, 1420, 1932, 2444, 2956])
            for kv in range(2):
                s = slab()
                load(s, slot(s, 16, S), kpn(I["nsa_cmp_w1_2"][0, kv]))
            column_slabs(I["w_out_2"][0], [0, 512, 1024])
            column_slabs(I["w_ff1_2"][0], list(range(0, FF2 + 1, BANK)))
            for n in range(8):
                s = slab()
                load(s, slot(s, 32, P), kpn(I["w_ff2_2"][0][:, P * n:P * (n + 1)]))
            column_slabs(I["w_ada_3"][0], wide, ada_view)
            w3 = I["w_in_3"][0]
            column_slabs(w3, list(range(0, 4097, BANK)) + [4480])
            s = slab()
            load(s, slot(s, KT, 320), kpn(w3[:, 4480:4800]))
            for half in range(2):
                load(s, slot(s, KT, 64, 2560)[:, :, 32 * half:32 * half + 32],
                     kpn(w3[:, 4736 + 32 * (1 - half):4768 + 32 * (1 - half)]))
            column_slabs(w3, [4800, 5312, 5824, 6336, 6848])
            column_slabs(I["w_ret_o_3"][0], [0, 512, 1024])
            for grp in range(2):
                s = slab()
                load(s, slot(s, 3, 768), kpn(I["w_uq_3"][0][:, 768 * grp:768 * (grp + 1)]))
                pe_cols = kpn(I["w_uq_3"][0]).rearrange("p k (h c) -> p k h c", h=8)
                for half in range(2):
                    dst = shaped(ring[:, s % SLOTS, 2304:3072], (3, 4, 64))[:, :, :, 32 * half:32 * half + 32]
                    c = P + 32 * (1 - half)
                    for k in range(3):
                        load(s, dst[:, k], pe_cols[:, k, 4 * grp:4 * grp + 4, c:c + 32])
            s = slab()
            load(s, slot(s, 2, 2048), kpn(I["w_ukv_3"][0]))
            column_slabs(I["w_mla_o_3"][0], [0, 512, 1024])
            column_slabs(I["w_out_3"][0], [0, 512, 1024])
            s0 = first_slab["moe3"]
            w1 = I["w1_3"][0].rearrange("g e d f -> (g e) d f")
            w3e = I["w3_3"][0].rearrange("g e d f -> (g e) d f")
            w2 = I["w2_3"][0].rearrange("g e f d -> (g e) f d")

            def moe3_slab(i, j):
                if j < 2:
                    load(s0 + j, slot(s0 + j, KT, F3), kpn(w1[2 * i + j]))
                    load(s0 + j, slot(s0 + j, KT, F3, 2048), kpn(w3e[2 * i + j]))
                else:
                    load(s0 + j, shaped(ring[:, (s0 + j) % SLOTS, :], (4, D)),
                         w2[bass.ds(2 * i, 2)].rearrange("e (k p) n -> p (e k) n", p=P))

            for j in range(3):
                slab()
                moe3_slab(0, j)
            freed3 = [2, 4, 12]
            with sp.Fori(0, E3 // 2 - 1) as i:
                for j in range(3):
                    sp.wait_ge(moe_product_ready, 12 * i + MOE_PRODUCTS["moe1"] + freed3[j])
                    moe3_slab(i + 1, j)
            sp.wait_ge(final_ready, 1)
            sp.dma_start(out[0].rearrange("(a p) n -> p a n", p=P), H[:, :, :]).then_inc(stored, 16)
            sp.wait_ge(stored, 16)

        @block.gpsimd
        def _(pool):
            n = [0]

            def const(dst, src):
                n[0] += 1
                pool.dma_start(dst, src).then_inc(consts_landed, 16)

            def row(ap):
                return ap.partition_broadcast(P)

            def vector(v):
                if v >= GVSLOTS:
                    pool.wait_ge(vec_used, v - GVSLOTS + 1)
                name = VECTORS[v]
                src = I[name] if name == "final_norm_3" else I[name][0]
                pool.dma_start(GV[:, v % GVSLOTS, :], row(src)).then_inc(vec_landed[v % GVSLOTS], 16)

            with nc.allow_non_contiguous_dma("short vectors"):
                const(cvec[:, 0, :], I["c"][0].rearrange("(p k) -> p k", k=KT))
                const(cvec[:, 1, :], I["c_3"][0].rearrange("(p k) -> p k", k=KT))
                const(ada_rows[0], I["b_ada"][0].rearrange("(n c) -> n c", c=BANK))
                const(ident[:, :], I["c_ident"])
                const(flip, I["c_flip"])
                const(onehot, I["c_onehot"])
                const(tab[0:32, :], I["rel_bias_2"].rearrange("h b -> b h"))
                vector(0)
                vector(1)
                vector(2)
                const(window[:, :], I["c_window"])
                const(causal[:, :], I["c_causal"])
                const(diag[:, :], I["c_diag"])
                const(heads2[:, :], I["c_heads2"])
                const(wr1[:, :, :], kpn(I["w_router"][0]))
                const(wr3[:, :, 0:G3], kpn(I["w_grp_3"][0]))
                const(wr3[:, :, G3:], kpn(I["w_exp_3"][0]))
                const(wgu[:, :], I["w_gla_gate_up"][0])
                const(b_gate, I["b_gla_gate"][0].rearrange("(c p) -> p c", p=P))
                const(conv_bias, I["conv_dw_b_2"][0].rearrange("(c p) -> p c", p=P))
                const(cmp_b1, I["nsa_cmp_b1_2"][0].rearrange("a (c p) -> p a c", p=P))
                const(cmp_pe, I["nsa_cmp_pe_2"][0].rearrange("a (j r) d -> (r d) a j", r=2))
                const(b_router, row(I["b_router"][0]))
                const(b_route3[:, 0:G3], row(I["b_grp_3"][0]))
                const(b_route3[:, G3:], row(I["b_exp_3"][0]))
                const(qn_row, row(I["q_norm_3"][0]))
                const(kvn_row, row(I["kv_norm_3"][0]))
                const(gla_norm, row(I["g_gla_norm"][0]))
                const(sinks, row(I["sinks"][0]))
                const(conv_g, row(I["conv_ln_g_2"][0]))
                const(conv_b, row(I["conv_ln_b_2"][0]))
                const(hgrn_g, row(I["hgrn_norm_g_2"][0]))
            assert n[0] == n_consts
            for i, (area, value) in enumerate(((tab[32:33, :], 1.0), (ones[:, :], 1.0), (BD[:, :, :, :], 0.0),
                                               (QD[:, :, :, :, :], 0.0), (KC[:, :, :], 0.0))):
                pool.memset(area, value).then_inc(zeros_ready, 1)
                pool.wait_ge(zeros_ready, i + 1)
            pool.wait_ge(rel_stored, 16)
            rs = rel_scratch
            pool.dma_start(BIASR, bass.AP(rs.tensor, 0, [[1, P], [BANK, 8], [1, S]])).then_inc(rel_landed, 16)
            with nc.allow_non_contiguous_dma("every sixteenth distance"):
                for t in range(NT):
                    for h in range(4):
                        pool.dma_start(BIASCR[:, t, h, :], bass.AP(rs.tensor, 159 - P * t + BANK * h, [[1, P], [16, NCMP]]))\
                            .then_inc(rel_landed, 16)
            vector(3)
            pool.wait_ge(h2_ready, 1)
            pool.dma_start(b1row, I["b_mlp1"][0]).then_inc(moe1_params_landed, 16)
            pool.dma_start(b2row, I["b_mlp2"][0]).then_inc(moe1_params_landed, 16)
            pool.dma_start(before, I["c_before"].rearrange("p (a b) -> p a b", a=32)).then_inc(moe1_params_landed, 16)
            pool.dma_start(cw2, I["nsa_cmp_w2_2"][0].rearrange("a (c p) n -> p a c n", p=P)).then_inc(block2_params_landed, 16)
            pool.dma_start(pww, kpn(I["conv_pw_w_2"][0])).then_inc(block2_params_landed, 16)
            pool.dma_start(convrow, I["conv_dw_w_2"][0]).then_inc(block2_params_landed, 16)
            for v in range(4, 8):
                vector(v)
            pool.wait_ge(mix_ready, 2)
            pool.dma_start(decay, I["c_decay"].rearrange("p (h s) -> p h s", h=4)).then_inc(tables_landed, 16)
            pool.dma_start(ropes, I["c_ropes"].rearrange("p (h s) -> p h s", h=4)).then_inc(tables_landed, 16)
            pool.wait_ge(y2_ready, 1)
            pool.dma_start(ada_rows[1], I["b_ada_3"][0].rearrange("(n c) -> n c", c=BANK)).then_inc(ada3_landed, 16)
            for v in range(8, 11):
                vector(v)
            pool.wait_ge(u2_ready, 1)
            pool.dma_start(before3, I["c_before"].rearrange("p (a b) -> p a b", a=32)).then_inc(before_landed, 16)

        @block.tensor
        def _(pe):
            done = [0]
            row_groups = [0]

            def bank():
                if done[0] >= PBANKS:
                    pe.wait_ge(product_free, done[0] - PBANKS + 1)
                return ps[:, done[0] % PBANKS, :]

            def close(mm):
                mm.then_inc(product_ready, 1)
                done[0] += 1

            def weights(s):
                pe.wait_ge(slab_landed[s % SLOTS], landed[s])

            def mm_k(o, lhs, rhs, nk, begin=True, end=True):
                for k in range(nk):
                    mm = pe.matmul(o, lhs(k), rhs(k), start=begin and k == 0, stop=end and k == nk - 1)
                return mm

            def turn(src, dst_k=None):
                for a in range(NT):
                    for half in range(2):
                        b = bank()
                        for k in range(4):
                            mm = pe.transpose(b[:, P * k:P * (k + 1)], src[:, a, P * (4 * half + k):P * (4 * half + k + 1)],
                                              ident[:, :])
                        close(mm)

            def tokens(rhs, width, lhs=HT, nk=KT, tiles=range(NT)):
                if width * NT <= BANK:
                    b = bank()
                    for a in range(NT):
                        mm = mm_k(b[:, a * width:(a + 1) * width], lambda k: lhs[:, k, P * a:P * (a + 1)], rhs, nk)
                    close(mm)
                else:
                    for a in range(NT):
                        b = bank()
                        close(mm_k(b[:, 0:width], lambda k: lhs[:, k, P * a:P * (a + 1)], rhs, nk))

            def features(cols_of, rhs=HT, nk=KT, m=P):
                b = bank()
                for i, c in enumerate(cols_of):
                    if isinstance(c, tuple):
                        for half in range(2):
                            mm = mm_k(b[64 * half:64 * half + 64, S * i:S * (i + 1)], c[half], lambda k: rhs[:, k, :], nk)
                    else:
                        mm = mm_k(b[0:m, S * i:S * (i + 1)], c, lambda k: rhs[:, k, :], nk)
                close(mm)

            def col(w, c, n=P):
                return lambda k: w[:, k, c:c + n]

            def twice(w, c):
                return col(w, c, 64), col(w, c, 64)

            def wide_stage(name, lhs=HT, width=BANK):
                n = len(dict((x[0], x[1]) for x in STAGES)[name])
                for i in range(n):
                    s = first_slab[name] + i
                    weights(s)
                    w = slot(s, KT, BANK)
                    tokens(lambda k: w[:, k, :], BANK, lhs)

            def modulation(name, j):
                for i in range(12):
                    s = first_slab[name] + i
                    weights(s)
                    w = slot(s, KT, BANK)
                    b = bank()
                    mm_k(b, lambda k: csil[:, j, k:k + 1].to_broadcast([P, P]), lambda k: w[:, k, :], KT, end=False)
                    close(pe.matmul(b, ident[0:12, i:i + 1].to_broadcast([12, P]), ada_rows[j], start=False, stop=True))

            def queries_of(u, pair):
                kind, t, grp, _, _ = units[u]
                q = {"window": Q1[:, 2 * grp + pair, :] if kind == "window" else None, "cmp": Q2[:, pair, :],
                     "sel": Q2[:, pair, :], "win": Q2[:, pair, :], "moba": QM[:, pair, :],
                     "mla": QPE[:, 0, 2 * grp + pair, :] if kind == "mla" else None}[kind]
                return q[:, P * t:P * (t + 1)]

            def keys_of(u, pair):
                kind, t, grp, nk, _ = units[u]
                if kind == "cmp":
                    return KC[:, :, :]
                return BD[:, {"window": grp, "sel": 0, "win": 1, "moba": 2 + pair, "mla": 0}[kind], :, 0:nk]

            def scores(u):
                kind, t, grp, nk, _ = units[u]
                if u >= 1:
                    pe.wait_ge(att["scores_read"], u)
                for pair in range(2):
                    o = ps[:, 4 + pair, 0:2 * nk].rearrange("p (h n) -> p h n", h=2)
                    if kind != "mla":
                        mm = pe.matmul(o, queries_of(u, pair), keys_of(u, pair), start=True, stop=True)
                        continue
                    for j in range(2):
                        h = 4 * grp + 2 * pair + j
                        pe.matmul(o[:, j, :], QNT[:, h, P * t:P * (t + 1)], KNT[:, h, 0:nk], start=True, stop=False)
                        mm = pe.matmul(o[:, j, :], queries_of(u, pair), keys_of(u, pair)[:, j, :], start=False, stop=True)
                mm.then_inc(att["scores"], 1)

            def attend(u):
                kind, t, grp, nk, width = units[u]
                pe.wait_ge(att["probs"], u + 1)
                if u >= 1:
                    pe.wait_ge(att["turned_copied"], u)
                for kt in range(-(-nk // P)):
                    n = min(P, nk - P * kt)
                    for h in range(4):
                        mm = pe.transpose(ps[0:n, 6 + kt, P * h:P * (h + 1)], sP[:, h, P * kt:P * kt + n], ident[:, :])
                mm.then_inc(att["turned"], 1)
                pe.wait_ge(att["turned_copied"], u + 1)
                if u >= 1:
                    pe.wait_ge(att["out_read"], u)
                kts = range(-(-nk // P))
                for h in range(4):
                    for kt in kts:
                        n = min(P, nk - P * kt)
                        mm = pe.matmul(ps[:, 3, h * width:(h + 1) * width], sPT[0:n, kt, h, :], values_of(u, kt, h),
                                       start=kt == 0, stop=kt == kts[-1])
                mm.then_inc(att["out"], 1)

            def attention(u0, u1):
                scores(u0)
                for u in range(u0, u1):
                    if u + 1 < u1:
                        scores(u + 1)
                    attend(u)

            def linear_attention(n, KDb, LDb, AT, v, dv):
                pe.wait_ge(lin["queries"], n + 1)
                for i in range(NBLK):
                    pe.wait_ge(lin["keys"], NBLK * n + i + 1)
                    for tile in range(1 if i < P // BLK else 2):
                        for pair in range(2):
                            if tile == 0:
                                o = ps[:, 4 + pair, :].rearrange("p (h t) -> p h t", h=2)[:, :, BLK * i:BLK * (i + 1)]
                            else:
                                o = ps[:, 6, :].rearrange("p (h t) -> p h t", h=4)[
                                    :, 2 * pair:2 * pair + 2, BLK * i - P:BLK * (i + 1) - P]
                            mm = pe.matmul(o, KDb[:, i % 2, pair, P * tile:P * (tile + 1)], QD[:, pair, i, :, :],
                                           start=True, stop=True)
                    mm.then_inc(lin["keys_used"], 1)
                for pair in range(2):
                    pe.wait_ge(lin["diag"], 2 * n + pair + 1)
                    for tile in range(NT):
                        for i in range(BLK):
                            c = ((tile * 2 + pair) * BLK + i) * 2
                            mm = pe.matmul(ps[:, 7, c:c + 2], LDb[:, i, P * tile:P * (tile + 1)], heads2[:, :],
                                           start=True, stop=True)
                    mm.then_inc(lin["diag_used"], 1)
                pe.wait_ge(lin["merged"], n + 1)
                for a in range(NT):
                    for h in range(4):
                        for kt in range(a + 1):
                            w = AT[0][:, h, P * a:P * (a + 1)] if kt == 0 else AT[1][:, h, :]
                            mm = pe.matmul(ps[:, 4 + a, h * dv:(h + 1) * dv], w, v[:, kt, h * dv:(h + 1) * dv],
                                           start=kt == 0, stop=kt == a)
                mm.then_inc(lin["out"], 1)

            pe.wait_ge(consts_landed, 16 * n_consts)
            pe.wait_ge(zeros_ready, 5)
            b = bank()
            close(pe.matmul(b[0:8, :], tab, onehot, start=True, stop=True))
            pe.wait_ge(cond_ready, 1)
            modulation("ada1", 0)
            pe.wait_ge(rel_landed, 16 * (1 + 4 * NT))
            for i in range(4):
                b = bank()
                close(pe.matmul(b, flip, BIASR[:, 2 * i:2 * i + 2, :], start=True, stop=True))
            b = bank()
            close(pe.matmul(b[:, 0:NT * 4 * NCMP], flip, BIASCR, start=True, stop=True))
            pe.wait_ge(h1_ready, 1)
            turn(H)
            pe.wait_ge(product_free, end["h1T"])
            s = first_slab["in1"]
            weights(s)
            w = slot(s, KT, BANK)
            features([col(w, 0), col(w, P)])
            features([col(w, 2 * P), col(w, 3 * P)])
            weights(s + 1)
            w = slot(s + 1, KT, BANK)
            features([twice(w, 0), twice(w, 64)])
            tokens(lambda k: w[:, k, P:2 * P], P)
            features([col(w, S), col(w, S + P)])
            weights(s + 2)
            w2 = slot(s + 2, KT, BANK)
            features([col(w2, 0), col(w2, P)])
            tokens(lambda k: w2[:, k, S:2 * S], S)
            weights(s + 3)
            w3 = slot(s + 3, KT, BANK)
            tokens(lambda k: w3[:, k, 0:S], S)
            tokens(lambda k: w3[:, k, S:2 * S], S)
            weights(s + 4)
            w4 = slot(s + 4, KT, 272)
            tokens(lambda k: w4[:, k, 0:S], S)
            features([col(w4, S, 16)], m=16)
            b = bank()
            pe.wait_ge(product_free, end["in1"])
            for c in range(2):
                mm = pe.matmul(b[:, S * c:S * (c + 1)], wgu[:, P * c:P * (c + 1)], GA[0:16, :], start=True, stop=True)
            close(mm)
            attention(0, n_window)
            linear_attention(0, GLA_KD, GLA_LD, GLA_AT, GVV, P)
            pe.wait_ge(mix_ready, 1)
            turn(Y)
            pe.wait_ge(product_free, end["mix1T"])
            wide_stage("out1")
            pe.wait_ge(h2_ready, 1)
            turn(H)
            pe.wait_ge(product_free, end["h2T"])
            tokens(lambda k: wr1[:, k, :], E1)
            pe.wait_ge(gates_ready, 1)
            b = bank()
            for a in range(NT):
                mm = pe.transpose(b[0:E1, P * a:P * (a + 1)], GT[:, a, :], ident[:, :])
            close(mm)
            pe.wait_ge(moe1_params_landed, 48)
            b = bank()
            b1v = b1row.rearrange("e (c f two) -> e c two f", two=2, f=P)
            for c in range(8):
                for j in range(2):
                    mm = pe.transpose(b[:, E1 * (2 * c + j):E1 * (2 * c + j + 1)], b1v[:, c, j, :], ident[0:E1, 0:E1])
            close(mm)
            pe.wait_ge(product_free, end["gates1T"])
            for a in range(NT):
                for half in range(2):
                    b = bank()
                    close(pe.matmul(b, gatesT[:, P * a:P * (a + 1)], b2row[:, BANK * half:BANK * (half + 1)],
                                    start=True, stop=True))
            pe.wait_ge(product_free, end["bacc1"])
            s0 = first_slab["moe1"]
            lap = [landed[s0 + j] for j in range(6)]
            with pe.Fori(0, E1) as e:
                n = 0
                for j in range(6):
                    pe.wait_ge(slab_landed[(s0 + j) % SLOTS], 32 * e + lap[j])
                    w = slot(s0 + j, KT, BANK)
                    for half in range(2):
                        pe.wait_ge(moe_product_free, 12 * e + n + 1)
                        b = ps[:, n % PBANKS, :]
                        if j < 4:
                            wv = w[:, :, S * half:S * (half + 1)].rearrange("p k (f two) -> p k two f", two=2)
                            for x in range(2):
                                mm = mm_k(b[:, S * x:S * (x + 1)], lambda k: wv[:, k, x, :], lambda k: HT[:, k, :], KT)
                        else:
                            if j == 4 and half == 0:
                                pe.wait_ge(hidden_ready, 8 * e + 8)
                            mm = mm_k(b, lambda k: aT[:, k, P * half:P * (half + 1)], lambda k: w[:, k, :], KT)
                        mm.then_inc(moe_product_ready, 1)
                        n += 1
            pe.wait_ge(x1_ready, 1)
            pe.wait_ge(block2_params_landed, 48)
            turn(X)
            b = bank()
            for c in range(2):
                mm = pe.transpose(b[:, 32 * c:32 * c + CONVW], convrow[:, P * c:P * (c + 1)], ident[0:CONVW, 0:CONVW])
            close(mm)
            pe.wait_ge(product_free, end["x1T"])
            s = first_slab["in2"]
            weights(s)
            w = slot(s, KT, BANK)
            features([col(w, 0), col(w, P)])
            features([twice(w, 256), twice(w, 320)])
            features([twice(w, 384)])
            tokens(lambda k: w[:, k, 448:512], 64)
            weights(s + 1)
            w1 = slot(s + 1, KT, 396)
            features([twice(w1, 0)])
            tokens(lambda k: w1[:, k, 64:140], 76)
            features([col(w1, 140), col(w1, 268)])
            for i in range(4):
                weights(s + 2 + i)
                wi = slot(s + 2 + i, KT, BANK)
                if i < 3:
                    features([col(wi, 0), col(wi, P)])
                if i in (1, 2):
                    features([col(wi, S), col(wi, S + P)])
                if i == 3:
                    tokens(lambda k: wi[:, k, 0:S], S)
                if i in (0, 3):
                    tokens(lambda k: wi[:, k, S:2 * S], S)
            pe.wait_ge(blocks_ready, 1)
            for kv in range(2):
                s = first_slab["cmp2"] + kv
                weights(s)
                w = slot(s, 16, S)
                b = bank()
                for c in range(2):
                    mm = mm_k(b[:, NCMP * c:NCMP * (c + 1)], lambda k: w[:, k, P * c:P * (c + 1)],
                              lambda k: BLOCKS[:, kv, k, :], 16)
                close(mm)
            pe.wait_ge(product_free, end["cmp2"] - 2)
            b = bank()
            for half in range(2):
                mm = mm_k(b[64 * half:64 * half + 64, 0:NCMP], lambda k: cw2[:, 0, k, :], lambda k: CHID[:, 0, k, :], 2)
            close(mm)
            b = bank()
            close(mm_k(b[0:NCMP, 0:64], lambda k: CHID[:, 1, k, :], lambda k: cw2[:, 1, k, :], 2))
            pe.wait_ge(product_free, end["cmp2"])
            attention(n_window, n_window + n_nsa)
            pe.wait_ge(conv_ready, 1)
            b = bank()
            for a in range(NT):
                for c in range(2):
                    mm = pe.transpose(b[:, S * a + P * c:S * a + P * (c + 1)], CACC[:, c, P * a:P * (a + 1)], ident[:, :])
            close(mm)
            pe.wait_ge(convsilu_ready, 1)
            b = bank()
            for c in range(2):
                for a in range(NT):
                    mm = pe.transpose(b[:, S * c + P * a:S * c + P * (a + 1)], CTOK[:, a, P * c:P * (c + 1)], ident[:, :])
            close(mm)
            pe.wait_ge(product_free, end["convback"])
            tokens(lambda k: pww[:, k, :], S, lhs=CSIL, nk=2)
            linear_attention(1, HG_KD, HG_LD, HG_AT, IH, 64)
            pe.wait_ge(mix_ready, 2)
            turn(Y)
            pe.wait_ge(product_free, end["mix2T"])
            wide_stage("out2")
            pe.wait_ge(y2_ready, 1)
            turn(X)
            pe.wait_ge(product_free, end["y2T"])
            for i in range(8):
                s = first_slab["ff1"] + i
                weights(s)
                w = slot(s, KT, BANK)
                features([col(w, 0), col(w, P)])
                features([col(w, 2 * P), col(w, 3 * P)])
            pe.wait_ge(relu_ready, 16)
            for i in range(8):
                s = first_slab["ff2"] + i
                weights(s)
                w = slot(s, 32, P)
                tokens(lambda k: w[:, k, :], P, lhs=FFT, nk=32)
            pe.wait_ge(ada3_landed, 16)
            modulation("ada3", 1)
            pe.wait_ge(u1_ready, 1)
            turn(H)
            pe.wait_ge(product_free, end["u1T"])
            s = first_slab["in3"]
            for i in range(9):
                weights(s + i)
                w = slot(s + i, KT, BANK if i < 8 else 384)
                if i < 4:
                    features([col(w, 0), col(w, P)])
                    features([col(w, 2 * P), col(w, 3 * P)])
                else:
                    tokens(lambda k: w[:, k, :], BANK if i < 8 else 384)
            weights(s + 9)
            w = slot(s + 9, KT, 320)
            wx = slot(s + 9, KT, 64, 2560)
            tokens(lambda k: w[:, k, 0:S], S)
            features([twice(w, S), twice(wx, 0)])
            pe.wait_ge(rope_ready, 1)
            pe.wait_ge(product_free, end["in3"])

            def ret_out_of(h):
                pe.wait_ge(ret_decayed, h + 1)
                if h >= 2:
                    pe.wait_ge(ret_copied, h - 1)
                for a in range(NT):
                    for kt in range(a + 1):
                        mm = pe.matmul(ps[:, 6 + h % 2, S * a:S * (a + 1)], RT[:, h, kt, P * a:P * (a + 1)],
                                       RV[:, kt, S * h:S * (h + 1)], start=kt == 0, stop=kt == a)
                mm.then_inc(ret_out, 1)

            for h in range(4):
                if h >= 2:
                    pe.wait_ge(ret_decayed, h - 1)
                for kt in range(NT):
                    o = ps[:, 4 + h % 2, 0:S] if kt == 0 else ps[:, 4 + h % 2, S:S + P]
                    mm = mm_k(o, lambda c: RK[:, 2 * h + c, P * kt:P * (kt + 1)], lambda c: RQ[:, 2 * h + c, P * kt:S], 2)
                mm.then_inc(ret_scores, 1)
                if h >= 1:
                    ret_out_of(h - 1)
            ret_out_of(3)
            wide_stage("gates3")
            pe.wait_ge(ret_ready, 1)
            turn(Y)
            pe.wait_ge(product_free, end["retT"])
            wide_stage("reto")
            pe.wait_ge(cq_ready, 1)
            for a in range(NT):
                b = bank()
                for c in range(3):
                    mm = pe.transpose(b[:, P * c:P * (c + 1)], CQ[:, a, P * c:P * (c + 1)], ident[:, :])
                close(mm)
            b = bank()
            for c in range(2):
                for a in range(NT):
                    mm = pe.transpose(b[:, S * c + P * a:S * c + P * (a + 1)], CKV[:, a, P * c:P * (c + 1)], ident[:, :])
            close(mm)
            pe.wait_ge(product_free, end["cqT"])
            for grp in range(2):
                s = first_slab["uq"] + grp
                weights(s)
                w = slot(s, 3, 768).rearrange("p k (h c) -> p k h c", h=4)
                wx = shaped(ring[:, s % SLOTS, 2304:3072], (3, 4, 64))
                for j in range(2):
                    features([lambda k, h=2 * j + i: w[:, k, h, 0:P] for i in range(2)], rhs=CQT, nk=3)
                features([tuple(lambda k, h=2 * i + x: w[:, k, h, P:] for x in range(2)) for i in range(2)], rhs=CQT, nk=3)
                features([tuple(lambda k, h=2 * i + x: wx[:, k, h, :] for x in range(2)) for i in range(2)], rhs=CQT, nk=3)
            s = first_slab["ukv"]
            weights(s)
            w = slot(s, 2, 2048).rearrange("p k (h c) -> p k h c", h=8)
            for j in range(4):
                features([lambda k, h=2 * j + i: w[:, k, h, 0:P] for i in range(2)], rhs=CKVT, nk=2)
            for half in range(2):
                tokens(lambda k: w[:, k, 4 * half:4 * half + 4, P:], BANK, lhs=CKVT, nk=2)
            pe.wait_ge(mlarope_ready, 1)
            pe.wait_ge(product_free, end["ukv"])
            attention(n_window + n_nsa, len(units))
            pe.wait_ge(mla_ready, 1)
            turn(Y)
            pe.wait_ge(product_free, end["mlaT"])
            wide_stage("mlao")
            pe.wait_ge(merge_ready, 1)
            turn(H)
            pe.wait_ge(product_free, end["mergeT"])
            wide_stage("out3")
            pe.wait_ge(u2_ready, 1)
            turn(H)
            pe.wait_ge(product_free, end["u2T"])
            tokens(lambda k: wr3[:, k, :], G3 + E3)
            pe.wait_ge(product_free, end["route3"])
            s0 = first_slab["moe3"]
            lap3 = [landed[s0 + j] for j in range(3)]
            f0 = MOE_PRODUCTS["moe1"]
            with pe.Fori(0, E3 // 2) as i:
                n = 0
                for j in range(2):
                    pe.wait_ge(slab_landed[(s0 + j) % SLOTS], 32 * i + lap3[j])
                    w = [slot(s0 + j, KT, F3), slot(s0 + j, KT, F3, 2048)]
                    for half in range(2):
                        pe.wait_ge(moe_product_free, 12 * i + f0 + n + 1)
                        b = ps[:, n % PBANKS, :]
                        for x in range(2):
                            mm = mm_k(b[:, S * x:S * (x + 1)], lambda k: w[x][:, k, P * half:P * (half + 1)],
                                      lambda k: HT[:, k, :], KT)
                        mm.then_inc(moe_product_ready, 1)
                        n += 1
                pe.wait_ge(slab_landed[(s0 + 2) % SLOTS], 16 * i + lap3[2])
                w = shaped(ring[:, (s0 + 2) % SLOTS, :], (4, D))
                for j in range(2):
                    pe.wait_ge(hidden_ready, 4 * i + 8 * E1 + 2 * j + 2)
                    for half in range(2):
                        for a in range(NT):
                            pe.wait_ge(moe_product_free, 12 * i + f0 + n + 1)
                            b = ps[:, n % PBANKS, :]
                            mm = mm_k(b, lambda k: aT3[:, 2 * j + k, 0, P * a:P * (a + 1)],
                                      lambda k: w[:, 2 * j + k, BANK * half:BANK * (half + 1)], 2)
                            mm.then_inc(moe_product_ready, 1)
                            n += 1

        @block.scalar
        def _(act):
            done = [0]
            steps = [0]
            roots = [0]

            def step(ins):
                ins.then_inc(act_step, 1)
                steps[0] += 1
                act.wait_ge(act_step, steps[0])

            def product():
                g = done[0]
                act.wait_ge(product_ready, g + 1)
                done[0] += 1
                return ps[:, g % PBANKS, :]

            def read(dst, src, func=ACT.Copy, **kw):
                act.activation(dst, src, func, **kw).then_inc(product_free, 1)

            def two(b, n=S):
                return b[:, 0:2 * n].rearrange("p (c n) -> p c n", c=2)

            def root(n):
                roots[0] += 1
                act.wait_ge(var_ready, roots[0])
                act.activation(std[:, 0:n], var[:, 0:n], ACT.Sqrt).then_inc(std_ready, 1)

            def turned():
                for a in range(NT):
                    for half in range(2):
                        b = product()
                        read(HT[:, 4 * half:4 * half + 4, P * a:P * (a + 1)], b.rearrange("p (k n) -> p k n", k=4))

            def wide(dst, func=ACT.Copy):
                for i in range(2):
                    for a in range(NT):
                        b = product()
                        read(dst[:, a, BANK * i:BANK * (i + 1)], b, func)

            def diagonal(b, first_slot, n):
                v = b[:, 0:S * n].rearrange("p (c n) -> p c n", c=n)
                act.activation(BD[0:64, first_slot:first_slot + n, 0, :], v[0:64], ACT.Copy)
                read(BD[64:P, first_slot:first_slot + n, 1, :], v[64:P])

            def modulation():
                for i in range(12):
                    b = product()
                    read(MOD.rearrange("p m d -> p (m d)")[:, BANK * i:BANK * (i + 1)], b)

            def attention(u0, u1):
                for u in range(u0, u1):
                    kind, t, grp, nk, _ = units[u]
                    st = att_stat[u % 2]
                    act.wait_ge(att["shift"], u + 1)
                    if u >= 1:
                        act.wait_ge(att["turned"], u)
                    if kind == "window":
                        act.activation(st["sink"], st["sink"], ACT.Exp)
                    for h in range(4):
                        ins = act.activation(sP[:, h, 0:nk], sS[:, h, 0:nk], ACT.Exp, bias=st["shift"][:, h:h + 1],
                                             accum_out=st["sum"][:, h:h + 1])
                    ins.then_inc(att["probs"], 1)
                    act.wait_ge(att["turned"], u + 1)
                    if u >= 1:
                        act.wait_ge(att["out"], u)
                    kts = -(-nk // P)
                    n = min(nk, P)
                    act.activation(sPT[0:n, 0:kts, :, :].rearrange("p k h q -> p k (h q)"), ps[0:n, 6:6 + kts, :], ACT.Copy)\
                        .then_inc(att["turned_copied"], 1)

            def linear_attention(n, cum, LQb, KDb, LDb, dst, dv):
                act.wait_ge(lin["qdiff"], n + 1)
                act.activation(LQb, LQb, ACT.Exp).then_inc(lin["qexp"], 1)
                act.wait_ge(lin["queries"], n + 1)
                for i in range(1, NBLK):
                    if i >= 2:
                        act.wait_ge(lin["keys_used"], NBLK * n + i - 1)
                    for pair in range(2):
                        ins = act.activation(KDb[:, i % 2, pair, 0:BLK * i], cum[:, pair, 0:BLK * i], ACT.Exp,
                                             bias=cum[:, pair, BLK * i - 1:BLK * i], scale=-1.0)
                    ins.then_inc(lin["kexp"], 1)
                for pair in range(2):
                    act.wait_ge(lin["ddiff"], 2 * n + pair + 1)
                    act.activation(LDb, LDb, ACT.Exp).then_inc(lin["dexp"], 1)
                act.wait_ge(lin["out"], n + 1)
                for a in range(NT):
                    act.activation(dst[:, a, :], ps[:, 4 + a, 0:4 * dv], ACT.Copy).then_inc(lin["read"], 1)

            def log_sigmoid_part(dst, src):
                step(act.activation(dst, src, ACT.Abs))
                step(act.activation(dst, dst, ACT.Exp, scale=-1.0))
                act.activation(dst, dst, ACT.Ln, bias=1.0).then_inc(loglog_ready, 1)

            act.wait_ge(consts_landed, 16 * n_consts)
            act.activation(csil[:, :, :], cvec[:, :, :], ACT.Silu).then_inc(cond_ready, 1)
            b = product()
            read(relv, b[0:8, :])
            act.wait_ge(product_free, 1)
            act.dma_start(rel_scratch, relv).then_inc(rel_stored, 16)
            root(2)
            modulation()
            for i in range(4):
                read(BIAS[:, 2 * i:2 * i + 2, :], two(product()))
            read(BIASC[:, :, :, :].rearrange("p t h n -> p (t h n)"), product()[:, 0:NT * 4 * NCMP])
            turned()
            for i in range(2):
                b = product()
                read(Q1[:, 2 * i:2 * i + 2, :], two(b))
            diagonal(product(), 0, 2)
            read(AV[:, :, :], two(product(), P))
            read(GQ[:, :, :], two(product()), scale=0.125)
            read(GK[:, :, :], two(product()))
            for i in range(2):
                read(GVV[:, :, S * i:S * (i + 1)], two(product()))
            for i in range(2):
                read(GG[:, :, S * i:S * (i + 1)], two(product()), ACT.Silu)
            read(GA[0:16, :], product()[0:16, 0:S])
            b = product()
            act.activation(GZ[:, 0, :], b[:, 0:S], ACT.Identity, bias=b_gate[:, 0:1])
            read(GZ[:, 1, :], b[:, S:2 * S], ACT.Identity, bias=b_gate[:, 1:2])
            act.wait_ge(product_free, end["gate1"])
            log_sigmoid_part(GL[:, :, :], GZ[:, :, :])
            attention(0, n_window)
            linear_attention(0, CUM, LQ[:, :, :, :], GLA_KD, GLA_LD[:, :, :], Y[:, :, BANK:], P)
            root(8)
            turned()
            wide(H)
            root(2)
            root(2)
            turned()
            read(LG[:, :, :], two(product(), E1))
            act.wait_ge(route_shift, 1)
            act.activation(LX[:, :, :], LX[:, :, :], ACT.Exp).then_inc(route_exp, 1)
            read(gatesT, product()[0:E1, 0:S])
            read(b1T[:, :, :], product().rearrange("p (c e) -> p c e", e=E1))
            for a in range(NT):
                for half in range(2):
                    read(Y[:, a, BANK * half:BANK * (half + 1)], product())
            with act.Fori(0, E1) as e:
                for j in range(8):
                    act.wait_ge(glu_ready, 8 * e + j + 1)
                    act.activation(sig[:, j % 2, :], glu[:, j % 2, :], ACT.Sigmoid, scale=1.702).then_inc(sig_ready, 1)
            root(2)
            turned()
            read(convw[:, :, 0:CONVW], two(product(), 32)[:, :, 0:CONVW])
            read(Q2[:, :, :], two(product()))
            read(KCT[:, :, :], two(product()))
            diagonal(product(), 0, 1)
            read(VS[:, :, :], two(product(), 64))
            diagonal(product(), 1, 1)
            b = two(product(), 76)
            act.activation(GN[:, :, :], b[:, :, 64:76], ACT.Sigmoid)
            read(VW[:, :, :], b[:, :, 0:64])
            read(QM[:, :, :], two(product()))
            diagonal(product(), 2, 2)
            read(VM[:, :, :], two(product()))
            read(CA[:, :, CONVW - 1:], two(product()))
            read(CG[:, :, :], two(product()), ACT.Sigmoid)
            read(QH[:, :, :], two(product()))
            read(FH[:, :, :], two(product()))
            read(IH[:, :, :], two(product()))
            read(GH[:, :, :], two(product()), ACT.Sigmoid)
            for kv in range(2):
                b = product()
                act.activation(CHID[:, kv, 0, :], b[:, 0:NCMP], ACT.Gelu_apprx_tanh, bias=cmp_b1[:, kv, 0:1])
                read(CHID[:, kv, 1, :], b[:, NCMP:2 * NCMP], ACT.Gelu_apprx_tanh, bias=cmp_b1[:, kv, 1:2])
            b = product()
            act.activation(KC[0:64, 0, :], b[0:64, 0:NCMP], ACT.Copy)
            read(KC[64:P, 1, :], b[64:P, 0:NCMP])
            read(VC[0:NCMP, :], product()[0:NCMP, 0:64])
            attention(n_window, n_window + n_nsa)
            read(CTOK[:, :, :], two(product()))
            root(2)
            act.wait_ge(convln_ready, 1)
            act.activation(CTOK[:, :, :], CTOK[:, :, :], ACT.Silu).then_inc(convsilu_ready, 1)
            read(CSIL[:, :, :], two(product()))
            read(Y[:, :, 512:768], two(product()))
            act.wait_ge(product_free, end["pw2"])
            log_sigmoid_part(HLOG[:, :, :], FH[:, :, :])
            act.wait_ge(log_ready, 1)
            act.activation(FH[:, :, :], FH[:, :, :], ACT.Sigmoid, scale=-1.0).then_inc(keep_ready, 1)
            linear_attention(1, HCUM, LQ2[:, :, :, :], HG_KD, HG_LD[:, :, :], Y[:, :, 768:], 64)
            root(8)
            turned()
            wide(H)
            root(2)
            turned()
            for i in range(16):
                read(FFT[:, 2 * i:2 * i + 2, :], two(product()), ACT.Relu)
            for i in range(8):
                read(H[:, :, P * i:P * (i + 1)], two(product(), P))
            root(2)
            root(2)
            modulation()
            turned()
            for i in range(4):
                read(RQ[:, 2 * i:2 * i + 2, :], two(product()))
            for i in range(4):
                read(RK[:, 2 * i:2 * i + 2, :], two(product()))
            wide(RV)
            wide(RG, ACT.Silu)
            for a in range(NT):
                read(CQ[:, a, :], product()[:, 0:384])
            read(CKV[:, :, :], two(product()))
            read(KPE[:, :, :], two(product()))
            root(4)
            for h in range(4):
                act.wait_ge(ret_out, h + 1)
                act.activation(Y[:, :, S * h:S * (h + 1)], two(ps[:, 6 + h % 2, :]), ACT.Copy).then_inc(ret_copied, 1)
            root(8)
            wide(MG1, ACT.Sigmoid)
            wide(MG2, ACT.Sigmoid)
            turned()
            wide(H)
            for a in range(NT):
                read(CQT[:, :, P * a:P * (a + 1)], product()[:, 0:384].rearrange("p (c n) -> p c n", c=3))
            read(CKVT[:, :, :], two(product()))
            act.wait_ge(ret_gated, 1)
            for grp in range(2):
                for j in range(2):
                    read(QNT[:, 4 * grp + 2 * j:4 * grp + 2 * j + 2, :], two(product()))
                for j in range(2):
                    read(QPE[:, j, 2 * grp:2 * grp + 2, :], two(product()))
            for j in range(4):
                read(KNT[:, 2 * j:2 * j + 2, :], two(product()))
            wide(VV)
            attention(n_window + n_nsa, len(units))
            turned()
            wide(YM)
            turned()
            wide(H)
            root(2)
            turned()
            read(LR[:, :, :], two(product(), G3 + E3))
            act.wait_ge(route_shift, 2)
            act.activation(LE[:, :, :], LE[:, :, :], ACT.Exp).then_inc(route_exp, 1)
            f0 = MOE_PRODUCTS["moe1"]
            with act.Fori(0, E3 // 2) as i:
                for n in range(4):
                    act.wait_ge(moe_product_ready, 12 * i + f0 + n + 1)
                    if n < 2:
                        act.wait_ge(hidden_ready, 4 * i + 8 * E1 + n)
                    else:
                        act.wait_ge(hidden_ready, 4 * i + 8 * E1 + n - 1)
                    act.activation(sil3[:, n % 2, :], ps[:, n % PBANKS, 0:S], ACT.Silu).then_inc(sig_ready, 1)
            root(2)

        @block.vector
        def _(dve):
            steps = [0]
            roots = [0]
            vectors = [0]

            def step(ins, *dyn):
                ins.then_inc(dve_step, 1)
                steps[0] += 1
                dve.wait_ge(dve_step, steps[0] if not dyn else dyn[0] + steps[0])

            def tell(ins, signal, value):
                ins.then_inc(signal, 1)
                dve.wait_ge(signal, value)

            def vector():
                v = vectors[0]
                dve.wait_ge(vec_landed[v % GVSLOTS], 16 * (v // GVSLOTS + 1))
                return GV[:, v % GVSLOTS, :]

            def vector_done(ins):
                vectors[0] += 1
                tell(ins, vec_used, vectors[0])

            def moments(src, i):
                n = src.shape[-1]
                parts = -(-n // BANK)
                for c in range(parts):
                    step(dve.bn_stats(bnst[:, 6 * c:6 * c + 6], src[:, BANK * c:min(n, BANK * (c + 1))]))
                step(dve.bn_aggr(moment[:, 2 * i:2 * i + 2], bnst[:, 0:6 * parts]))

            def inverse_roots(n, eps, square=False):
                mean, variance = moment[:, 0:2 * n:2], moment[:, 1:2 * n:2]
                if square:
                    step(dve.tensor_tensor(var[:, 0:n], mean, mean, ALU.mult))
                    step(dve.tensor_tensor(var[:, 0:n], var[:, 0:n], variance, ALU.add))
                    variance = var[:, 0:n]
                roots[0] += 1
                tell(dve.tensor_scalar(var[:, 0:n], variance, eps, None, ALU.add), var_ready, roots[0])
                dve.wait_ge(std_ready, roots[0])
                step(dve.reciprocal(rstd[:, 0:n], std[:, 0:n]))

            def both(v):
                return v.unsqueeze(1).to_broadcast([P, NT, v.shape[-1]])

            def rms_modulate(src, shift, scale, stage, ready, value, mod_stage=None):
                for a in range(NT):
                    moments(src[:, a, :], a)
                inverse_roots(NT, 1e-6, square=True)
                g = vector()
                for a in range(NT):
                    ins = dve.scalar_tensor_tensor(H[:, a, :], src[:, a, :], rstd[:, a:a + 1], g, ALU.mult, ALU.mult)
                    if a == 0:
                        step(ins)
                vector_done(ins)
                if mod_stage:
                    dve.wait_ge(product_free, end[mod_stage])
                step(dve.tensor_scalar(MOD[:, scale, :], MOD[:, scale, :], 1.0, None, ALU.add))
                step(dve.tensor_tensor(H[:, :, :], H[:, :, :], both(MOD[:, scale, :]), ALU.mult))
                tell(dve.tensor_tensor(H[:, :, :], H[:, :, :], both(MOD[:, shift, :]), ALU.add), ready, value)

            def add_gated_norm(src, gate):
                for a in range(NT):
                    moments(src[:, a, :], a)
                inverse_roots(NT, 1e-6, square=True)
                g = vector()
                for a in range(NT):
                    ins = dve.scalar_tensor_tensor(src[:, a, :], src[:, a, :], rstd[:, a:a + 1], g, ALU.mult, ALU.mult)
                    if a == 0:
                        step(ins)
                vector_done(ins)
                add_gated(src, gate)

            def add_gated(src, gate):
                step(dve.tensor_tensor(src[:, :, :], src[:, :, :], both(MOD[:, gate, :]), ALU.mult))
                step(dve.tensor_tensor(X[:, :, :], X[:, :, :], src[:, :, :], ALU.add))

            def center_scale(dst, src, i):
                step(dve.tensor_scalar(dst, src, moment[:, 2 * i:2 * i + 1], rstd[:, i:i + 1], ALU.subtract, ALU.mult))

            def add_layer_norm(src, last=None, value=None):
                for a in range(NT):
                    step(dve.scalar_tensor_tensor(X[:, a, :], X[:, a, :], 2.0 ** 0.25, src[:, a, :], ALU.mult, ALU.add))
                    moments(X[:, a, :], a)
                inverse_roots(NT, 1e-5)
                for a in range(NT):
                    center_scale(X[:, a, :], X[:, a, :], a)
                g = vector()
                vector_done(dve.tensor_tensor(X[:, :, :], X[:, :, :], both(g), ALU.mult))
                g = vector()
                vector_done(dve.tensor_tensor(X[:, :, :], X[:, :, :], both(g), ALU.add))

            scale_of = {"window": 0.125, "cmp": 0.125, "sel": 0.125, "win": 0.125, "moba": 0.125, "mla": 192.0 ** -0.5}

            def shift(u):
                kind, t, grp, nk, _ = units[u]
                st = att_stat[u % 2]
                dve.wait_ge(att["scores"], u + 1)
                if u >= 1:
                    dve.wait_ge(att["probs"], u)
                for pair in range(2):
                    ins = dve.scalar_tensor_tensor(
                        sS[:, 2 * pair:2 * pair + 2, 0:nk], ps[:, 4 + pair, 0:2 * nk].rearrange("p (h n) -> p h n", h=2),
                        scale_of[kind], bias_of(u, pair), ALU.mult, ALU.add)
                    if pair == 0:
                        step(ins)
                tell(ins, att["scores_read"], u + 1)
                step(dve.tensor_reduce(st["max"], sS[:, :, 0:nk], AX.X, ALU.max))
                if kind == "window":
                    sink = sinks[:, 4 * grp:4 * grp + 4]
                    step(dve.tensor_tensor(st["max"], st["max"], sink, ALU.max))
                    step(dve.tensor_tensor(st["sink"], sink, st["max"], ALU.subtract))
                tell(dve.tensor_scalar(st["shift"], st["max"], FLOOR, -1.0, ALU.max, ALU.mult), att["shift"], u + 1)

            def finish(u):
                kind, t, grp, nk, width = units[u]
                st = att_stat[u % 2]
                dve.wait_ge(att["probs"], u + 1)
                if kind == "window":
                    step(dve.tensor_tensor(st["sum"], st["sum"], st["sink"], ALU.add))
                else:
                    step(dve.tensor_scalar(st["sum"], st["sum"], 1e-30, None, ALU.max))
                step(dve.reciprocal(st["inv"], st["sum"]))
                if kind in ("cmp", "sel", "win"):
                    branch = ("cmp", "sel", "win").index(kind)
                    step(dve.tensor_tensor(st["inv"], st["inv"], GN[:, t, branch:12:3], ALU.mult))
                dve.wait_ge(att["out"], u + 1)
                o = ps[:, 3, 0:4 * width].rearrange("p (h d) -> p h d", h=4)
                at = {"window": 256 * grp, "moba": 256, "mla": 512 * grp}.get(kind, 0)
                dst = Y[:, t, at:at + 4 * width].rearrange("p (h d) -> p h d", h=4)
                add = kind in ("sel", "win")
                tell(dve.tensor_tensor(ONSA if add else dst, o, st["inv"].unsqueeze(2).to_broadcast([P, 4, width]), ALU.mult),
                     att["out_read"], u + 1)
                if add:
                    step(dve.tensor_tensor(dst, dst, ONSA, ALU.add))

            def attention(u0, u1):
                shift(u0)
                for u in range(u0, u1):
                    if u + 1 < u1:
                        shift(u + 1)
                    finish(u)

            def linear_attention(n, q, k, cum, LQb, KDb, LDb, AT):
                c4 = cum.rearrange("p c (b i) -> p c b i", i=BLK)
                step(dve.tensor_copy(LQb[:, :, 0, :], c4[:, :, 0, :]))
                for pair in range(2):
                    ins = dve.tensor_tensor(LQb[:, pair, 1:, :], c4[:, pair, 1:, :],
                                            c4[:, pair, 0:NBLK - 1, BLK - 1:BLK].to_broadcast([P, NBLK - 1, BLK]), ALU.subtract)
                    if pair == 0:
                        step(ins)
                tell(ins, lin["qdiff"], n + 1)
                for i in range(2):
                    step(dve.memset(KDb[:, i, :, :], 0.0))
                dve.wait_ge(lin["qexp"], n + 1)
                q4 = q.rearrange("p c (b i) -> p c b i", i=BLK)
                for h in range(2):
                    for pair in range(2):
                        rows_ = slice(64 * h, 64 * h + 64)
                        ins = dve.tensor_tensor(QD[rows_, pair, :, h, :], q4[rows_, pair, :, :], LQb[rows_, pair, :, :], ALU.mult)
                        if h + pair < 2:
                            step(ins)
                tell(ins, lin["queries"], n + 1)
                dve.sem_inc(lin["keys"], 1)
                for i in range(1, NBLK):
                    dve.wait_ge(lin["kexp"], (NBLK - 1) * n + i)
                    kd = KDb[:, i % 2, :, 0:BLK * i]
                    dve.tensor_tensor(kd, kd, k[:, :, 0:BLK * i], ALU.mult).then_inc(lin["keys"], 1)
                for pair in range(2):
                    if pair + n:
                        dve.wait_ge(lin["diag_used"], 2 * n + pair)
                    ld4 = LDb.rearrange("p i (b s) -> p i b s", s=BLK)

                    def later(x):
                        return x[:, pair, :].rearrange("p (b i) -> p i b", i=BLK).unsqueeze(3).to_broadcast([P, BLK, NBLK, BLK])

                    def earlier(x):
                        return x[:, pair, :].unsqueeze(1).to_broadcast([P, BLK, S])

                    step(dve.tensor_tensor(ld4, later(cum), earlier(cum).rearrange("p i (b s) -> p i b s", s=BLK), ALU.subtract))
                    tell(dve.tensor_scalar(LDb, LDb, 0.0, None, ALU.min), lin["ddiff"], 2 * n + pair + 1)
                    dve.wait_ge(lin["dexp"], 2 * n + pair + 1)
                    step(dve.tensor_tensor(ld4, ld4, later(q), ALU.mult))
                    tell(dve.tensor_tensor(LDb, LDb, earlier(k), ALU.mult), lin["diag"], 2 * n + pair + 1)
                dve.wait_ge(lin["keys_used"], NBLK * (n + 1))
                dve.wait_ge(lin["diag_used"], 2 * n + 2)
                nb = P // BLK
                for tile in range(NT):
                    d = ps[:, 7, 64 * tile:64 * tile + 64].rearrange("p (c i h) -> p c h i", c=2, i=BLK)
                    a4 = AT[tile].rearrange("p h (b i) -> p h b i", i=BLK)[:, :, 0:nb, :]
                    for h in range(4):
                        step(dve.tensor_tensor(a4[:, h], d[:, h // 2, h % 2, :].unsqueeze(1).to_broadcast([P, nb, BLK]),
                                               diag.rearrange("p (b i) -> p b i", i=BLK), ALU.mult))
                for pair in range(2):
                    o = ps[:, 4 + pair, :].rearrange("p (h t) -> p h t", h=2)
                    a = AT[0][:, 2 * pair:2 * pair + 2, :]
                    step(dve.tensor_tensor(a[:, :, 0:P], a[:, :, 0:P], o[:, :, 0:P], ALU.add))
                    step(dve.tensor_copy(a[:, :, P:S], o[:, :, P:S]))
                tell(dve.tensor_tensor(AT[1], AT[1], ps[:, 6, :].rearrange("p (h t) -> p h t", h=4), ALU.add),
                     lin["merged"], n + 1)

            def log_sigmoid_sums(n, z, part, cum, factor):
                dve.wait_ge(loglog_ready, n)
                for c in range(2):
                    ins = dve.scalar_tensor_tensor(part[:, c, :], z[:, c, :], 0.0, part[:, c, :], ALU.min, ALU.subtract)
                    if c == 0:
                        step(ins)
                tell(ins, log_ready, 1) if n == 2 else step(ins)
                if factor != 1.0:
                    step(dve.tensor_scalar(part, part, factor, None, ALU.mult))
                for c in range(2):
                    step(dve.tensor_tensor_scan(cum[:, c, :], ones[:, :], part[:, c, :], 0.0, ALU.mult, ALU.add))

            def head_rms(o, width, n0=0):
                for a in range(NT):
                    for h in range(4):
                        moments(o[:, a, width * h:width * (h + 1)], 4 * a + h)
                inverse_roots(8, 1e-6, square=True)

            def ranks(dst, v, groups, n, c1, c2, order):
                shape = [P, groups, n, n] if groups > 1 else [P, n, n]
                ax = 2 if groups > 1 else 1
                other, own = v.unsqueeze(ax).to_broadcast(shape), v.unsqueeze(ax + 1).to_broadcast(shape)
                o = order[:, 0:n, 0:n]
                if groups > 1:
                    o = o.unsqueeze(1).to_broadcast(shape)
                step(dve.tensor_tensor(c1, other, own, ALU.is_gt))
                step(dve.tensor_tensor(c2, other, own, ALU.is_equal))
                step(dve.tensor_tensor(c2, c2, o, ALU.mult))
                step(dve.tensor_tensor(c1, c1, c2, ALU.add))
                step(dve.tensor_reduce(dst, c1, AX.X, ALU.add))

            dve.wait_ge(consts_landed, 16 * n_consts)
            dve.wait_ge(zeros_ready, 5)
            dve.wait_ge(x_landed, 16)
            rms_modulate(X, 0, 1, "h1", h1_ready, 1, "ada1")
            log_sigmoid_sums(1, GZ, GL[:, :, :], CUM, 1.0 / 16.0)
            attention(0, n_window)
            linear_attention(0, GQ[:, :, :], GK[:, :, :], CUM[:, :, :], LQ, GLA_KD, GLA_LD[:, :, :], GLA_AT)
            dve.wait_ge(lin["read"], 2)
            o = Y[:, :, BANK:]
            head_rms(o, P)
            for a in range(NT):
                for h in range(4):
                    oh = o[:, a, P * h:P * (h + 1)]
                    step(dve.scalar_tensor_tensor(oh, oh, rstd[:, 4 * a + h:4 * a + h + 1], gla_norm, ALU.mult, ALU.mult))
            tell(dve.tensor_tensor(o, o, GG[:, :, :], ALU.mult), mix_ready, 1)
            dve.wait_ge(product_free, end["out1"])
            add_gated_norm(H, 2)
            rms_modulate(X, 3, 4, "h2", h2_ready, 1)
            dve.wait_ge(moe1_params_landed, 48)
            dve.wait_ge(product_free, end["route1"])
            step(dve.tensor_tensor(LG[:, :, :], LG[:, :, :], both(b_router), ALU.add))
            for a in range(NT):
                ranks(GT[:, a, :], LG[:, a, :], 1, E1, cmp1, cmp2, before)
                step(dve.tensor_reduce(moment[:, a:a + 1], LG[:, a, :], AX.X, ALU.max))
                step(dve.tensor_scalar(LX[:, a, :], LG[:, a, :], moment[:, a:a + 1], None, ALU.subtract))
            tell(dve.tensor_scalar(GT[:, :, :], GT[:, :, :], float(TOP1), None, ALU.is_lt), route_shift, 1)
            dve.wait_ge(route_exp, 1)
            step(dve.tensor_tensor(GT[:, :, :], GT[:, :, :], LX[:, :, :], ALU.mult))
            step(dve.tensor_reduce(moment[:, 0:NT], GT[:, :, :], AX.X, ALU.add))
            step(dve.reciprocal(moment[:, 2:2 + NT], moment[:, 0:NT]))
            tell(dve.tensor_tensor(GT[:, :, :], GT[:, :, :], moment[:, 2:2 + NT].unsqueeze(2).to_broadcast([P, NT, E1]),
                                   ALU.mult), gates_ready, 1)
            dve.wait_ge(product_free, end["bacc1"])
            dve.sem_inc(moe_product_free, PBANKS)
            base = steps[0]
            with dve.Fori(0, E1) as e:
                steps[0] = base
                own = 0
                per = 2 + 3 * 8 + 4 - 4

                def astep(ins):
                    step(ins, EXPERT_STEPS * e)

                astep(dve.tensor_copy(b1cur[:, :], b1T[:, :, e]))
                astep(dve.tensor_copy(gcur[:, :], GT[:, :, e]))

                def limit(j):
                    dve.wait_ge(moe_product_ready, 12 * e + j + 1)
                    b = ps[:, j % PBANKS, :]
                    dve.tensor_scalar(glu[:, j % 2, :], b[:, 0:S], b1cur[:, 2 * j:2 * j + 1], 7.0, ALU.add, ALU.min)\
                        .then_inc(glu_ready, 1)
                    tell2(dve.tensor_scalar(lnr[:, j % 2, :], b[:, S:2 * S], b1cur[:, 2 * j + 1:2 * j + 2], 7.0, ALU.add, ALU.min),
                          moe_product_free, 12 * e + PBANKS + j + 1)
                    astep(dve.tensor_scalar(lnr[:, j % 2, :], lnr[:, j % 2, :], -7.0, 1.0, ALU.max, ALU.add))

                def tell2(ins, signal, value):
                    ins.then_inc(signal, 1)
                    dve.wait_ge(signal, value)

                def combine(j):
                    dve.wait_ge(sig_ready, 8 * e + j + 1)
                    astep(dve.tensor_tensor(sig[:, j % 2, :], sig[:, j % 2, :], glu[:, j % 2, :], ALU.mult))
                    tell2(dve.tensor_tensor(aT[:, j, :], sig[:, j % 2, :], lnr[:, j % 2, :], ALU.mult), hidden_ready, 8 * e + j + 1)

                limit(0)
                for j in range(1, 8):
                    limit(j)
                    combine(j - 1)
                combine(7)
                for half in range(2):
                    for a in range(NT):
                        n = 8 + 2 * half + a
                        dve.wait_ge(moe_product_ready, 12 * e + n + 1)
                        y = Y[:, a, BANK * half:BANK * (half + 1)]
                        tell2(dve.scalar_tensor_tensor(y, ps[:, n % PBANKS, :], gcur[:, a:a + 1], y, ALU.mult, ALU.add),
                              moe_product_free, 12 * e + PBANKS + n + 1)
                assert steps[0] - base == EXPERT_STEPS, steps[0] - base
            steps[0] = base + E1 * EXPERT_STEPS
            add_gated_norm(Y, 5)
            dve.sem_inc(x1_ready, 1)
            dve.wait_ge(product_free, end["in2"])
            kct = KCT.rearrange("p a (m q r) -> p a q m r", q=8, r=2)
            for kv in range(2):
                for r in range(2):
                    for jh in range(2):
                        hs = slice(64 * r, 64 * r + 64)
                        ins = dve.tensor_tensor(
                            BLOCKS[hs, kv, 8 * jh:8 * jh + 8, :], kct[hs, kv, :, jh:jh + NCMP, r],
                            cmp_pe[hs, kv, 8 * jh:8 * jh + 8].unsqueeze(2).to_broadcast([64, 8, NCMP]), ALU.add)
                        if kv + r + jh < 3:
                            step(ins)
            tell(ins, blocks_ready, 1)
            attention(n_window, n_window + n_nsa)
            step(dve.memset(CA[:, :, 0:CONVW - 1], 0.0))
            step(dve.tensor_tensor(CA[:, :, CONVW - 1:], CA[:, :, CONVW - 1:], CG[:, :, :], ALU.mult))
            for c in range(2):
                step(dve.tensor_scalar(CACC[:, c, :], CA[:, c, 0:S], convw[:, c, 0:1], conv_bias[:, c:c + 1], ALU.mult, ALU.add))
            for i in range(1, CONVW):
                for c in range(2):
                    ins = dve.scalar_tensor_tensor(CACC[:, c, :], CA[:, c, i:i + S], convw[:, c, i:i + 1], CACC[:, c, :],
                                                   ALU.mult, ALU.add)
                    if i + c < CONVW:
                        step(ins)
            tell(ins, conv_ready, 1)
            dve.wait_ge(product_free, end["convT"])
            for a in range(NT):
                moments(CTOK[:, a, :], a)
            inverse_roots(NT, 1e-5)
            for a in range(NT):
                center_scale(CTOK[:, a, :], CTOK[:, a, :], a)
            step(dve.tensor_tensor(CTOK[:, :, :], CTOK[:, :, :], both(conv_g), ALU.mult))
            tell(dve.tensor_tensor(CTOK[:, :, :], CTOK[:, :, :], both(conv_b), ALU.add), convln_ready, 1)
            log_sigmoid_sums(2, FH, HLOG[:, :, :], HCUM, 1.0)
            dve.wait_ge(keep_ready, 1)
            dve.wait_ge(product_free, end["pw2"])
            linear_attention(1, QH[:, :, :], FH[:, :, :], HCUM[:, :, :], LQ2, HG_KD, HG_LD[:, :, :], HG_AT)
            dve.wait_ge(lin["read"], 4)
            o = Y[:, :, 768:]
            head_rms(o, 64)
            for a in range(NT):
                oa = o[:, a, :].rearrange("p (h d) -> p h d", h=4)
                step(dve.tensor_tensor(oa, oa, rstd[:, 4 * a:4 * a + 4].unsqueeze(2).to_broadcast([P, 4, 64]), ALU.mult))
            step(dve.tensor_tensor(o, o, both(hgrn_g), ALU.mult))
            tell(dve.tensor_tensor(o, o, GH[:, :, :], ALU.mult), mix_ready, 2)
            dve.wait_ge(product_free, end["out2"])
            add_layer_norm(H)
            dve.sem_inc(y2_ready, 1)
            for i in range(16):
                dve.wait_ge(product_free, end["y2T"] + i + 1)
                f = FFT[:, 2 * i:2 * i + 2, :]
                dve.tensor_tensor(f, f, f, ALU.mult).then_inc(relu_ready, 1)
            dve.wait_ge(product_free, end["ff2"])
            add_layer_norm(H)
            rms_modulate(X, 0, 1, "u1", u1_ready, 1, "ada3")
            dve.wait_ge(tables_landed, 32)
            dve.wait_ge(product_free, end["in3"])
            for r in (RQ, RK):
                x1, x2 = r[:, 0:8:2, :], r[:, 1:8:2, :]
                cos, sin = (ropes[:, i, :].unsqueeze(1).to_broadcast([P, 4, S]) for i in range(2))
                step(dve.tensor_tensor(RTMP[:, 0], x1, sin, ALU.mult))
                step(dve.tensor_tensor(RTMP[:, 1], x2, sin, ALU.mult))
                step(dve.tensor_tensor(x1, x1, cos, ALU.mult))
                step(dve.tensor_tensor(x2, x2, cos, ALU.mult))
                step(dve.tensor_tensor(x1, x1, RTMP[:, 1], ALU.subtract))
                ins = dve.tensor_tensor(x2, x2, RTMP[:, 0], ALU.add)
                step(ins) if r is RQ else tell(ins, rope_ready, 1)
            step(dve.tensor_tensor(KPE[:, 0, :], KPE[:, 0, :], ropes[:, 2, :], ALU.mult))
            step(dve.tensor_tensor(KPE[:, 1, :], KPE[:, 1, :], ropes[:, 3, :], ALU.mult))
            for h in range(2):
                hs = slice(64 * h, 64 * h + 64)
                step(dve.tensor_tensor(BD[hs, 0, h, :], KPE[hs, 0, :], KPE[hs, 1, :], ALU.add))
            for a in range(NT):
                moments(CQ[:, a, :], 2 * a)
                moments(CKV[:, a, :], 2 * a + 1)
            inverse_roots(4, 1e-6, square=True)
            for a in range(NT):
                step(dve.scalar_tensor_tensor(CQ[:, a, :], CQ[:, a, :], rstd[:, 2 * a:2 * a + 1], qn_row, ALU.mult, ALU.mult))
                ins = dve.scalar_tensor_tensor(CKV[:, a, :], CKV[:, a, :], rstd[:, 2 * a + 1:2 * a + 2], kvn_row, ALU.mult, ALU.mult)
                if a == 0:
                    step(ins)
            tell(ins, cq_ready, 1)
            for h in range(4):
                dve.wait_ge(ret_scores, h + 1)
                b = ps[:, 4 + h % 2, :]
                step(dve.tensor_tensor(RT[:, h, 0, :], b[:, 0:S], decay[:, h, :], ALU.mult))
                tell(dve.tensor_tensor(RT[:, h, 1, P:S], b[:, S:S + P], decay[:, h, 0:P], ALU.mult), ret_decayed, h + 1)
            dve.wait_ge(ret_copied, 4)
            for a in range(NT):
                for h in range(4):
                    moments(Y[:, a, S * h:S * (h + 1)], 4 * a + h)
            inverse_roots(8, 1e-6)
            for a in range(NT):
                for h in range(4):
                    yh = Y[:, a, S * h:S * (h + 1)]
                    center_scale(yh, yh, 4 * a + h)
            tell(dve.tensor_tensor(Y[:, :, :], Y[:, :, :], RG[:, :, :], ALU.mult), ret_ready, 1)
            dve.wait_ge(product_free, end["reto"])
            tell(dve.tensor_tensor(H[:, :, :], H[:, :, :], MG1[:, :, :], ALU.mult), ret_gated, 1)
            dve.wait_ge(product_free, end["uq"])
            for j in range(2):
                step(dve.tensor_tensor(QPE[:, j, :, :], QPE[:, j, :, :],
                                       ropes[:, 2 + j, :].unsqueeze(1).to_broadcast([P, 4, S]), ALU.mult))
            tell(dve.tensor_tensor(QPE[:, 0, :, :], QPE[:, 0, :, :], QPE[:, 1, :, :], ALU.add), mlarope_ready, 1)
            attention(n_window + n_nsa, len(units))
            dve.sem_inc(mla_ready, 1)
            dve.wait_ge(product_free, end["mlao"])
            step(dve.tensor_tensor(YM[:, :, :], YM[:, :, :], MG2[:, :, :], ALU.mult))
            tell(dve.tensor_tensor(H[:, :, :], H[:, :, :], YM[:, :, :], ALU.add), merge_ready, 1)
            dve.wait_ge(product_free, end["out3"])
            add_gated(H, 2)
            rms_modulate(X, 3, 4, "u2", u2_ready, 1)
            dve.wait_ge(before_landed, 16)
            dve.wait_ge(product_free, end["route3"])
            step(dve.tensor_tensor(LR[:, :, :], LR[:, :, :], both(b_route3), ALU.add))
            GSEL, ESEL, GMAX = moment[:, 0:8], GE, moment[:, 8:24]
            for a in range(NT):
                grp, exp = LR[:, a, 0:G3], LR[:, a, G3:].rearrange("p (g e) -> p g e", g=G3)
                ranks(GSEL[:, G3 * a:G3 * (a + 1)], grp, 1, G3, cmp3[:, 0, 0:G3, 0:G3], cmp4[:, 0, 0:G3, 0:G3], before3)
                ranks(GE[:, a, :].rearrange("p (g e) -> p g e", g=G3), exp, G3, PG3, cmp3, cmp4, before3)
                step(dve.tensor_reduce(GMAX[:, 8 * a:8 * a + 1], grp, AX.X, ALU.max))
                step(dve.tensor_reduce(GMAX[:, 8 * a + 4:8 * a + 8], exp, AX.X, ALU.max))
                step(dve.tensor_scalar(LE[:, a, 0:G3], grp, GMAX[:, 8 * a:8 * a + 1], None, ALU.subtract))
                step(dve.tensor_tensor(LE[:, a, G3:].rearrange("p (g e) -> p g e", g=G3), exp,
                                       GMAX[:, 8 * a + 4:8 * a + 8].unsqueeze(2).to_broadcast([P, G3, PG3]), ALU.subtract))
            step(dve.tensor_scalar(GSEL, GSEL, 1.0, None, ALU.is_lt))
            tell(dve.tensor_scalar(GE[:, :, :], GE[:, :, :], float(TOP3), None, ALU.is_lt), route_shift, 2)
            dve.wait_ge(route_exp, 2)
            for a in range(NT):
                e8 = GE[:, a, :].rearrange("p (g e) -> p g e", g=G3)
                step(dve.tensor_reduce(GMAX[:, 0:1], LE[:, a, 0:G3], AX.X, ALU.add))
                step(dve.reciprocal(GMAX[:, 1:2], GMAX[:, 0:1]))
                step(dve.scalar_tensor_tensor(GMAX[:, 4:8], LE[:, a, 0:G3], GMAX[:, 1:2], GSEL[:, G3 * a:G3 * (a + 1)],
                                              ALU.mult, ALU.mult))
                step(dve.tensor_tensor(GE[:, a, :], GE[:, a, :], LE[:, a, G3:], ALU.mult))
                step(dve.tensor_reduce(GMAX[:, 8:12], e8, AX.X, ALU.add))
                step(dve.reciprocal(GMAX[:, 12:16], GMAX[:, 8:12]))
                step(dve.tensor_tensor(GMAX[:, 4:8], GMAX[:, 4:8], GMAX[:, 12:16], ALU.mult))
                step(dve.tensor_tensor(e8, e8, GMAX[:, 4:8].unsqueeze(2).to_broadcast([P, G3, PG3]), ALU.mult))
            step(dve.memset(Y[:, :, :], 0.0))
            base = steps[0]
            f0 = MOE_PRODUCTS["moe1"]
            with dve.Fori(0, E3 // 2) as i:
                steps[0] = base
                step(dve.tensor_copy(gcur3[:, :, :], GE[:, :, bass.ds(2 * i, 2)]), i)
                for n in range(4):
                    dve.wait_ge(sig_ready, 4 * i + 8 * E1 + n + 1)
                    dve.tensor_tensor(aT3[:, n, 0, :], sil3[:, n % 2, :], ps[:, n % PBANKS, S:2 * S], ALU.mult)\
                        .then_inc(hidden_ready, 1)
                    dve.wait_ge(hidden_ready, 4 * i + 8 * E1 + n + 1)
                    dve.sem_inc(moe_product_free, 1)
                for j in range(2):
                    for half in range(2):
                        for a in range(NT):
                            n = 4 + 4 * j + 2 * half + a
                            dve.wait_ge(moe_product_ready, 12 * i + f0 + n + 1)
                            y = Y[:, a, BANK * half:BANK * (half + 1)]
                            dve.scalar_tensor_tensor(y, ps[:, n % PBANKS, :], gcur3[:, a, j:j + 1], y, ALU.mult, ALU.add)\
                                .then_inc(moe_product_free, 1)
                            dve.wait_ge(moe_product_free, 12 * i + f0 + PBANKS + n + 1)
            steps[0] = base + E3 // 2
            add_gated(Y, 5)
            for a in range(NT):
                moments(X[:, a, :], a)
            inverse_roots(NT, 1e-6, square=True)
            g = vector()
            for a in range(NT):
                ins = dve.scalar_tensor_tensor(H[:, a, :], X[:, a, :], rstd[:, a:a + 1], g, ALU.mult, ALU.mult)
                if a == 0:
                    step(ins)
            vector_done(ins)
            dve.sem_inc(final_ready, 1)


OUT_SHAPE = (1, S, D)


def kernel(**inputs):
    import concourse.bacc as _bacc
    from concourse.bass_utils import run_bass_kernel_spmd as _run

    nc = _bacc.Bacc("TRN2", target_bir_lowering=False, num_devices=1)
    arrays, args = {}, {}
    for name, a in {**inputs, **constants()}.items():
        a = np.ascontiguousarray(a)
        arrays[f"in_{name}"] = a
        args[name] = nc.dram_tensor(f"in_{name}", a.shape, F32, kind="ExternalInput").ap()
    out = nc.dram_tensor("out_0", OUT_SHAPE, F32, kind="ExternalOutput").ap()
    rel_scratch = nc.dram_tensor("rel_scratch", (8, BANK), F32, kind="Internal").ap()
    build(nc, args, out, rel_scratch)
    r = _run(nc, [arrays], core_ids=[0])
    return r.results[0]["out_0"]
```

```python
from contextlib import ExitStack

import numpy as np

import concourse.bass as bass
from concourse import mybir

F32 = mybir.dt.float32
ALU = mybir.AluOpType
ACT = mybir.ActivationFunctionType
AX = mybir.AxisListType

P = 128
S = 256
NT = S // P
D = 1024
KT = D // P
E1, F1 = 32, 1024
TOP1 = 4
E3, F3, G3, PG3 = 32, 256, 4, 8
TOP3 = 2
NCMP = 15
CONVW = 31
FF2 = 4096
SLOTS = 3
SLAB = 4096
BANK = 512
PBANKS = 3
NEG = -1.0e30
FLOOR = -1.0e20
C = 96
ROUNDS = -(-S // C)
EXPERT_STEPS = 14
BLK = 16
NBLK = S // BLK

STAGES = [
    ("rel", [], 1), ("ada1", [1] * 12, 0), ("flip", [], 5), ("h1T", [], 4), ("in1", [2, 3, 2, 2, 2], 0), ("gate1", [], 1),
    ("mix1T", [], 4), ("out1", [2, 2], 0), ("h2T", [], 4), ("route1", [], 1), ("gates1T", [], 2), ("rank1", [], 1),
    ("x1T", [], 4), ("convw", [], 1), ("in2", [4, 3, 2, 2, 2, 2], 0), ("cmp2", [1, 1], 2), ("convT", [], 1),
    ("convback", [], 1), ("pw2", [], 1), ("mix2T", [], 4), ("out2", [2, 2], 0), ("y2T", [], 4), ("ff1", [2] * 8, 0),
    ("ff2", [1] * 8, 0),
    ("ada3", [1] * 12, 0), ("u1T", [], 4), ("in3", [2] * 10, 0), ("gates3", [2] * 4, 0),
    ("retT", [], 4), ("reto", [2, 2], 0), ("cqT", [], 3), ("uq", [4, 4], 0), ("ukv", [8], 0),
    ("mlaT", [], 4), ("mlao", [2, 2], 0), ("mergeT", [], 4), ("out3", [2, 2], 0),
    ("u2T", [], 4), ("route3", [], 1), ("rank3", [], 1),
]


def product_plan():
    first, end, first_slab, release, product, slab = {}, {}, {}, [], 0, 0
    for name, per_slab, extra in STAGES:
        first[name], first_slab[name] = product, slab
        for n in per_slab:
            product += n
            release.append(product)
            slab += 1
        product += extra
        end[name] = product
    return first, end, first_slab, release


def constants():
    p, j = np.arange(P)[:, None], np.arange(2 * P)[None, :]
    rel = p + P - j
    window = np.where((rel >= 0) & (rel < P), 0.0, NEG)
    causal = np.where(rel >= 0, 0.0, NEG)
    dist = 255 - np.arange(BANK)
    nf = np.maximum(dist, 1).astype(np.float32)
    large = 16 + (np.log(nf / np.float32(16)) / np.float32(np.log(8.0)) * 16).astype(np.int32)
    n = np.maximum(dist, 0)
    bucket = np.where(n < 16, n, np.minimum(large, 31))
    onehot = np.zeros((33, BANK))
    onehot[bucket, np.arange(BANK)] = (dist >= 0)
    onehot[32] = np.where(dist >= 0, 0.0, NEG)
    s = np.arange(P)[:, None, None]
    b = np.arange(P // BLK)[None, :, None]
    i = np.arange(BLK)[None, None, :]
    diag = ((s // BLK == b) & (i >= s % BLK)).reshape(P, P)
    heads2 = np.stack([np.arange(P) < 64, np.arange(P) >= 64], 1)
    e = np.arange(32)
    before = np.broadcast_to((e[None, :] < e[:, None]).reshape(1, -1), (P, 1024))
    log_gamma = np.log1p(-np.exp2(-5.0 - np.arange(4)))
    relT = np.arange(2 * P)[None, :] - np.arange(P)[:, None]
    decay = np.where(relT[:, None, :] >= 0, np.exp(log_gamma[None, :, None] * np.maximum(relT, 0)[:, None, :]), 0.0) / 16.0

    def rope(dim):
        inv = np.float32(10000.0) ** (-np.arange(0, dim, 2, dtype=np.float32) / np.float32(dim))
        ang = inv[:, None].astype(np.float32) * np.arange(S, dtype=np.float32)[None, :]
        return np.cos(ang), np.sin(ang)

    cr, sr = rope(256)
    cm, sm = rope(64)
    ropes = np.stack([cr, sr, np.concatenate([cm, cm, cm, cm]), np.concatenate([-sm, sm, -sm, sm])], 1)
    c = {
        "c_ident": np.eye(P), "c_flip": np.eye(P)[::-1], "c_window": window, "c_causal": causal, "c_onehot": onehot, "c_diag": diag,
        "c_heads2": heads2, "c_before": before, "c_tri": np.arange(P)[:, None] < np.arange(P)[None, :],
        "c_iota": np.broadcast_to(np.arange(C), (P, C)), "c_decay": decay.reshape(P, -1), "c_ropes": ropes.reshape(P, -1),
    }
    return {k: np.ascontiguousarray(v, dtype=np.float32) for k, v in c.items()}


PARTS = {("in3", 9): 3, ("uq", 0): 7, ("uq", 1): 7}
VECTORS = ["g_pre_mix", "g_post_mix", "g_pre_ffn", "g_post_ffn", "ln1_g_2", "ln1_b_2", "ln2_g_2", "ln2_b_2",
           "norm1_3", "norm2_3", "final_norm_3"]
GVSLOTS = 3


def landed_plan():
    at, out = [0] * SLOTS, []
    for name, per_slab, _ in STAGES:
        for i in range(len(per_slab)):
            at[len(out) % SLOTS] += 16 * PARTS.get((name, i), 1)
            out.append(at[len(out) % SLOTS])
    return out


def build(nc, I, out, rel_scratch, dbg=None):
    first, end, first_slab, release = product_plan()
    landed = landed_plan()
    with ExitStack() as ctx:
        def sb(name, shape):
            return ctx.enter_context(nc.sbuf_tensor(name, shape, F32))

        def sem(name):
            return ctx.enter_context(nc.semaphore(name))

        ring = sb("ring", [P, SLOTS, SLAB])
        X = sb("X", [P, NT, D])
        H = sb("H", [P, NT, D])
        HT = sb("HT", [P, KT, S])
        Y = sb("Y", [P, NT, D])
        MOD = sb("MOD", [P, 6, D])
        GV = sb("GV", [P, GVSLOTS, D])
        BD = sb("BD", [P, 4, 2, S])
        QD = sb("QD", [P, 2, NBLK, 2, BLK])
        KC = sb("KC", [P, 2, NCMP])
        BIAS = sb("BIAS", [P, 8, S])
        BIASC = sb("BIASC", [P, NT, 4, NCMP])
        decay = BIAS[:, 0:4, :]
        ropes = BIAS[:, 4:8, :]
        ident = sb("ident", [P, P])
        window = sb("window", [P, S])
        causal = sb("causal", [P, S])
        diag = sb("diag", [P, P])
        heads2 = sb("heads2", [P, 2])
        ones = sb("ones", [P, S])
        tri = sb("tri", [P, P])
        rounds = ctx.enter_context(nc.sbuf_tensor("rounds", [P, 2], mybir.dt.int32))
        wr1 = sb("wr1", [P, KT, E1])
        wr3 = sb("wr3", [P, KT, G3 + E3])
        wgu = sb("wgu", [16, S])
        rows = sb("rows", [P, 1920])
        cols = sb("cols", [P, 128])
        stat = sb("stat", [P, 256])
        scr = sb("scr", [P, 13312])
        ps = ctx.enter_context(nc.psum_tensor("ps", [P, 8, BANK], F32))

        def shaped(v, shape):
            names = "abcd"[:len(shape)]
            if len(shape) == 1:
                return v
            return v.rearrange(f"p ({' '.join(names)}) -> p {' '.join(names)}",
                               **{k: s for k, s in zip(names, shape)})

        def carve(base, *shape):
            n = int(np.prod(shape))
            assert base + n <= 13312, (base, shape)
            return shaped(scr[:, base:base + n], shape)

        b_router, b_route3 = rows[:, 0:32], rows[:, 32:68]
        qn_row, kvn_row = rows[:, 128:512], rows[:, 512:768]
        gla_norm, sinks = rows[:, 768:896], rows[:, 896:904]
        conv_g, conv_b, hgrn_g = rows[:, 1024:1280], rows[:, 1280:1536], rows[:, 1536:1792]
        iota = rows[:, 1792:1792 + C]
        cvec = shaped(cols[:, 0:16], (2, KT))
        b_gate = cols[:, 16:18]
        conv_bias = cols[:, 18:20]
        cmp_b1 = shaped(cols[:, 20:24], (2, 2))
        tab = cols[0:33, 24:32]
        cmp_pe = shaped(cols[:, 32:64], (2, 16))
        csil = shaped(cols[:, 64:80], (2, KT))
        var, std, rstd = stat[:, 64:80], stat[:, 80:96], stat[:, 96:112]
        moment = stat[:, 0:64]
        bnst = stat[:, 128:140]
        att_stat = [{n: stat[:, 144 + 32 * b + 4 * i:148 + 32 * b + 4 * i]
                     for i, n in enumerate(("max", "shift", "sum", "inv", "sink"))} for b in range(2)]
        ada_rows = [Y[0:12, 0, 0:BANK], Y[0:12, 0, 0:BANK]]
        relv = Y[0:8, 1, 0:BANK]
        onehot = Y[0:33, 1, BANK:2 * BANK]

        slab_landed = [sem(f"slab_landed{i}") for i in range(SLOTS)]
        product_ready, product_free = sem("product_ready"), sem("product_free")
        consts_landed = sem("consts_landed")
        vec_landed = [sem(f"vec_landed{i}") for i in range(GVSLOTS)]
        vec_used = sem("vec_used")
        zeros_ready = sem("zeros_ready")
        rel_stored, rel_landed = sem("rel_stored"), sem("rel_landed")
        ada3_landed, moe1_params_landed = sem("ada3_landed"), sem("moe1_params_landed")
        block2_params_landed, tables_landed, before_landed = sem("block2_params"), sem("tables"), sem("before_landed")
        x_landed, stored = sem("x_landed"), sem("stored")
        dve_step, act_step = sem("dve_step"), sem("act_step")
        var_ready, std_ready = sem("var_ready"), sem("std_ready")
        cond_ready, h1_ready, abs_ready, glog_ready, loglog_ready = (sem(n) for n in (
            "cond_ready", "h1_ready", "abs_ready", "glog_ready", "loglog_ready"))
        mix_ready, h2_ready, route_shift, route_exp, gates_ready = (sem(n) for n in (
            "mix_ready", "h2_ready", "route_shift", "route_exp", "gates_ready"))
        m1 = {n: sem("m1_" + n) for n in (
            "rounds", "pick", "gather", "gather_read", "up", "up_read", "glu", "sig", "hidden", "down", "down_read",
            "scatter", "sum", "sum_read", "step")}
        m1_landed = [sem(f"m1_landed{i}") for i in range(SLOTS)]
        m3 = {n: sem("m3_" + n) for n in (
            "rounds", "pick", "gather", "gather_read", "up", "up_read", "sil", "hidden", "down", "down_read",
            "scatter", "sum", "sum_read", "zero", "step", "pair_step")}
        m3_landed = [sem(f"m3_landed{i}") for i in range(SLOTS)]
        x1_ready, blocks_ready, conv_ready, convln_ready, keep_ready, log_ready = (sem(n) for n in (
            "x1_ready", "blocks_ready", "conv_ready", "convln_ready", "keep_ready", "log_ready"))
        y2_ready, relu_ready, x2_ready, u1_ready, cq_ready, rope_ready = (sem(n) for n in (
            "y2_ready", "relu_ready", "x2_ready", "u1_ready", "cq_ready", "rope_ready"))
        ret_scores, ret_decayed, ret_out, ret_copied, ret_ready, mlarope_ready = (sem(n) for n in (
            "ret_scores", "ret_decayed", "ret_out", "ret_copied", "ret_ready", "mlarope_ready"))
        ret_gated, merge_ready, u2_ready, final_ready, mla_ready, convsilu_ready = (sem(n) for n in (
            "ret_gated", "merge_ready", "u2_ready", "final_ready", "mla_ready", "convsilu_ready"))
        att = {n: sem("att_" + n) for n in (
            "scores", "scores_read", "shift", "probs", "turned", "turned_copied", "out", "out_read", "sink")}
        lin = {n: sem("lin_" + n) for n in (
            "cum", "qdiff", "qexp", "queries", "kexp", "keys", "keys_used", "ddiff", "dexp", "diag", "diag_used", "tiles",
            "merged", "out", "read")}

        sS, sP, sPT = carve(6400, 4, S), carve(7424, 4, S), carve(8448, 2, 4, P)
        BIASR, BIASCR, flip = carve(0, 8, S), carve(2048, NT, 4, NCMP), carve(2304, P)
        Q1, AV = carve(0, 4, S), carve(1024, NT, P)
        GQ, GK = carve(1280, 2, S), carve(1792, 2, S)
        GVV, GG = carve(2304, NT, BANK), carve(3328, NT, BANK)
        GA, GZ, GL, CUM = carve(4352, S), carve(4608, 2, S), carve(5120, 2, S), carve(5632, 2, S)
        b1row, b2row = scr[0:E1, 0:2 * F1], scr[0:E1, 2560:3584]
        b1T = carve(2048, 16, E1)
        LG, GT, LX = carve(3584, NT, E1), carve(3648, NT, E1), carve(3712, NT, E1)
        gatesT = scr[0:E1, 3776:4032]
        XG, aT = carve(4032, KT, C), carve(4800, KT, C)
        pre, sig = carve(5568, 2, 4, C), carve(6336, 2, 2, C)
        YS = scr[0:C, 6720:7744]
        PICK, PICKG = carve(7744, NT, C), carve(7936, NT, C)
        GPT = shaped(scr[0:C, 8128:8640], (2, S))
        RANK, GATE = carve(8640, NT, 128), carve(8896, NT, 128)
        MASK = carve(9152, NT, E1)
        MASKED = carve(9216, 3 * E1)
        cmp1, cmp2, before = carve(9664, 32, 32), carve(10688, 32, 32), carve(11776, 32, 32)
        b1cur, gcur, rcur = carve(11712, 16), carve(11728, NT), carve(11732, NT)
        GLA_KD, GLA_LD = carve(10496, 2, 2, S), carve(6400, BLK, S)
        LQ = carve(11520, 2, NBLK, BLK)
        GLA_AT, NCUM1 = (carve(12032, 4, S), carve(4608, 4, P)), carve(5120, 2, S)
        Q2, QM = carve(0, 2, S), carve(512, 2, S)
        VS, VW, VM = carve(1024, NT, 64), carve(1152, NT, 64), carve(1280, NT, S)
        GN = carve(1792, NT, 12)
        KCT, BLOCKS, CHID = carve(1824, 2, S), carve(2336, 2, 16, NCMP), carve(2816, 2, 2, NCMP)
        VC = carve(2880, 64)
        cw2 = shaped(MOD[:, 0, 0:256], (2, 2, 64))
        pww = shaped(MOD[:, 0, 256:768], (2, S))
        convrow = MOD[0:CONVW, 0, 768:1024]
        convw = carve(2944, 2, 32)
        CA, CG, CACC = carve(3520, 2, CONVW - 1 + S), carve(4096, 2, S), carve(4608, 2, S)
        CTOK, CSIL = carve(5120, NT, S), carve(5632, 2, S)
        QH, FH, IH, GH = carve(9472, 2, S), carve(9984, 2, S), carve(10496, NT, S), carve(11008, NT, S)
        HCUM, HLOG = carve(11520, 2, S), carve(4096, 2, S)
        ONSA = carve(12032, 4, 64)
        HG_KD, HG_LD, LQ2 = carve(0, 2, 2, S), carve(5120, BLK, S), carve(1024, 2, NBLK, BLK)
        HG_AT, NCUM2 = (carve(1824, 4, S), carve(3520, 4, P)), carve(12032, 2, S)
        FFT = carve(0, 32, S)
        RQ, RK = carve(0, 8, S), carve(2048, 8, S)
        RV, RG = carve(4096, NT, D), carve(6144, NT, D)
        RTMP = carve(8192, 2, 4, S)
        RT = carve(8192, 4, 2, S)
        CQ, CKV, KPE = carve(10240, NT, 384), carve(11008, NT, S), carve(11520, 2, S)
        CQT, CKVT = carve(12032, 3, S), carve(12800, 2, S)
        MG1, MG2 = carve(0, NT, D), MOD[:, 0:2, :]
        QNT, QPE, KNT, VV = carve(0, 8, S), carve(2048, 2, 4, S), carve(4096, 8, S), carve(9472, NT, D)
        YM = carve(0, NT, D)
        LR, GE, LE = carve(0, NT, 36), carve(128, NT, E3), carve(256, NT, G3 + E3)
        cmp3, cmp4 = carve(512, 4, 8, 8), carve(768, 4, 8, 8)
        XG3, aT3 = carve(5120, KT, C), carve(5888, 2, 2, C)
        sil3 = carve(6272, 2, 2, C)
        YA = scr[0:C, 6656:7680]
        PICK3, RANK3, MASK3 = carve(7680, NT, C), carve(7872, NT, 16), carve(7904, NT, G3)
        PT3, GS, gcur3, rcur3 = scr[0:C, 7936:8192], scr[0:C, 8192:8224], scr[0:C, 8224:8226], carve(8226, NT)
        MASKED3 = carve(8232, 3 * G3)
        zero_row = scr[0:1, 8256:8768]
        before3 = carve(4096, 32, 32)

        units = []

        def unit(kind, tile, group, nk, width):
            units.append((kind, tile, group, nk, width))

        for t in range(NT):
            for grp in range(2):
                unit("window", t, grp, P * (t + 1), 64)
        for t in range(NT):
            for kind in ("cmp", "sel", "win", "moba"):
                unit(kind, t, 0, NCMP if kind == "cmp" else P * (t + 1), 64)
        for t in range(NT):
            for grp in range(2):
                unit("mla", t, grp, P * (t + 1), P)
        n_window, n_nsa = 4, 8

        def bias_of(u, pair):
            kind, t, grp, nk, _ = units[u]
            if kind == "cmp":
                return BIASC[:, t, 2 * pair:2 * pair + 2, :]
            k0 = S - nk
            if kind in ("sel", "win", "moba"):
                h = (4 if kind == "moba" else 0) + 2 * pair
                return BIAS[:, h:h + 2, k0:S]
            m = window if kind == "window" else causal
            return m[:, k0:S].unsqueeze(1).to_broadcast([P, 2, nk])

        def values_of(u, kt, h):
            kind, _, grp, _, _ = units[u]
            if kind == "window":
                return AV[:, kt, 64 * grp:64 * grp + 64]
            if kind == "cmp":
                return VC[0:NCMP, :]
            if kind == "sel":
                return VS[:, kt, :]
            if kind == "win":
                return VW[:, kt, :]
            if kind == "moba":
                return VM[:, kt, 64 * h:64 * h + 64]
            return VV[:, kt, (4 * grp + h) * P:(4 * grp + h + 1) * P]

        block = ctx.enter_context(nc.Block())

        def kpn(ap):
            return ap.rearrange("(k p) n -> p k n", p=P)

        def slot(s, k, n, off=0):
            return shaped(ring[:, s % SLOTS, off:off + k * n], (k, n))

        n_consts = 31

        @block.sync
        def _(sp):
            at = [0]

            def slab():
                s = at[0]
                at[0] += 1
                if s >= SLOTS:
                    sp.wait_ge(product_ready, release[s - SLOTS])
                return s

            def load(s, dst, src):
                sp.dma_start(dst, src).then_inc(slab_landed[s % SLOTS], 16)

            def column_slabs(w, bounds, view=kpn):
                for lo, hi in zip(bounds, bounds[1:]):
                    s = slab()
                    load(s, slot(s, KT, hi - lo), view(w[:, lo:hi]))

            sp.dma_start(X[:, :, :], I["x"][0].rearrange("(a p) n -> p a n", p=P)).then_inc(x_landed, 16)

            def ada_view(ap):
                return ap.rearrange("(p k) n -> p k n", k=KT)

            wide = list(range(0, 6 * D + 1, BANK))
            column_slabs(I["w_ada"][0], wide, ada_view)
            column_slabs(I["w_in"][0], [0, 512, 1024, 1536, 2048, 2320])
            column_slabs(I["w_out"][0], [0, 512, 1024])
            sp.wait_ge(product_ready, end["out1"])
            sp.wait_ge(m1["rounds"], 1)
            n_rounds = sp.value_load(rounds[0:1, 0:1], min_val=1, max_val=ROUNDS)
            with sp.Fori(0, n_rounds) as r:
                with sp.Fori(0, E1) as e:
                    n = E1 * r + e
                    held = [("up", 4 * n + 1), ("down", 2 * n + 1), ("down", 2 * n + 2),
                            ("up", 4 * n + 2), ("up", 4 * n + 3), ("up", 4 * n + 4)]
                    for j in range(6):
                        sp.wait_ge(m1[held[j][0]], held[j][1])
                        w = I["w_mlp1"][0][e][:, BANK * j:BANK * (j + 1)] if j < 4 else \
                            I["w_mlp2"][0][e][:, BANK * (j - 4):BANK * (j - 3)]
                        sp.dma_start(slot(j, KT, BANK), kpn(w)).then_inc(m1_landed[j % SLOTS], 16)
            sp.wait_ge(m1["sum"], 1)
            column_slabs(I["w_in_2"][0], [0, 512, 908, 1420, 1932, 2444, 2956])
            for kv in range(2):
                s = slab()
                load(s, slot(s, 16, S), kpn(I["nsa_cmp_w1_2"][0, kv]))
            column_slabs(I["w_out_2"][0], [0, 512, 1024])
            column_slabs(I["w_ff1_2"][0], list(range(0, FF2 + 1, BANK)))
            for n in range(8):
                s = slab()
                load(s, slot(s, 32, P), kpn(I["w_ff2_2"][0][:, P * n:P * (n + 1)]))
            column_slabs(I["w_ada_3"][0], wide, ada_view)
            w3 = I["w_in_3"][0]
            column_slabs(w3, list(range(0, 4097, BANK)) + [4480])
            s = slab()
            load(s, slot(s, KT, 320), kpn(w3[:, 4480:4800]))
            for half in range(2):
                load(s, slot(s, KT, 64, 2560)[:, :, 32 * half:32 * half + 32],
                     kpn(w3[:, 4736 + 32 * (1 - half):4768 + 32 * (1 - half)]))
            column_slabs(w3, [4800, 5312, 5824, 6336, 6848])
            column_slabs(I["w_ret_o_3"][0], [0, 512, 1024])
            for grp in range(2):
                s = slab()
                load(s, slot(s, 3, 768), kpn(I["w_uq_3"][0][:, 768 * grp:768 * (grp + 1)]))
                pe_cols = kpn(I["w_uq_3"][0]).rearrange("p k (h c) -> p k h c", h=8)
                for half in range(2):
                    dst = shaped(ring[:, s % SLOTS, 2304:3072], (3, 4, 64))[:, :, :, 32 * half:32 * half + 32]
                    c = P + 32 * (1 - half)
                    for k in range(3):
                        load(s, dst[:, k], pe_cols[:, k, 4 * grp:4 * grp + 4, c:c + 32])
            s = slab()
            load(s, slot(s, 2, 2048), kpn(I["w_ukv_3"][0]))
            column_slabs(I["w_mla_o_3"][0], [0, 512, 1024])
            column_slabs(I["w_out_3"][0], [0, 512, 1024])
            w1 = I["w1_3"][0].rearrange("g e d f -> (g e) d f")
            w3e = I["w3_3"][0].rearrange("g e d f -> (g e) d f")
            w2 = I["w2_3"][0].rearrange("g e f d -> (g e) f d")
            sp.wait_ge(product_ready, end["out3"])
            sp.wait_ge(m3["rounds"], 1)
            n_rounds = sp.value_load(rounds[0:1, 1:2], min_val=1, max_val=ROUNDS)
            with sp.Fori(0, n_rounds) as r:
                with sp.Fori(0, E3 // 2) as h:
                    n = E3 // 2 * r + h
                    for j in range(2):
                        sp.wait_ge(m3["up"], 2 * n + j + 1)
                        sp.dma_start(slot(j, KT, F3), kpn(w1[2 * h + j])).then_inc(m3_landed[j], 16)
                        sp.dma_start(slot(j, KT, F3, 2048), kpn(w3e[2 * h + j])).then_inc(m3_landed[j], 16)
                    sp.wait_ge(m3["down"], 4 * n + 1)
                    sp.dma_start(shaped(ring[:, 2, :], (4, D)),
                                 w2[bass.ds(2 * h, 2)].rearrange("e (k p) n -> p (e k) n", p=P)).then_inc(m3_landed[2], 16)
            sp.wait_ge(final_ready, 1)
            sp.dma_start(out[0].rearrange("(a p) n -> p a n", p=P), H[:, :, :]).then_inc(stored, 16)
            sp.wait_ge(stored, 16)

        @block.gpsimd
        def _(pool):
            n = [0]

            def const(dst, src):
                n[0] += 1
                pool.dma_start(dst, src).then_inc(consts_landed, 16)

            def row(ap):
                return ap.partition_broadcast(P)

            def vector(v):
                if v >= GVSLOTS:
                    pool.wait_ge(vec_used, v - GVSLOTS + 1)
                name = VECTORS[v]
                src = I[name] if name == "final_norm_3" else I[name][0]
                pool.dma_start(GV[:, v % GVSLOTS, :], row(src)).then_inc(vec_landed[v % GVSLOTS], 16)

            with nc.allow_non_contiguous_dma("short vectors"):
                const(cvec[:, 0, :], I["c"][0].rearrange("(p k) -> p k", k=KT))
                const(cvec[:, 1, :], I["c_3"][0].rearrange("(p k) -> p k", k=KT))
                const(ada_rows[0], I["b_ada"][0].rearrange("(n c) -> n c", c=BANK))
                const(ident[:, :], I["c_ident"])
                const(flip, I["c_flip"])
                const(onehot, I["c_onehot"])
                const(tab[0:32, :], I["rel_bias_2"].rearrange("h b -> b h"))
                vector(0)
                vector(1)
                vector(2)
                const(window[:, :], I["c_window"])
                const(causal[:, :], I["c_causal"])
                const(diag[:, :], I["c_diag"])
                const(heads2[:, :], I["c_heads2"])
                const(tri[:, :], I["c_tri"])
                const(iota, I["c_iota"])
                const(wr1[:, :, :], kpn(I["w_router"][0]))
                const(wr3[:, :, 0:G3], kpn(I["w_grp_3"][0]))
                const(wr3[:, :, G3:], kpn(I["w_exp_3"][0]))
                const(wgu[:, :], I["w_gla_gate_up"][0])
                const(b_gate, I["b_gla_gate"][0].rearrange("(c p) -> p c", p=P))
                const(conv_bias, I["conv_dw_b_2"][0].rearrange("(c p) -> p c", p=P))
                const(cmp_b1, I["nsa_cmp_b1_2"][0].rearrange("a (c p) -> p a c", p=P))
                const(cmp_pe, I["nsa_cmp_pe_2"][0].rearrange("a (j r) d -> (r d) a j", r=2))
                const(b_router, row(I["b_router"][0]))
                const(b_route3[:, 0:G3], row(I["b_grp_3"][0]))
                const(b_route3[:, G3:], row(I["b_exp_3"][0]))
                const(qn_row, row(I["q_norm_3"][0]))
                const(kvn_row, row(I["kv_norm_3"][0]))
                const(gla_norm, row(I["g_gla_norm"][0]))
                const(sinks, row(I["sinks"][0]))
                const(conv_g, row(I["conv_ln_g_2"][0]))
                const(conv_b, row(I["conv_ln_b_2"][0]))
                const(hgrn_g, row(I["hgrn_norm_g_2"][0]))
            assert n[0] == n_consts
            for i, (area, value) in enumerate(((tab[32:33, :], 1.0), (ones[:, :], 1.0), (BD[:, :, :, :], 0.0),
                                               (QD[:, :, :, :, :], 0.0), (KC[:, :, :], 0.0))):
                pool.memset(area, value).then_inc(zeros_ready, 1)
                pool.wait_ge(zeros_ready, i + 1)
            pool.wait_ge(rel_stored, 16)
            rs = rel_scratch
            pool.dma_start(BIASR, bass.AP(rs.tensor, 0, [[1, P], [BANK, 8], [1, S]])).then_inc(rel_landed, 16)
            with nc.allow_non_contiguous_dma("every sixteenth distance"):
                for t in range(NT):
                    for h in range(4):
                        pool.dma_start(BIASCR[:, t, h, :], bass.AP(rs.tensor, 159 - P * t + BANK * h, [[1, P], [16, NCMP]]))\
                            .then_inc(rel_landed, 16)
            vector(3)
            pool.wait_ge(h2_ready, 1)
            pool.dma_start(b1row, I["b_mlp1"][0]).then_inc(moe1_params_landed, 16)
            pool.dma_start(b2row, I["b_mlp2"][0]).then_inc(moe1_params_landed, 16)
            pool.dma_start(before, I["c_before"].rearrange("p (a b) -> p a b", a=32)).then_inc(moe1_params_landed, 16)
            pool.dma_start(cw2, I["nsa_cmp_w2_2"][0].rearrange("a (c p) n -> p a c n", p=P)).then_inc(block2_params_landed, 16)
            pool.dma_start(pww, kpn(I["conv_pw_w_2"][0])).then_inc(block2_params_landed, 16)
            pool.dma_start(convrow, I["conv_dw_w_2"][0]).then_inc(block2_params_landed, 16)
            for v in range(4, 8):
                vector(v)
            pool.wait_ge(mix_ready, 2)
            pool.dma_start(decay, I["c_decay"].rearrange("p (h s) -> p h s", h=4)).then_inc(tables_landed, 16)
            pool.dma_start(ropes, I["c_ropes"].rearrange("p (h s) -> p h s", h=4)).then_inc(tables_landed, 16)
            pool.wait_ge(y2_ready, 1)
            pool.dma_start(ada_rows[1], I["b_ada_3"][0].rearrange("(n c) -> n c", c=BANK)).then_inc(ada3_landed, 16)
            for v in range(8, 11):
                vector(v)
            pool.wait_ge(u2_ready, 1)
            pool.dma_start(before3, I["c_before"].rearrange("p (a b) -> p a b", a=32)).then_inc(before_landed, 16)

        @block.tensor
        def _(pe):
            done = [0]
            row_groups = [0]

            def bank():
                if done[0] >= PBANKS:
                    pe.wait_ge(product_free, done[0] - PBANKS + 1)
                return ps[:, done[0] % PBANKS, :]

            def close(mm):
                mm.then_inc(product_ready, 1)
                done[0] += 1

            def weights(s):
                pe.wait_ge(slab_landed[s % SLOTS], landed[s])

            def mm_k(o, lhs, rhs, nk, begin=True, end=True):
                for k in range(nk):
                    mm = pe.matmul(o, lhs(k), rhs(k), start=begin and k == 0, stop=end and k == nk - 1)
                return mm

            def turn(src, dst_k=None):
                for a in range(NT):
                    for half in range(2):
                        b = bank()
                        for k in range(4):
                            mm = pe.transpose(b[:, P * k:P * (k + 1)], src[:, a, P * (4 * half + k):P * (4 * half + k + 1)],
                                              ident[:, :])
                        close(mm)

            def tokens(rhs, width, lhs=HT, nk=KT, tiles=range(NT)):
                if width * NT <= BANK:
                    b = bank()
                    for a in range(NT):
                        mm = mm_k(b[:, a * width:(a + 1) * width], lambda k: lhs[:, k, P * a:P * (a + 1)], rhs, nk)
                    close(mm)
                else:
                    for a in range(NT):
                        b = bank()
                        close(mm_k(b[:, 0:width], lambda k: lhs[:, k, P * a:P * (a + 1)], rhs, nk))

            def features(cols_of, rhs=HT, nk=KT, m=P):
                b = bank()
                for i, c in enumerate(cols_of):
                    if isinstance(c, tuple):
                        for half in range(2):
                            mm = mm_k(b[64 * half:64 * half + 64, S * i:S * (i + 1)], c[half], lambda k: rhs[:, k, :], nk)
                    else:
                        mm = mm_k(b[0:m, S * i:S * (i + 1)], c, lambda k: rhs[:, k, :], nk)
                close(mm)

            def col(w, c, n=P):
                return lambda k: w[:, k, c:c + n]

            def twice(w, c):
                return col(w, c, 64), col(w, c, 64)

            def wide_stage(name, lhs=HT, width=BANK):
                n = len(dict((x[0], x[1]) for x in STAGES)[name])
                for i in range(n):
                    s = first_slab[name] + i
                    weights(s)
                    w = slot(s, KT, BANK)
                    tokens(lambda k: w[:, k, :], BANK, lhs)

            def modulation(name, j):
                for i in range(12):
                    s = first_slab[name] + i
                    weights(s)
                    w = slot(s, KT, BANK)
                    b = bank()
                    mm_k(b, lambda k: csil[:, j, k:k + 1].to_broadcast([P, P]), lambda k: w[:, k, :], KT, end=False)
                    close(pe.matmul(b, ident[0:12, i:i + 1].to_broadcast([12, P]), ada_rows[j], start=False, stop=True))

            def queries_of(u, pair):
                kind, t, grp, _, _ = units[u]
                q = {"window": Q1[:, 2 * grp + pair, :] if kind == "window" else None, "cmp": Q2[:, pair, :],
                     "sel": Q2[:, pair, :], "win": Q2[:, pair, :], "moba": QM[:, pair, :],
                     "mla": QPE[:, 0, 2 * grp + pair, :] if kind == "mla" else None}[kind]
                return q[:, P * t:P * (t + 1)]

            def keys_of(u, pair):
                kind, t, grp, nk, _ = units[u]
                if kind == "cmp":
                    return KC[:, :, :]
                return BD[:, {"window": grp, "sel": 0, "win": 1, "moba": 2 + pair, "mla": 0}[kind], :, 0:nk]

            def scores(u):
                kind, t, grp, nk, _ = units[u]
                if u >= 1:
                    pe.wait_ge(att["scores_read"], u)
                for pair in range(2):
                    o = ps[:, 4 + pair, 0:2 * nk].rearrange("p (h n) -> p h n", h=2)
                    if kind != "mla":
                        mm = pe.matmul(o, queries_of(u, pair), keys_of(u, pair), start=True, stop=True)
                        continue
                    for j in range(2):
                        h = 4 * grp + 2 * pair + j
                        pe.matmul(o[:, j, :], QNT[:, h, P * t:P * (t + 1)], KNT[:, h, 0:nk], start=True, stop=False)
                        mm = pe.matmul(o[:, j, :], queries_of(u, pair), keys_of(u, pair)[:, j, :], start=False, stop=True)
                mm.then_inc(att["scores"], 1)

            def attend(u):
                kind, t, grp, nk, width = units[u]
                pe.wait_ge(att["probs"], u + 1)
                if u >= 1:
                    pe.wait_ge(att["turned_copied"], u)
                for kt in range(-(-nk // P)):
                    n = min(P, nk - P * kt)
                    for h in range(4):
                        mm = pe.transpose(ps[0:n, 6 + kt, P * h:P * (h + 1)], sP[:, h, P * kt:P * kt + n], ident[:, :])
                mm.then_inc(att["turned"], 1)
                pe.wait_ge(att["turned_copied"], u + 1)
                if u >= 1:
                    pe.wait_ge(att["out_read"], u)
                kts = range(-(-nk // P))
                for h in range(4):
                    for kt in kts:
                        n = min(P, nk - P * kt)
                        mm = pe.matmul(ps[:, 3, h * width:(h + 1) * width], sPT[0:n, kt, h, :], values_of(u, kt, h),
                                       start=kt == 0, stop=kt == kts[-1])
                mm.then_inc(att["out"], 1)

            def attention(u0, u1):
                scores(u0)
                for u in range(u0, u1):
                    if u + 1 < u1:
                        scores(u + 1)
                    attend(u)

            def linear_attention(n, KDb, LDb, AT, v, dv):
                pe.wait_ge(lin["queries"], n + 1)
                for i in range(NBLK):
                    pe.wait_ge(lin["keys"], NBLK * n + i + 1)
                    for tile in range(1 if i < P // BLK else 2):
                        for pair in range(2):
                            if tile == 0:
                                o = ps[:, 4 + pair, :].rearrange("p (h t) -> p h t", h=2)[:, :, BLK * i:BLK * (i + 1)]
                            else:
                                o = ps[:, 6, :].rearrange("p (h t) -> p h t", h=4)[
                                    :, 2 * pair:2 * pair + 2, BLK * i - P:BLK * (i + 1) - P]
                            mm = pe.matmul(o, KDb[:, i % 2, pair, P * tile:P * (tile + 1)], QD[:, pair, i, :, :],
                                           start=True, stop=True)
                    mm.then_inc(lin["keys_used"], 1)
                for pair in range(2):
                    pe.wait_ge(lin["diag"], 2 * n + pair + 1)
                    for tile in range(NT):
                        for i in range(BLK):
                            c = ((tile * 2 + pair) * BLK + i) * 2
                            mm = pe.matmul(ps[:, 7, c:c + 2], LDb[:, i, P * tile:P * (tile + 1)], heads2[:, :],
                                           start=True, stop=True)
                    mm.then_inc(lin["diag_used"], 1)
                pe.wait_ge(lin["merged"], n + 1)
                for a in range(NT):
                    for h in range(4):
                        for kt in range(a + 1):
                            w = AT[0][:, h, P * a:P * (a + 1)] if kt == 0 else AT[1][:, h, :]
                            mm = pe.matmul(ps[:, 4 + a, h * dv:(h + 1) * dv], w, v[:, kt, h * dv:(h + 1) * dv],
                                           start=kt == 0, stop=kt == a)
                mm.then_inc(lin["out"], 1)

            pe.wait_ge(consts_landed, 16 * n_consts)
            pe.wait_ge(zeros_ready, 5)
            b = bank()
            close(pe.matmul(b[0:8, :], tab, onehot, start=True, stop=True))
            pe.wait_ge(cond_ready, 1)
            modulation("ada1", 0)
            pe.wait_ge(rel_landed, 16 * (1 + 4 * NT))
            for i in range(4):
                b = bank()
                close(pe.matmul(b, flip, BIASR[:, 2 * i:2 * i + 2, :], start=True, stop=True))
            b = bank()
            close(pe.matmul(b[:, 0:NT * 4 * NCMP], flip, BIASCR, start=True, stop=True))
            pe.wait_ge(h1_ready, 1)
            turn(H)
            pe.wait_ge(product_free, end["h1T"])
            s = first_slab["in1"]
            weights(s)
            w = slot(s, KT, BANK)
            features([col(w, 0), col(w, P)])
            features([col(w, 2 * P), col(w, 3 * P)])
            weights(s + 1)
            w = slot(s + 1, KT, BANK)
            features([twice(w, 0), twice(w, 64)])
            tokens(lambda k: w[:, k, P:2 * P], P)
            features([col(w, S), col(w, S + P)])
            weights(s + 2)
            w2 = slot(s + 2, KT, BANK)
            features([col(w2, 0), col(w2, P)])
            tokens(lambda k: w2[:, k, S:2 * S], S)
            weights(s + 3)
            w3 = slot(s + 3, KT, BANK)
            tokens(lambda k: w3[:, k, 0:S], S)
            tokens(lambda k: w3[:, k, S:2 * S], S)
            weights(s + 4)
            w4 = slot(s + 4, KT, 272)
            tokens(lambda k: w4[:, k, 0:S], S)
            features([col(w4, S, 16)], m=16)
            b = bank()
            pe.wait_ge(product_free, end["in1"])
            for c in range(2):
                mm = pe.matmul(b[:, S * c:S * (c + 1)], wgu[:, P * c:P * (c + 1)], GA[0:16, :], start=True, stop=True)
            close(mm)
            attention(0, n_window)
            linear_attention(0, GLA_KD, GLA_LD, GLA_AT, GVV, P)
            pe.wait_ge(mix_ready, 1)
            turn(Y)
            pe.wait_ge(product_free, end["mix1T"])
            wide_stage("out1")
            pe.wait_ge(h2_ready, 1)
            turn(H)
            pe.wait_ge(product_free, end["h2T"])
            tokens(lambda k: wr1[:, k, :], E1)
            pe.wait_ge(gates_ready, 1)
            b = bank()
            for a in range(NT):
                mm = pe.transpose(b[0:E1, P * a:P * (a + 1)], GT[:, a, :], ident[:, :])
            close(mm)
            pe.wait_ge(moe1_params_landed, 48)
            b = bank()
            b1v = b1row.rearrange("e (c f two) -> e c two f", two=2, f=P)
            for c in range(8):
                for j in range(2):
                    mm = pe.transpose(b[:, E1 * (2 * c + j):E1 * (2 * c + j + 1)], b1v[:, c, j, :], ident[0:E1, 0:E1])
            close(mm)
            b = bank()
            for a in range(NT):
                pe.matmul(b[:, E1 * a:E1 * (a + 1)], tri[:, :], MASK[:, a, :], start=True, stop=a == 0)
                if a == 1:
                    pe.matmul(b[:, E1:2 * E1], ones[:, 0:P], MASK[:, 0, :], start=False, stop=True)
            for a in range(NT):
                mm = pe.matmul(b[:, 2 * E1:3 * E1], ones[:, 0:P], MASK[:, a, :], start=a == 0, stop=a == 1)
            close(mm)
            pe.wait_ge(product_free, end["gates1T"])

            def sum_bank(a, half):
                return ps[:, 4 + 2 * a + half, :]

            for a in range(NT):
                for half in range(2):
                    pe.matmul(sum_bank(a, half), gatesT[:, P * a:P * (a + 1)], b2row[:, BANK * half:BANK * (half + 1)],
                              start=True, stop=False, skip_group_check=True)
            pe.sem_inc(m1["up"], 1)
            pe.sem_inc(m1["down"], 2)

            def gather(n, x):
                pe.wait_ge(m1["pick"], n + 1)
                for half in range(2):
                    for k in range(4):
                        mm = mm_k(ps[:, 2 + half, C * k:C * (k + 1)],
                                  lambda a: H[:, a, P * (4 * half + k):P * (4 * half + k + 1)], lambda a: PICK[:, a, :], NT)
                    mm.then_inc(m1["gather"], 1)
                for a in range(NT):
                    mm = pe.transpose(ps[0:C, 0, P * a:P * (a + 1)], PICKG[:, a, :], ident[:, :])
                mm.then_inc(m1["gather"], 1)

            def scatter(x, last=False):
                for a in range(NT):
                    for half in range(2):
                        mm = pe.matmul(sum_bank(a, half), GPT[:, x, P * a:P * (a + 1)], YS[:, BANK * half:BANK * (half + 1)],
                                       start=False, stop=last, skip_group_check=True)
                return mm

            pe.wait_ge(m1["rounds"], 1)
            n_rounds = pe.value_load(rounds[0:1, 0:1], min_val=1, max_val=ROUNDS)
            pe.wait_ge(product_free, end["rank1"])
            gather(0, 0)
            with pe.Fori(0, n_rounds) as r:
                with pe.Fori(0, E1 // 2) as h:
                    for x in range(2):
                        n = E1 * r + 2 * h + x
                        pe.wait_ge(m1["gather_read"], 3 * n + 3)
                        for j in range(4):
                            pe.wait_ge(m1_landed[j % SLOTS], 32 * n + 16 * (j // SLOTS) + 16)
                            if j:
                                pe.wait_ge(m1["up_read"], 4 * n + j)
                            wv = slot(j, KT, BANK).rearrange("p k (c f two) -> p k c two f", two=2, c=2)
                            for c in range(2):
                                for two_ in range(2):
                                    mm = mm_k(ps[:, j % 2, C * (2 * c + two_):C * (2 * c + two_ + 1)],
                                              lambda k: wv[:, k, c, two_, :], lambda k: XG[:, k, :], KT)
                            mm.then_inc(m1["up"], 1)
                            if j == 0:
                                pe.wait_ge(m1["down_read"], 2 * n + 2)
                                scatter(1 - x).then_inc(m1["scatter"], 1)
                        pe.wait_ge(m1["up_read"], 4 * n + 4)
                        gather(n + 1, 1 - x)
                        pe.wait_ge(m1["hidden"], 4 * n + 4)
                        for j in range(2):
                            pe.wait_ge(m1_landed[(4 + j) % SLOTS], 32 * n + 32)
                            pe.wait_ge(m1["gather_read"], 3 * n + 4 + j)
                            w = slot(4 + j, KT, BANK)
                            mm_k(ps[0:C, 2 + j, :], lambda k: aT[:, k, :], lambda k: w[:, k, :], KT).then_inc(m1["down"], 1)
            n = E1 * n_rounds
            pe.wait_ge(m1["down_read"], 2 * n + 2)
            pe.wait_ge(m1["up_read"], 4 * n + 1)
            pe.wait_ge(m1["gather_read"], 3 * n + 3)
            scatter(1, last=True).then_inc(m1["sum"], 1)
            pe.wait_ge(x1_ready, 1)
            pe.wait_ge(block2_params_landed, 48)
            turn(X)
            b = bank()
            for c in range(2):
                mm = pe.transpose(b[:, 32 * c:32 * c + CONVW], convrow[:, P * c:P * (c + 1)], ident[0:CONVW, 0:CONVW])
            close(mm)
            pe.wait_ge(product_free, end["x1T"])
            s = first_slab["in2"]
            weights(s)
            w = slot(s, KT, BANK)
            features([col(w, 0), col(w, P)])
            features([twice(w, 256), twice(w, 320)])
            features([twice(w, 384)])
            tokens(lambda k: w[:, k, 448:512], 64)
            weights(s + 1)
            w1 = slot(s + 1, KT, 396)
            features([twice(w1, 0)])
            tokens(lambda k: w1[:, k, 64:140], 76)
            features([col(w1, 140), col(w1, 268)])
            for i in range(4):
                weights(s + 2 + i)
                wi = slot(s + 2 + i, KT, BANK)
                if i < 3:
                    features([col(wi, 0), col(wi, P)])
                if i in (1, 2):
                    features([col(wi, S), col(wi, S + P)])
                if i == 3:
                    tokens(lambda k: wi[:, k, 0:S], S)
                if i in (0, 3):
                    tokens(lambda k: wi[:, k, S:2 * S], S)
            pe.wait_ge(blocks_ready, 1)
            for kv in range(2):
                s = first_slab["cmp2"] + kv
                weights(s)
                w = slot(s, 16, S)
                b = bank()
                for c in range(2):
                    mm = mm_k(b[:, NCMP * c:NCMP * (c + 1)], lambda k: w[:, k, P * c:P * (c + 1)],
                              lambda k: BLOCKS[:, kv, k, :], 16)
                close(mm)
            pe.wait_ge(product_free, end["cmp2"] - 2)
            b = bank()
            for half in range(2):
                mm = mm_k(b[64 * half:64 * half + 64, 0:NCMP], lambda k: cw2[:, 0, k, :], lambda k: CHID[:, 0, k, :], 2)
            close(mm)
            b = bank()
            close(mm_k(b[0:NCMP, 0:64], lambda k: CHID[:, 1, k, :], lambda k: cw2[:, 1, k, :], 2))
            pe.wait_ge(product_free, end["cmp2"])
            attention(n_window, n_window + n_nsa)
            pe.wait_ge(conv_ready, 1)
            b = bank()
            for a in range(NT):
                for c in range(2):
                    mm = pe.transpose(b[:, S * a + P * c:S * a + P * (c + 1)], CACC[:, c, P * a:P * (a + 1)], ident[:, :])
            close(mm)
            pe.wait_ge(convsilu_ready, 1)
            b = bank()
            for c in range(2):
                for a in range(NT):
                    mm = pe.transpose(b[:, S * c + P * a:S * c + P * (a + 1)], CTOK[:, a, P * c:P * (c + 1)], ident[:, :])
            close(mm)
            pe.wait_ge(product_free, end["convback"])
            tokens(lambda k: pww[:, k, :], S, lhs=CSIL, nk=2)
            linear_attention(1, HG_KD, HG_LD, HG_AT, IH, 64)
            pe.wait_ge(mix_ready, 2)
            turn(Y)
            pe.wait_ge(product_free, end["mix2T"])
            wide_stage("out2")
            pe.wait_ge(y2_ready, 1)
            turn(X)
            pe.wait_ge(product_free, end["y2T"])
            for i in range(8):
                s = first_slab["ff1"] + i
                weights(s)
                w = slot(s, KT, BANK)
                features([col(w, 0), col(w, P)])
                features([col(w, 2 * P), col(w, 3 * P)])
            pe.wait_ge(relu_ready, 16)
            for i in range(8):
                s = first_slab["ff2"] + i
                weights(s)
                w = slot(s, 32, P)
                tokens(lambda k: w[:, k, :], P, lhs=FFT, nk=32)
            pe.wait_ge(ada3_landed, 16)
            modulation("ada3", 1)
            pe.wait_ge(u1_ready, 1)
            turn(H)
            pe.wait_ge(product_free, end["u1T"])
            s = first_slab["in3"]
            for i in range(9):
                weights(s + i)
                w = slot(s + i, KT, BANK if i < 8 else 384)
                if i < 4:
                    features([col(w, 0), col(w, P)])
                    features([col(w, 2 * P), col(w, 3 * P)])
                else:
                    tokens(lambda k: w[:, k, :], BANK if i < 8 else 384)
            weights(s + 9)
            w = slot(s + 9, KT, 320)
            wx = slot(s + 9, KT, 64, 2560)
            tokens(lambda k: w[:, k, 0:S], S)
            features([twice(w, S), twice(wx, 0)])
            pe.wait_ge(rope_ready, 1)
            pe.wait_ge(product_free, end["in3"])

            def ret_out_of(h):
                pe.wait_ge(ret_decayed, h + 1)
                if h >= 2:
                    pe.wait_ge(ret_copied, h - 1)
                for a in range(NT):
                    for kt in range(a + 1):
                        mm = pe.matmul(ps[:, 6 + h % 2, S * a:S * (a + 1)], RT[:, h, kt, P * a:P * (a + 1)],
                                       RV[:, kt, S * h:S * (h + 1)], start=kt == 0, stop=kt == a)
                mm.then_inc(ret_out, 1)

            for h in range(4):
                if h >= 2:
                    pe.wait_ge(ret_decayed, h - 1)
                for kt in range(NT):
                    o = ps[:, 4 + h % 2, 0:S] if kt == 0 else ps[:, 4 + h % 2, S:S + P]
                    mm = mm_k(o, lambda c: RK[:, 2 * h + c, P * kt:P * (kt + 1)], lambda c: RQ[:, 2 * h + c, P * kt:S], 2)
                mm.then_inc(ret_scores, 1)
                if h >= 1:
                    ret_out_of(h - 1)
            ret_out_of(3)
            wide_stage("gates3")
            pe.wait_ge(ret_ready, 1)
            turn(Y)
            pe.wait_ge(product_free, end["retT"])
            wide_stage("reto")
            pe.wait_ge(cq_ready, 1)
            for a in range(NT):
                b = bank()
                for c in range(3):
                    mm = pe.transpose(b[:, P * c:P * (c + 1)], CQ[:, a, P * c:P * (c + 1)], ident[:, :])
                close(mm)
            b = bank()
            for c in range(2):
                for a in range(NT):
                    mm = pe.transpose(b[:, S * c + P * a:S * c + P * (a + 1)], CKV[:, a, P * c:P * (c + 1)], ident[:, :])
            close(mm)
            pe.wait_ge(product_free, end["cqT"])
            for grp in range(2):
                s = first_slab["uq"] + grp
                weights(s)
                w = slot(s, 3, 768).rearrange("p k (h c) -> p k h c", h=4)
                wx = shaped(ring[:, s % SLOTS, 2304:3072], (3, 4, 64))
                for j in range(2):
                    features([lambda k, h=2 * j + i: w[:, k, h, 0:P] for i in range(2)], rhs=CQT, nk=3)
                features([tuple(lambda k, h=2 * i + x: w[:, k, h, P:] for x in range(2)) for i in range(2)], rhs=CQT, nk=3)
                features([tuple(lambda k, h=2 * i + x: wx[:, k, h, :] for x in range(2)) for i in range(2)], rhs=CQT, nk=3)
            s = first_slab["ukv"]
            weights(s)
            w = slot(s, 2, 2048).rearrange("p k (h c) -> p k h c", h=8)
            for j in range(4):
                features([lambda k, h=2 * j + i: w[:, k, h, 0:P] for i in range(2)], rhs=CKVT, nk=2)
            for half in range(2):
                tokens(lambda k: w[:, k, 4 * half:4 * half + 4, P:], BANK, lhs=CKVT, nk=2)
            pe.wait_ge(mlarope_ready, 1)
            pe.wait_ge(product_free, end["ukv"])
            attention(n_window + n_nsa, len(units))
            pe.wait_ge(mla_ready, 1)
            turn(Y)
            pe.wait_ge(product_free, end["mlaT"])
            wide_stage("mlao")
            pe.wait_ge(merge_ready, 1)
            turn(H)
            pe.wait_ge(product_free, end["mergeT"])
            wide_stage("out3")
            pe.wait_ge(u2_ready, 1)
            turn(H)
            pe.wait_ge(product_free, end["u2T"])
            tokens(lambda k: wr3[:, k, :], G3 + E3)
            pe.wait_ge(product_free, end["route3"])
            pe.wait_ge(m3["zero"], 1)
            for a in range(NT):
                for half in range(2):
                    pe.matmul(sum_bank(a, half), ones[0:1, 0:P], zero_row, start=True, stop=False, skip_group_check=True)
            b = bank()
            for a in range(NT):
                pe.matmul(b[:, G3 * a:G3 * (a + 1)], tri[:, :], MASK3[:, a, :], start=True, stop=a == 0)
                if a == 1:
                    pe.matmul(b[:, G3:2 * G3], ones[:, 0:P], MASK3[:, 0, :], start=False, stop=True)
            for a in range(NT):
                mm = pe.matmul(b[:, 2 * G3:3 * G3], ones[:, 0:P], MASK3[:, a, :], start=a == 0, stop=a == 1)
            close(mm)
            pe.sem_inc(m3["up"], 2)
            pe.sem_inc(m3["down"], 1)
            pe.sem_inc(m3["scatter"], 1)
            pe.wait_ge(m3["rounds"], 1)
            n_rounds = pe.value_load(rounds[0:1, 1:2], min_val=1, max_val=ROUNDS)
            pe.wait_ge(product_free, end["rank3"])
            with pe.Fori(0, n_rounds) as r:
                with pe.Fori(0, G3) as g:
                    n = G3 * r + g
                    pe.wait_ge(m3["pick"], n + 1)
                    pe.wait_ge(m3["down_read"], 16 * n + 2)
                    pe.wait_ge(m3["up_read"], 8 * n + 2)
                    for half in range(2):
                        for k in range(4):
                            mm = mm_k(ps[:, 2 + half, C * k:C * (k + 1)],
                                      lambda a: H[:, a, P * (4 * half + k):P * (4 * half + k + 1)],
                                      lambda a: PICK3[:, a, :], NT)
                        mm.then_inc(m3["gather"], 1)
                    for a in range(NT):
                        pe.transpose(ps[0:C, 0, P * a:P * (a + 1)], PICK3[:, a, :], ident[:, :])
                    mm_k(ps[0:C, 0, S:S + E3], lambda a: PICK3[:, a, :], lambda a: GE[:, a, :], NT).then_inc(m3["gather"], 1)
                    with pe.Fori(0, PG3 // 2) as h:
                        m = PG3 // 2 * n + h
                        pe.wait_ge(m3["gather_read"], 3 * n + 3)
                        for j in range(2):
                            pe.wait_ge(m3_landed[j], 32 * m + 32)
                            pe.wait_ge(m3["up_read"], 2 * m + j + 1)
                            for x in range(2):
                                w = slot(j, KT, F3, 2048 * x)
                                for c in range(2):
                                    mm = mm_k(ps[:, j, C * (2 * x + c):C * (2 * x + c + 1)],
                                              lambda k: w[:, k, P * c:P * (c + 1)], lambda k: XG3[:, k, :], KT)
                            mm.then_inc(m3["up"], 1)
                        pe.wait_ge(m3_landed[2], 16 * m + 16)
                        w = shaped(ring[:, 2, :], (4, D))
                        for j in range(2):
                            pe.wait_ge(m3["hidden"], 2 * m + j + 1)
                            for half in range(2):
                                pe.wait_ge(m3["down_read"], 4 * m + 2 * j + half + 1)
                                mm_k(ps[0:C, 2 + half, :], lambda k: aT3[:, j, k, :],
                                     lambda k: w[:, 2 * j + k, BANK * half:BANK * (half + 1)], 2).then_inc(m3["down"], 1)
                    pe.wait_ge(m3["down_read"], 16 * n + 18)
                    for a in range(NT):
                        for half in range(2):
                            mm = pe.matmul(sum_bank(a, half), PT3[:, P * a:P * (a + 1)], YA[:, BANK * half:BANK * (half + 1)],
                                           start=False, stop=False, skip_group_check=True)
                    mm.then_inc(m3["scatter"], 1)
            for a in range(NT):
                for half in range(2):
                    mm = pe.matmul(sum_bank(a, half), ones[0:1, 0:P], zero_row, start=False, stop=True, skip_group_check=True)
            mm.then_inc(m3["sum"], 1)

        @block.scalar
        def _(act):
            done = [0]
            steps = [0]
            roots = [0]

            def step(ins):
                ins.then_inc(act_step, 1)
                steps[0] += 1
                act.wait_ge(act_step, steps[0])

            def product():
                g = done[0]
                act.wait_ge(product_ready, g + 1)
                done[0] += 1
                return ps[:, g % PBANKS, :]

            def read(dst, src, func=ACT.Copy, **kw):
                act.activation(dst, src, func, **kw).then_inc(product_free, 1)

            def two(b, n=S):
                return b[:, 0:2 * n].rearrange("p (c n) -> p c n", c=2)

            def root(n):
                roots[0] += 1
                act.wait_ge(var_ready, roots[0])
                act.activation(std[:, 0:n], var[:, 0:n], ACT.Sqrt).then_inc(std_ready, 1)

            def turned():
                for a in range(NT):
                    for half in range(2):
                        b = product()
                        read(HT[:, 4 * half:4 * half + 4, P * a:P * (a + 1)], b.rearrange("p (k n) -> p k n", k=4))

            def wide(dst, func=ACT.Copy):
                for i in range(2):
                    for a in range(NT):
                        b = product()
                        read(dst[:, a, BANK * i:BANK * (i + 1)], b, func)

            def diagonal(b, first_slot, n):
                v = b[:, 0:S * n].rearrange("p (c n) -> p c n", c=n)
                act.activation(BD[0:64, first_slot:first_slot + n, 0, :], v[0:64], ACT.Copy)
                read(BD[64:P, first_slot:first_slot + n, 1, :], v[64:P])

            def modulation():
                for i in range(12):
                    b = product()
                    read(MOD.rearrange("p m d -> p (m d)")[:, BANK * i:BANK * (i + 1)], b)

            def attention(u0, u1):
                for u in range(u0, u1):
                    kind, t, grp, nk, _ = units[u]
                    st = att_stat[u % 2]
                    act.wait_ge(att["shift"], u + 1)
                    if u >= 1:
                        act.wait_ge(att["turned"], u)
                    if kind == "window":
                        act.activation(st["sink"], st["sink"], ACT.Exp)
                    for h in range(4):
                        ins = act.activation(sP[:, h, 0:nk], sS[:, h, 0:nk], ACT.Exp, bias=st["shift"][:, h:h + 1],
                                             accum_out=st["sum"][:, h:h + 1])
                    ins.then_inc(att["probs"], 1)
                    act.wait_ge(att["turned"], u + 1)
                    if u >= 1:
                        act.wait_ge(att["out"], u)
                    kts = -(-nk // P)
                    n = min(nk, P)
                    act.activation(sPT[0:n, 0:kts, :, :].rearrange("p k h q -> p k (h q)"), ps[0:n, 6:6 + kts, :], ACT.Copy)\
                        .then_inc(att["turned_copied"], 1)

            def linear_attention(n, cum, LQb, KDb, LDb, dst, dv):
                act.wait_ge(lin["qdiff"], n + 1)
                act.activation(LQb, LQb, ACT.Exp).then_inc(lin["qexp"], 1)
                act.wait_ge(lin["queries"], n + 1)
                for i in range(1, NBLK):
                    if i >= 2:
                        act.wait_ge(lin["keys_used"], NBLK * n + i - 1)
                    for pair in range(2):
                        ins = act.activation(KDb[:, i % 2, pair, 0:BLK * i], cum[:, pair, 0:BLK * i], ACT.Exp,
                                             bias=cum[:, pair, BLK * i - 1:BLK * i], scale=-1.0)
                    ins.then_inc(lin["kexp"], 1)
                for pair in range(2):
                    act.wait_ge(lin["ddiff"], 2 * n + pair + 1)
                    act.activation(LDb, LDb, ACT.Exp).then_inc(lin["dexp"], 1)
                act.wait_ge(lin["out"], n + 1)
                for a in range(NT):
                    act.activation(dst[:, a, :], ps[:, 4 + a, 0:4 * dv], ACT.Copy).then_inc(lin["read"], 1)

            def log_sigmoid_part(dst, src):
                step(act.activation(dst, src, ACT.Abs))
                step(act.activation(dst, dst, ACT.Exp, scale=-1.0))
                act.activation(dst, dst, ACT.Ln, bias=1.0).then_inc(loglog_ready, 1)

            act.wait_ge(consts_landed, 16 * n_consts)
            act.activation(csil[:, :, :], cvec[:, :, :], ACT.Silu).then_inc(cond_ready, 1)
            b = product()
            read(relv, b[0:8, :])
            act.wait_ge(product_free, 1)
            act.dma_start(rel_scratch, relv).then_inc(rel_stored, 16)
            root(2)
            modulation()
            for i in range(4):
                read(BIAS[:, 2 * i:2 * i + 2, :], two(product()))
            read(BIASC[:, :, :, :].rearrange("p t h n -> p (t h n)"), product()[:, 0:NT * 4 * NCMP])
            turned()
            for i in range(2):
                b = product()
                read(Q1[:, 2 * i:2 * i + 2, :], two(b))
            diagonal(product(), 0, 2)
            read(AV[:, :, :], two(product(), P))
            read(GQ[:, :, :], two(product()), scale=0.125)
            read(GK[:, :, :], two(product()))
            for i in range(2):
                read(GVV[:, :, S * i:S * (i + 1)], two(product()))
            for i in range(2):
                read(GG[:, :, S * i:S * (i + 1)], two(product()), ACT.Silu)
            read(GA[0:16, :], product()[0:16, 0:S])
            b = product()
            act.activation(GZ[:, 0, :], b[:, 0:S], ACT.Identity, bias=b_gate[:, 0:1])
            read(GZ[:, 1, :], b[:, S:2 * S], ACT.Identity, bias=b_gate[:, 1:2])
            act.wait_ge(product_free, end["gate1"])
            log_sigmoid_part(GL[:, :, :], GZ[:, :, :])
            attention(0, n_window)
            linear_attention(0, CUM, LQ[:, :, :, :], GLA_KD, GLA_LD[:, :, :], Y[:, :, BANK:], P)
            root(8)
            turned()
            wide(H)
            root(2)
            root(2)
            turned()
            read(LG[:, :, :], two(product(), E1))
            act.wait_ge(route_shift, 1)
            act.activation(LX[:, :, :], LX[:, :, :], ACT.Exp).then_inc(route_exp, 1)
            read(gatesT, product()[0:E1, 0:S])
            read(b1T[:, :, :], product().rearrange("p (c e) -> p c e", e=E1))
            read(MASKED[:, :], product()[:, 0:3 * E1])
            act.wait_ge(m1["rounds"], 1)
            n_rounds = act.value_load(rounds[0:1, 0:1], min_val=1, max_val=ROUNDS)

            def gathered(n, x):
                for half in range(2):
                    act.wait_ge(m1["gather"], 3 * n + half + 1)
                    act.activation(XG[:, 4 * half:4 * half + 4, :], ps[:, 2 + half, 0:4 * C].rearrange("p (k c) -> p k c", k=4),
                                   ACT.Copy).then_inc(m1["gather_read"], 1)
                act.wait_ge(m1["gather"], 3 * n + 3)
                act.activation(GPT[:, x, :], ps[0:C, 0, 0:S], ACT.Copy).then_inc(m1["gather_read"], 1)

            gathered(0, 0)
            with act.Fori(0, n_rounds) as r:
                with act.Fori(0, E1 // 2) as h:
                    for x in range(2):
                        n = E1 * r + 2 * h + x
                        for j in range(4):
                            act.wait_ge(m1["glu"], 4 * n + j + 1)
                            act.activation(sig[:, j % 2, :, :], pre[:, j % 2, 0:4:2, :], ACT.Sigmoid, scale=1.702)\
                                .then_inc(m1["sig"], 1)
                        act.wait_ge(m1["scatter"], n + 1)
                        gathered(n + 1, 1 - x)
                        for j in range(2):
                            act.wait_ge(m1["down"], 2 * n + j + 3)
                            act.activation(YS[:, BANK * j:BANK * (j + 1)], ps[0:C, 2 + j, :], ACT.Copy)\
                                .then_inc(m1["down_read"], 1)
            act.wait_ge(m1["sum"], 1)
            for a in range(NT):
                act.activation(Y[:, a, :].rearrange("p (c n) -> p c n", c=2), ps[:, 4 + 2 * a:6 + 2 * a, :], ACT.Copy)\
                    .then_inc(m1["sum_read"], 1)
            root(2)
            turned()
            read(convw[:, :, 0:CONVW], two(product(), 32)[:, :, 0:CONVW])
            read(Q2[:, :, :], two(product()))
            read(KCT[:, :, :], two(product()))
            diagonal(product(), 0, 1)
            read(VS[:, :, :], two(product(), 64))
            diagonal(product(), 1, 1)
            b = two(product(), 76)
            act.activation(GN[:, :, :], b[:, :, 64:76], ACT.Sigmoid)
            read(VW[:, :, :], b[:, :, 0:64])
            read(QM[:, :, :], two(product()))
            diagonal(product(), 2, 2)
            read(VM[:, :, :], two(product()))
            read(CA[:, :, CONVW - 1:], two(product()))
            read(CG[:, :, :], two(product()), ACT.Sigmoid)
            read(QH[:, :, :], two(product()))
            read(FH[:, :, :], two(product()))
            read(IH[:, :, :], two(product()))
            read(GH[:, :, :], two(product()), ACT.Sigmoid)
            for kv in range(2):
                b = product()
                act.activation(CHID[:, kv, 0, :], b[:, 0:NCMP], ACT.Gelu_apprx_tanh, bias=cmp_b1[:, kv, 0:1])
                read(CHID[:, kv, 1, :], b[:, NCMP:2 * NCMP], ACT.Gelu_apprx_tanh, bias=cmp_b1[:, kv, 1:2])
            b = product()
            act.activation(KC[0:64, 0, :], b[0:64, 0:NCMP], ACT.Copy)
            read(KC[64:P, 1, :], b[64:P, 0:NCMP])
            read(VC[0:NCMP, :], product()[0:NCMP, 0:64])
            attention(n_window, n_window + n_nsa)
            read(CTOK[:, :, :], two(product()))
            root(2)
            act.wait_ge(convln_ready, 1)
            act.activation(CTOK[:, :, :], CTOK[:, :, :], ACT.Silu).then_inc(convsilu_ready, 1)
            read(CSIL[:, :, :], two(product()))
            read(Y[:, :, 512:768], two(product()))
            act.wait_ge(product_free, end["pw2"])
            log_sigmoid_part(HLOG[:, :, :], FH[:, :, :])
            act.wait_ge(log_ready, 1)
            act.activation(FH[:, :, :], FH[:, :, :], ACT.Sigmoid, scale=-1.0).then_inc(keep_ready, 1)
            linear_attention(1, HCUM, LQ2[:, :, :, :], HG_KD, HG_LD[:, :, :], Y[:, :, 768:], 64)
            root(8)
            turned()
            wide(H)
            root(2)
            turned()
            for i in range(16):
                read(FFT[:, 2 * i:2 * i + 2, :], two(product()), ACT.Relu)
            for i in range(8):
                read(H[:, :, P * i:P * (i + 1)], two(product(), P))
            root(2)
            root(2)
            modulation()
            turned()
            for i in range(4):
                read(RQ[:, 2 * i:2 * i + 2, :], two(product()))
            for i in range(4):
                read(RK[:, 2 * i:2 * i + 2, :], two(product()))
            wide(RV)
            wide(RG, ACT.Silu)
            for a in range(NT):
                read(CQ[:, a, :], product()[:, 0:384])
            read(CKV[:, :, :], two(product()))
            read(KPE[:, :, :], two(product()))
            root(4)
            for h in range(4):
                act.wait_ge(ret_out, h + 1)
                act.activation(Y[:, :, S * h:S * (h + 1)], two(ps[:, 6 + h % 2, :]), ACT.Copy).then_inc(ret_copied, 1)
            root(8)
            wide(MG1, ACT.Sigmoid)
            wide(MG2, ACT.Sigmoid)
            turned()
            wide(H)
            for a in range(NT):
                read(CQT[:, :, P * a:P * (a + 1)], product()[:, 0:384].rearrange("p (c n) -> p c n", c=3))
            read(CKVT[:, :, :], two(product()))
            act.wait_ge(ret_gated, 1)
            for grp in range(2):
                for j in range(2):
                    read(QNT[:, 4 * grp + 2 * j:4 * grp + 2 * j + 2, :], two(product()))
                for j in range(2):
                    read(QPE[:, j, 2 * grp:2 * grp + 2, :], two(product()))
            for j in range(4):
                read(KNT[:, 2 * j:2 * j + 2, :], two(product()))
            wide(VV)
            attention(n_window + n_nsa, len(units))
            turned()
            wide(YM)
            turned()
            wide(H)
            root(2)
            turned()
            read(LR[:, :, :], two(product(), G3 + E3))
            act.wait_ge(route_shift, 2)
            act.activation(LE[:, :, :], LE[:, :, :], ACT.Exp).then_inc(route_exp, 1)
            read(MASKED3[:, :], product()[:, 0:3 * G3])
            act.wait_ge(m3["rounds"], 1)
            n_rounds = act.value_load(rounds[0:1, 1:2], min_val=1, max_val=ROUNDS)
            with act.Fori(0, n_rounds) as r:
                with act.Fori(0, G3) as g:
                    n = G3 * r + g
                    for half in range(2):
                        act.wait_ge(m3["gather"], 3 * n + half + 1)
                        act.activation(XG3[:, 4 * half:4 * half + 4, :],
                                       ps[:, 2 + half, 0:4 * C].rearrange("p (k c) -> p k c", k=4), ACT.Copy)\
                            .then_inc(m3["gather_read"], 1)
                    act.wait_ge(m3["gather"], 3 * n + 3)
                    act.activation(PT3, ps[0:C, 0, 0:S], ACT.Copy)
                    act.activation(GS, ps[0:C, 0, S:S + E3], ACT.Copy).then_inc(m3["gather_read"], 1)
                    with act.Fori(0, PG3 // 2) as h:
                        m = PG3 // 2 * n + h
                        for j in range(2):
                            act.wait_ge(m3["up"], 2 * m + j + 3)
                            act.wait_ge(m3["up_read"], 2 * m + j + 1)
                            act.activation(sil3[:, j, :, :], ps[:, j, 0:2 * C].rearrange("p (c s) -> p c s", c=2), ACT.Silu)\
                                .then_inc(m3["sil"], 1)
            act.wait_ge(m3["sum"], 1)
            for a in range(NT):
                act.activation(Y[:, a, :].rearrange("p (c n) -> p c n", c=2), ps[:, 4 + 2 * a:6 + 2 * a, :], ACT.Copy)\
                    .then_inc(m3["sum_read"], 1)
            root(2)

        @block.vector
        def _(dve):
            steps = [0]
            roots = [0]
            vectors = [0]

            def step(ins):
                ins.then_inc(dve_step, 1)
                steps[0] += 1
                dve.wait_ge(dve_step, steps[0])

            def tell(ins, signal, value):
                ins.then_inc(signal, 1)
                dve.wait_ge(signal, value)

            def vector():
                v = vectors[0]
                dve.wait_ge(vec_landed[v % GVSLOTS], 16 * (v // GVSLOTS + 1))
                return GV[:, v % GVSLOTS, :]

            def vector_done(ins):
                vectors[0] += 1
                tell(ins, vec_used, vectors[0])

            def moments(src, i):
                n = src.shape[-1]
                parts = -(-n // BANK)
                for c in range(parts):
                    step(dve.bn_stats(bnst[:, 6 * c:6 * c + 6], src[:, BANK * c:min(n, BANK * (c + 1))]))
                step(dve.bn_aggr(moment[:, 2 * i:2 * i + 2], bnst[:, 0:6 * parts]))

            def inverse_roots(n, eps, square=False):
                mean, variance = moment[:, 0:2 * n:2], moment[:, 1:2 * n:2]
                if square:
                    step(dve.tensor_tensor(var[:, 0:n], mean, mean, ALU.mult))
                    step(dve.tensor_tensor(var[:, 0:n], var[:, 0:n], variance, ALU.add))
                    variance = var[:, 0:n]
                roots[0] += 1
                tell(dve.tensor_scalar(var[:, 0:n], variance, eps, None, ALU.add), var_ready, roots[0])
                dve.wait_ge(std_ready, roots[0])
                step(dve.reciprocal(rstd[:, 0:n], std[:, 0:n]))

            def both(v):
                return v.unsqueeze(1).to_broadcast([P, NT, v.shape[-1]])

            def rms_modulate(src, shift, scale, stage, ready, value, mod_stage=None):
                for a in range(NT):
                    moments(src[:, a, :], a)
                inverse_roots(NT, 1e-6, square=True)
                g = vector()
                for a in range(NT):
                    ins = dve.scalar_tensor_tensor(H[:, a, :], src[:, a, :], rstd[:, a:a + 1], g, ALU.mult, ALU.mult)
                    if a == 0:
                        step(ins)
                vector_done(ins)
                if mod_stage:
                    dve.wait_ge(product_free, end[mod_stage])
                step(dve.tensor_scalar(MOD[:, scale, :], MOD[:, scale, :], 1.0, None, ALU.add))
                step(dve.tensor_tensor(H[:, :, :], H[:, :, :], both(MOD[:, scale, :]), ALU.mult))
                tell(dve.tensor_tensor(H[:, :, :], H[:, :, :], both(MOD[:, shift, :]), ALU.add), ready, value)

            def add_gated_norm(src, gate):
                for a in range(NT):
                    moments(src[:, a, :], a)
                inverse_roots(NT, 1e-6, square=True)
                g = vector()
                for a in range(NT):
                    ins = dve.scalar_tensor_tensor(src[:, a, :], src[:, a, :], rstd[:, a:a + 1], g, ALU.mult, ALU.mult)
                    if a == 0:
                        step(ins)
                vector_done(ins)
                add_gated(src, gate)

            def add_gated(src, gate):
                step(dve.tensor_tensor(src[:, :, :], src[:, :, :], both(MOD[:, gate, :]), ALU.mult))
                step(dve.tensor_tensor(X[:, :, :], X[:, :, :], src[:, :, :], ALU.add))

            def center_scale(dst, src, i):
                step(dve.tensor_scalar(dst, src, moment[:, 2 * i:2 * i + 1], rstd[:, i:i + 1], ALU.subtract, ALU.mult))

            def add_layer_norm(src, last=None, value=None):
                for a in range(NT):
                    step(dve.scalar_tensor_tensor(X[:, a, :], X[:, a, :], 2.0 ** 0.25, src[:, a, :], ALU.mult, ALU.add))
                    moments(X[:, a, :], a)
                inverse_roots(NT, 1e-5)
                for a in range(NT):
                    center_scale(X[:, a, :], X[:, a, :], a)
                g = vector()
                vector_done(dve.tensor_tensor(X[:, :, :], X[:, :, :], both(g), ALU.mult))
                g = vector()
                vector_done(dve.tensor_tensor(X[:, :, :], X[:, :, :], both(g), ALU.add))

            scale_of = {"window": 0.125, "cmp": 0.125, "sel": 0.125, "win": 0.125, "moba": 0.125, "mla": 192.0 ** -0.5}

            def shift(u):
                kind, t, grp, nk, _ = units[u]
                st = att_stat[u % 2]
                dve.wait_ge(att["scores"], u + 1)
                if u >= 1:
                    dve.wait_ge(att["probs"], u)
                for pair in range(2):
                    ins = dve.scalar_tensor_tensor(
                        sS[:, 2 * pair:2 * pair + 2, 0:nk], ps[:, 4 + pair, 0:2 * nk].rearrange("p (h n) -> p h n", h=2),
                        scale_of[kind], bias_of(u, pair), ALU.mult, ALU.add)
                    if pair == 0:
                        step(ins)
                tell(ins, att["scores_read"], u + 1)
                step(dve.tensor_reduce(st["max"], sS[:, :, 0:nk], AX.X, ALU.max))
                if kind == "window":
                    sink = sinks[:, 4 * grp:4 * grp + 4]
                    step(dve.tensor_tensor(st["max"], st["max"], sink, ALU.max))
                    step(dve.tensor_tensor(st["sink"], sink, st["max"], ALU.subtract))
                tell(dve.tensor_scalar(st["shift"], st["max"], FLOOR, -1.0, ALU.max, ALU.mult), att["shift"], u + 1)

            def finish(u):
                kind, t, grp, nk, width = units[u]
                st = att_stat[u % 2]
                dve.wait_ge(att["probs"], u + 1)
                if kind == "window":
                    step(dve.tensor_tensor(st["sum"], st["sum"], st["sink"], ALU.add))
                else:
                    step(dve.tensor_scalar(st["sum"], st["sum"], 1e-30, None, ALU.max))
                step(dve.reciprocal(st["inv"], st["sum"]))
                if kind in ("cmp", "sel", "win"):
                    branch = ("cmp", "sel", "win").index(kind)
                    step(dve.tensor_tensor(st["inv"], st["inv"], GN[:, t, branch:12:3], ALU.mult))
                dve.wait_ge(att["out"], u + 1)
                o = ps[:, 3, 0:4 * width].rearrange("p (h d) -> p h d", h=4)
                at = {"window": 256 * grp, "moba": 256, "mla": 512 * grp}.get(kind, 0)
                dst = Y[:, t, at:at + 4 * width].rearrange("p (h d) -> p h d", h=4)
                add = kind in ("sel", "win")
                tell(dve.tensor_tensor(ONSA if add else dst, o, st["inv"].unsqueeze(2).to_broadcast([P, 4, width]), ALU.mult),
                     att["out_read"], u + 1)
                if add:
                    step(dve.tensor_tensor(dst, dst, ONSA, ALU.add))

            def attention(u0, u1):
                shift(u0)
                for u in range(u0, u1):
                    if u + 1 < u1:
                        shift(u + 1)
                    finish(u)

            def linear_attention(n, q, k, cum, LQb, KDb, LDb, AT):
                c4 = cum.rearrange("p c (b i) -> p c b i", i=BLK)
                step(dve.tensor_copy(LQb[:, :, 0, :], c4[:, :, 0, :]))
                for pair in range(2):
                    ins = dve.tensor_tensor(LQb[:, pair, 1:, :], c4[:, pair, 1:, :],
                                            c4[:, pair, 0:NBLK - 1, BLK - 1:BLK].to_broadcast([P, NBLK - 1, BLK]), ALU.subtract)
                    if pair == 0:
                        step(ins)
                tell(ins, lin["qdiff"], n + 1)
                for i in range(2):
                    step(dve.memset(KDb[:, i, :, :], 0.0))
                dve.wait_ge(lin["qexp"], n + 1)
                q4 = q.rearrange("p c (b i) -> p c b i", i=BLK)
                for h in range(2):
                    for pair in range(2):
                        rows_ = slice(64 * h, 64 * h + 64)
                        ins = dve.tensor_tensor(QD[rows_, pair, :, h, :], q4[rows_, pair, :, :], LQb[rows_, pair, :, :], ALU.mult)
                        if h + pair < 2:
                            step(ins)
                tell(ins, lin["queries"], n + 1)
                dve.sem_inc(lin["keys"], 1)
                for i in range(1, NBLK):
                    dve.wait_ge(lin["kexp"], (NBLK - 1) * n + i)
                    kd = KDb[:, i % 2, :, 0:BLK * i]
                    dve.tensor_tensor(kd, kd, k[:, :, 0:BLK * i], ALU.mult).then_inc(lin["keys"], 1)
                for pair in range(2):
                    if pair + n:
                        dve.wait_ge(lin["diag_used"], 2 * n + pair)
                    ld4 = LDb.rearrange("p i (b s) -> p i b s", s=BLK)

                    def later(x):
                        return x[:, pair, :].rearrange("p (b i) -> p i b", i=BLK).unsqueeze(3).to_broadcast([P, BLK, NBLK, BLK])

                    def earlier(x):
                        return x[:, pair, :].unsqueeze(1).to_broadcast([P, BLK, S])

                    step(dve.tensor_tensor(ld4, later(cum), earlier(cum).rearrange("p i (b s) -> p i b s", s=BLK), ALU.subtract))
                    tell(dve.tensor_scalar(LDb, LDb, 0.0, None, ALU.min), lin["ddiff"], 2 * n + pair + 1)
                    dve.wait_ge(lin["dexp"], 2 * n + pair + 1)
                    step(dve.tensor_tensor(ld4, ld4, later(q), ALU.mult))
                    tell(dve.tensor_tensor(LDb, LDb, earlier(k), ALU.mult), lin["diag"], 2 * n + pair + 1)
                dve.wait_ge(lin["keys_used"], NBLK * (n + 1))
                dve.wait_ge(lin["diag_used"], 2 * n + 2)
                nb = P // BLK
                for tile in range(NT):
                    d = ps[:, 7, 64 * tile:64 * tile + 64].rearrange("p (c i h) -> p c h i", c=2, i=BLK)
                    a4 = AT[tile].rearrange("p h (b i) -> p h b i", i=BLK)[:, :, 0:nb, :]
                    for h in range(4):
                        step(dve.tensor_tensor(a4[:, h], d[:, h // 2, h % 2, :].unsqueeze(1).to_broadcast([P, nb, BLK]),
                                               diag.rearrange("p (b i) -> p b i", i=BLK), ALU.mult))
                for pair in range(2):
                    o = ps[:, 4 + pair, :].rearrange("p (h t) -> p h t", h=2)
                    a = AT[0][:, 2 * pair:2 * pair + 2, :]
                    step(dve.tensor_tensor(a[:, :, 0:P], a[:, :, 0:P], o[:, :, 0:P], ALU.add))
                    step(dve.tensor_copy(a[:, :, P:S], o[:, :, P:S]))
                tell(dve.tensor_tensor(AT[1], AT[1], ps[:, 6, :].rearrange("p (h t) -> p h t", h=4), ALU.add),
                     lin["merged"], n + 1)

            def log_sigmoid_sums(n, z, part, cum, factor):
                dve.wait_ge(loglog_ready, n)
                for c in range(2):
                    ins = dve.scalar_tensor_tensor(part[:, c, :], z[:, c, :], 0.0, part[:, c, :], ALU.min, ALU.subtract)
                    if c == 0:
                        step(ins)
                tell(ins, log_ready, 1) if n == 2 else step(ins)
                if factor != 1.0:
                    step(dve.tensor_scalar(part, part, factor, None, ALU.mult))
                for c in range(2):
                    step(dve.tensor_tensor_scan(cum[:, c, :], ones[:, :], part[:, c, :], 0.0, ALU.mult, ALU.add))

            def head_rms(o, width, n0=0):
                for a in range(NT):
                    for h in range(4):
                        moments(o[:, a, width * h:width * (h + 1)], 4 * a + h)
                inverse_roots(8, 1e-6, square=True)

            def ranks(dst, v, groups, n, c1, c2, order):
                shape = [P, groups, n, n] if groups > 1 else [P, n, n]
                ax = 2 if groups > 1 else 1
                other, own = v.unsqueeze(ax).to_broadcast(shape), v.unsqueeze(ax + 1).to_broadcast(shape)
                o = order[:, 0:n, 0:n]
                if groups > 1:
                    o = o.unsqueeze(1).to_broadcast(shape)
                step(dve.tensor_tensor(c1, other, own, ALU.is_gt))
                step(dve.tensor_tensor(c2, other, own, ALU.is_equal))
                step(dve.tensor_tensor(c2, c2, o, ALU.mult))
                step(dve.tensor_tensor(c1, c1, c2, ALU.add))
                step(dve.tensor_reduce(dst, c1, AX.X, ALU.add))

            dve.wait_ge(consts_landed, 16 * n_consts)
            dve.wait_ge(zeros_ready, 5)
            dve.wait_ge(x_landed, 16)
            rms_modulate(X, 0, 1, "h1", h1_ready, 1, "ada1")
            log_sigmoid_sums(1, GZ, GL[:, :, :], CUM, 1.0 / 16.0)
            attention(0, n_window)
            linear_attention(0, GQ[:, :, :], GK[:, :, :], CUM[:, :, :], LQ, GLA_KD, GLA_LD[:, :, :], GLA_AT)
            dve.wait_ge(lin["read"], 2)
            o = Y[:, :, BANK:]
            head_rms(o, P)
            for a in range(NT):
                for h in range(4):
                    oh = o[:, a, P * h:P * (h + 1)]
                    step(dve.scalar_tensor_tensor(oh, oh, rstd[:, 4 * a + h:4 * a + h + 1], gla_norm, ALU.mult, ALU.mult))
            tell(dve.tensor_tensor(o, o, GG[:, :, :], ALU.mult), mix_ready, 1)
            dve.wait_ge(product_free, end["out1"])
            add_gated_norm(H, 2)
            rms_modulate(X, 3, 4, "h2", h2_ready, 1)
            dve.wait_ge(moe1_params_landed, 48)
            dve.wait_ge(product_free, end["route1"])
            step(dve.tensor_tensor(LG[:, :, :], LG[:, :, :], both(b_router), ALU.add))
            for a in range(NT):
                ranks(GT[:, a, :], LG[:, a, :], 1, E1, cmp1, cmp2, before)
                step(dve.tensor_reduce(moment[:, a:a + 1], LG[:, a, :], AX.X, ALU.max))
                step(dve.tensor_scalar(LX[:, a, :], LG[:, a, :], moment[:, a:a + 1], None, ALU.subtract))
            tell(dve.tensor_scalar(MASK[:, :, :], GT[:, :, :], float(TOP1), None, ALU.is_lt), route_shift, 1)
            dve.wait_ge(route_exp, 1)
            step(dve.tensor_tensor(GT[:, :, :], MASK[:, :, :], LX[:, :, :], ALU.mult))
            step(dve.tensor_reduce(moment[:, 0:NT], GT[:, :, :], AX.X, ALU.add))
            step(dve.reciprocal(moment[:, 2:2 + NT], moment[:, 0:NT]))
            tell(dve.tensor_tensor(GT[:, :, :], GT[:, :, :], moment[:, 2:2 + NT].unsqueeze(2).to_broadcast([P, NT, E1]),
                                   ALU.mult), gates_ready, 1)

            def passes(rank, mask, counted, groups, column, ready):
                step(dve.memset(rank, -1.0))
                r0 = counted[:, 0:NT * groups].rearrange("p (a e) -> p a e", a=NT)
                step(dve.scalar_tensor_tensor(r0, r0, 1.0, mask, ALU.add, ALU.mult))
                for r in range(ROUNDS):
                    step(dve.tensor_scalar(rank[:, :, groups * r:groups * (r + 1)], r0, -1.0 - C * r, None, ALU.add))
                step(dve.tensor_reduce(moment[:, 0:1], counted[:, NT * groups:(NT + 1) * groups], AX.X, ALU.max))
                step(dve.tensor_scalar(moment[:, 1:2], moment[:, 0:1], float(C), 1.0, ALU.is_gt, ALU.add))
                for r in range(2, ROUNDS):
                    step(dve.tensor_scalar(moment[:, 2:3], moment[:, 0:1], float(C * r), None, ALU.is_gt))
                    step(dve.tensor_tensor(moment[:, 1:2], moment[:, 1:2], moment[:, 2:3], ALU.add))
                step(dve.tensor_copy(rounds[:, column:column + 1], moment[:, 1:2]))
                dve.sem_inc(ready, 1)
                return dve.value_load(rounds[0:1, column:column + 1], min_val=1, max_val=ROUNDS)

            step(dve.memset(GATE[:, :, :], 0.0))
            for r in range(ROUNDS):
                step(dve.tensor_copy(GATE[:, :, E1 * r:E1 * (r + 1)], GT[:, :, :]))
            step(dve.memset(YS, 0.0))
            step(dve.memset(GPT[:, :, :], 0.0))
            dve.wait_ge(product_free, end["rank1"])
            n_rounds = passes(RANK[:, :, :], MASK[:, :, :], MASKED, E1, 0, m1["rounds"])
            dve.sem_inc(m1["up_read"], 1)
            dve.sem_inc(m1["down_read"], 2)

            def pick(n, astep):
                astep(dve.tensor_copy(rcur, RANK[:, :, n]))
                astep(dve.tensor_copy(gcur, GATE[:, :, n]))
                for a in range(NT):
                    astep(dve.tensor_scalar(PICK[:, a, :], iota, rcur[:, a:a + 1], None, ALU.is_equal))
                    ins = dve.tensor_scalar(PICKG[:, a, :], iota, rcur[:, a:a + 1], gcur[:, a:a + 1], ALU.is_equal, ALU.mult)
                    if a == 0:
                        astep(ins)
                tell(ins, m1["pick"], n + 1)

            pick(0, step)
            with dve.Fori(0, n_rounds) as r:
                with dve.Fori(0, E1 // 2) as h:
                    own = [0]
                    for x in range(2):
                        n = E1 * r + 2 * h + x

                        def astep(ins):
                            own[0] += 1
                            ins.then_inc(m1["step"], 1)
                            dve.wait_ge(m1["step"], 2 * EXPERT_STEPS * (E1 // 2 * r + h) + own[0])

                        astep(dve.tensor_copy(b1cur, b1T[:, :, 2 * h + x]))
                        dve.wait_ge(m1["gather"], 3 * n + 3)
                        pick(n + 1, astep)

                        def limit(j):
                            dve.wait_ge(m1["up"], 4 * n + j + 2)
                            p = pre[:, j % 2, :, :]
                            tell(dve.tensor_tensor(p, ps[:, j % 2, 0:4 * C].rearrange("p (c s) -> p c s", c=4),
                                                   b1cur[:, 4 * j:4 * j + 4].unsqueeze(2).to_broadcast([P, 4, C]), ALU.add),
                                 m1["up_read"], 4 * n + j + 2)
                            tell(dve.tensor_scalar(p[:, 0:4:2, :], p[:, 0:4:2, :], 7.0, None, ALU.min), m1["glu"], 4 * n + j + 1)
                            astep(dve.tensor_scalar(p[:, 1:4:2, :], p[:, 1:4:2, :], 7.0, -7.0, ALU.min, ALU.max))

                        def combine(j):
                            p, q = pre[:, j % 2, :, :], sig[:, j % 2, :, :]
                            dve.wait_ge(m1["sig"], 4 * n + j + 1)
                            astep(dve.tensor_tensor(q, q, p[:, 0:4:2, :], ALU.mult))
                            tell(dve.scalar_tensor_tensor(aT[:, 2 * j:2 * j + 2, :], p[:, 1:4:2, :], 1.0, q, ALU.add, ALU.mult),
                                 m1["hidden"], 4 * n + j + 1)

                        limit(0)
                        for j in range(1, 4):
                            limit(j)
                            combine(j - 1)
                        combine(3)
                    assert own[0] == 2 * EXPERT_STEPS, own[0]
            dve.wait_ge(m1["sum_read"], NT)
            add_gated_norm(Y, 5)
            dve.sem_inc(x1_ready, 1)
            dve.wait_ge(product_free, end["in2"])
            kct = KCT.rearrange("p a (m q r) -> p a q m r", q=8, r=2)
            for kv in range(2):
                for r in range(2):
                    for jh in range(2):
                        hs = slice(64 * r, 64 * r + 64)
                        ins = dve.tensor_tensor(
                            BLOCKS[hs, kv, 8 * jh:8 * jh + 8, :], kct[hs, kv, :, jh:jh + NCMP, r],
                            cmp_pe[hs, kv, 8 * jh:8 * jh + 8].unsqueeze(2).to_broadcast([64, 8, NCMP]), ALU.add)
                        if kv + r + jh < 3:
                            step(ins)
            tell(ins, blocks_ready, 1)
            attention(n_window, n_window + n_nsa)
            step(dve.memset(CA[:, :, 0:CONVW - 1], 0.0))
            step(dve.tensor_tensor(CA[:, :, CONVW - 1:], CA[:, :, CONVW - 1:], CG[:, :, :], ALU.mult))
            for c in range(2):
                step(dve.tensor_scalar(CACC[:, c, :], CA[:, c, 0:S], convw[:, c, 0:1], conv_bias[:, c:c + 1], ALU.mult, ALU.add))
            for i in range(1, CONVW):
                for c in range(2):
                    ins = dve.scalar_tensor_tensor(CACC[:, c, :], CA[:, c, i:i + S], convw[:, c, i:i + 1], CACC[:, c, :],
                                                   ALU.mult, ALU.add)
                    if i + c < CONVW:
                        step(ins)
            tell(ins, conv_ready, 1)
            dve.wait_ge(product_free, end["convT"])
            for a in range(NT):
                moments(CTOK[:, a, :], a)
            inverse_roots(NT, 1e-5)
            for a in range(NT):
                center_scale(CTOK[:, a, :], CTOK[:, a, :], a)
            step(dve.tensor_tensor(CTOK[:, :, :], CTOK[:, :, :], both(conv_g), ALU.mult))
            tell(dve.tensor_tensor(CTOK[:, :, :], CTOK[:, :, :], both(conv_b), ALU.add), convln_ready, 1)
            log_sigmoid_sums(2, FH, HLOG[:, :, :], HCUM, 1.0)
            dve.wait_ge(keep_ready, 1)
            dve.wait_ge(product_free, end["pw2"])
            linear_attention(1, QH[:, :, :], FH[:, :, :], HCUM[:, :, :], LQ2, HG_KD, HG_LD[:, :, :], HG_AT)
            dve.wait_ge(lin["read"], 4)
            o = Y[:, :, 768:]
            head_rms(o, 64)
            for a in range(NT):
                oa = o[:, a, :].rearrange("p (h d) -> p h d", h=4)
                step(dve.tensor_tensor(oa, oa, rstd[:, 4 * a:4 * a + 4].unsqueeze(2).to_broadcast([P, 4, 64]), ALU.mult))
            step(dve.tensor_tensor(o, o, both(hgrn_g), ALU.mult))
            tell(dve.tensor_tensor(o, o, GH[:, :, :], ALU.mult), mix_ready, 2)
            dve.wait_ge(product_free, end["out2"])
            add_layer_norm(H)
            dve.sem_inc(y2_ready, 1)
            for i in range(16):
                dve.wait_ge(product_free, end["y2T"] + i + 1)
                f = FFT[:, 2 * i:2 * i + 2, :]
                dve.tensor_tensor(f, f, f, ALU.mult).then_inc(relu_ready, 1)
            dve.wait_ge(product_free, end["ff2"])
            add_layer_norm(H)
            rms_modulate(X, 0, 1, "u1", u1_ready, 1, "ada3")
            dve.wait_ge(tables_landed, 32)
            dve.wait_ge(product_free, end["in3"])
            for r in (RQ, RK):
                x1, x2 = r[:, 0:8:2, :], r[:, 1:8:2, :]
                cos, sin = (ropes[:, i, :].unsqueeze(1).to_broadcast([P, 4, S]) for i in range(2))
                step(dve.tensor_tensor(RTMP[:, 0], x1, sin, ALU.mult))
                step(dve.tensor_tensor(RTMP[:, 1], x2, sin, ALU.mult))
                step(dve.tensor_tensor(x1, x1, cos, ALU.mult))
                step(dve.tensor_tensor(x2, x2, cos, ALU.mult))
                step(dve.tensor_tensor(x1, x1, RTMP[:, 1], ALU.subtract))
                ins = dve.tensor_tensor(x2, x2, RTMP[:, 0], ALU.add)
                step(ins) if r is RQ else tell(ins, rope_ready, 1)
            step(dve.tensor_tensor(KPE[:, 0, :], KPE[:, 0, :], ropes[:, 2, :], ALU.mult))
            step(dve.tensor_tensor(KPE[:, 1, :], KPE[:, 1, :], ropes[:, 3, :], ALU.mult))
            for h in range(2):
                hs = slice(64 * h, 64 * h + 64)
                step(dve.tensor_tensor(BD[hs, 0, h, :], KPE[hs, 0, :], KPE[hs, 1, :], ALU.add))
            for a in range(NT):
                moments(CQ[:, a, :], 2 * a)
                moments(CKV[:, a, :], 2 * a + 1)
            inverse_roots(4, 1e-6, square=True)
            for a in range(NT):
                step(dve.scalar_tensor_tensor(CQ[:, a, :], CQ[:, a, :], rstd[:, 2 * a:2 * a + 1], qn_row, ALU.mult, ALU.mult))
                ins = dve.scalar_tensor_tensor(CKV[:, a, :], CKV[:, a, :], rstd[:, 2 * a + 1:2 * a + 2], kvn_row, ALU.mult, ALU.mult)
                if a == 0:
                    step(ins)
            tell(ins, cq_ready, 1)
            for h in range(4):
                dve.wait_ge(ret_scores, h + 1)
                b = ps[:, 4 + h % 2, :]
                step(dve.tensor_tensor(RT[:, h, 0, :], b[:, 0:S], decay[:, h, :], ALU.mult))
                tell(dve.tensor_tensor(RT[:, h, 1, P:S], b[:, S:S + P], decay[:, h, 0:P], ALU.mult), ret_decayed, h + 1)
            dve.wait_ge(ret_copied, 4)
            for a in range(NT):
                for h in range(4):
                    moments(Y[:, a, S * h:S * (h + 1)], 4 * a + h)
            inverse_roots(8, 1e-6)
            for a in range(NT):
                for h in range(4):
                    yh = Y[:, a, S * h:S * (h + 1)]
                    center_scale(yh, yh, 4 * a + h)
            tell(dve.tensor_tensor(Y[:, :, :], Y[:, :, :], RG[:, :, :], ALU.mult), ret_ready, 1)
            dve.wait_ge(product_free, end["reto"])
            tell(dve.tensor_tensor(H[:, :, :], H[:, :, :], MG1[:, :, :], ALU.mult), ret_gated, 1)
            dve.wait_ge(product_free, end["uq"])
            for j in range(2):
                step(dve.tensor_tensor(QPE[:, j, :, :], QPE[:, j, :, :],
                                       ropes[:, 2 + j, :].unsqueeze(1).to_broadcast([P, 4, S]), ALU.mult))
            tell(dve.tensor_tensor(QPE[:, 0, :, :], QPE[:, 0, :, :], QPE[:, 1, :, :], ALU.add), mlarope_ready, 1)
            attention(n_window + n_nsa, len(units))
            dve.sem_inc(mla_ready, 1)
            dve.wait_ge(product_free, end["mlao"])
            step(dve.tensor_tensor(YM[:, :, :], YM[:, :, :], MG2[:, :, :], ALU.mult))
            tell(dve.tensor_tensor(H[:, :, :], H[:, :, :], YM[:, :, :], ALU.add), merge_ready, 1)
            dve.wait_ge(product_free, end["out3"])
            add_gated(H, 2)
            rms_modulate(X, 3, 4, "u2", u2_ready, 1)
            dve.wait_ge(before_landed, 16)
            dve.wait_ge(product_free, end["route3"])
            step(dve.tensor_tensor(LR[:, :, :], LR[:, :, :], both(b_route3), ALU.add))
            GSEL, ESEL, GMAX = moment[:, 0:8], GE, moment[:, 8:24]
            for a in range(NT):
                grp, exp = LR[:, a, 0:G3], LR[:, a, G3:].rearrange("p (g e) -> p g e", g=G3)
                ranks(GSEL[:, G3 * a:G3 * (a + 1)], grp, 1, G3, cmp3[:, 0, 0:G3, 0:G3], cmp4[:, 0, 0:G3, 0:G3], before3)
                ranks(GE[:, a, :].rearrange("p (g e) -> p g e", g=G3), exp, G3, PG3, cmp3, cmp4, before3)
                step(dve.tensor_reduce(GMAX[:, 8 * a:8 * a + 1], grp, AX.X, ALU.max))
                step(dve.tensor_reduce(GMAX[:, 8 * a + 4:8 * a + 8], exp, AX.X, ALU.max))
                step(dve.tensor_scalar(LE[:, a, 0:G3], grp, GMAX[:, 8 * a:8 * a + 1], None, ALU.subtract))
                step(dve.tensor_tensor(LE[:, a, G3:].rearrange("p (g e) -> p g e", g=G3), exp,
                                       GMAX[:, 8 * a + 4:8 * a + 8].unsqueeze(2).to_broadcast([P, G3, PG3]), ALU.subtract))
            step(dve.tensor_scalar(GSEL, GSEL, 1.0, None, ALU.is_lt))
            tell(dve.tensor_scalar(GE[:, :, :], GE[:, :, :], float(TOP3), None, ALU.is_lt), route_shift, 2)
            dve.wait_ge(route_exp, 2)
            for a in range(NT):
                e8 = GE[:, a, :].rearrange("p (g e) -> p g e", g=G3)
                step(dve.tensor_reduce(GMAX[:, 0:1], LE[:, a, 0:G3], AX.X, ALU.add))
                step(dve.reciprocal(GMAX[:, 1:2], GMAX[:, 0:1]))
                step(dve.scalar_tensor_tensor(GMAX[:, 4:8], LE[:, a, 0:G3], GMAX[:, 1:2], GSEL[:, G3 * a:G3 * (a + 1)],
                                              ALU.mult, ALU.mult))
                step(dve.tensor_tensor(GE[:, a, :], GE[:, a, :], LE[:, a, G3:], ALU.mult))
                step(dve.tensor_reduce(GMAX[:, 8:12], e8, AX.X, ALU.add))
                step(dve.reciprocal(GMAX[:, 12:16], GMAX[:, 8:12]))
                step(dve.tensor_tensor(GMAX[:, 4:8], GMAX[:, 4:8], GMAX[:, 12:16], ALU.mult))
                step(dve.tensor_tensor(e8, e8, GMAX[:, 4:8].unsqueeze(2).to_broadcast([P, G3, PG3]), ALU.mult))
            step(dve.memset(zero_row, 0.0))
            tell(dve.tensor_copy(MASK3[:, :, :], GSEL.rearrange("p (a g) -> p a g", a=NT)), m3["zero"], 1)
            dve.wait_ge(product_free, end["rank3"])
            n_rounds = passes(RANK3[:, :, :], MASK3[:, :, :], MASKED3, G3, 1, m3["rounds"])
            dve.sem_inc(m3["up_read"], 2)
            dve.sem_inc(m3["down_read"], 2)
            with dve.Fori(0, n_rounds) as r:
                with dve.Fori(0, G3) as g:
                    n = G3 * r + g
                    dve.tensor_copy(rcur3, RANK3[:, :, n]).then_inc(m3["step"], 1)
                    dve.wait_ge(m3["step"], 3 * n + 1)
                    dve.tensor_scalar(PICK3[:, 0, :], iota, rcur3[:, 0:1], None, ALU.is_equal).then_inc(m3["step"], 1)
                    dve.wait_ge(m3["step"], 3 * n + 2)
                    tell(dve.tensor_scalar(PICK3[:, 1, :], iota, rcur3[:, 1:2], None, ALU.is_equal), m3["pick"], n + 1)
                    dve.wait_ge(m3["scatter"], n + 1)
                    dve.memset(YA, 0.0).then_inc(m3["step"], 1)
                    with dve.Fori(0, PG3 // 2) as h:
                        m = PG3 // 2 * n + h
                        dve.wait_ge(m3["gather_read"], 3 * n + 3)
                        dve.wait_ge(m3["step"], 3 * n + 3)
                        dve.tensor_copy(gcur3, GS[:, bass.ds(PG3 * g + 2 * h, 2)]).then_inc(m3["pair_step"], 1)
                        dve.wait_ge(m3["pair_step"], m + 1)
                        for j in range(2):
                            dve.wait_ge(m3["sil"], 2 * m + j + 1)
                            tell(dve.tensor_tensor(aT3[:, j, :, :], sil3[:, j, :, :],
                                                   ps[:, j, 2 * C:4 * C].rearrange("p (c s) -> p c s", c=2), ALU.mult),
                                 m3["hidden"], 2 * m + j + 1)
                            dve.sem_inc(m3["up_read"], 1)
                        for j in range(2):
                            for half in range(2):
                                i = 4 * m + 2 * j + half
                                y = YA[:, BANK * half:BANK * (half + 1)]
                                dve.wait_ge(m3["down"], i + 2)
                                tell(dve.scalar_tensor_tensor(y, ps[0:C, 2 + half, :], gcur3[:, j:j + 1], y, ALU.mult, ALU.add),
                                     m3["down_read"], i + 3)
            dve.wait_ge(m3["sum_read"], NT)
            add_gated(Y, 5)
            for a in range(NT):
                moments(X[:, a, :], a)
            inverse_roots(NT, 1e-6, square=True)
            g = vector()
            for a in range(NT):
                ins = dve.scalar_tensor_tensor(H[:, a, :], X[:, a, :], rstd[:, a:a + 1], g, ALU.mult, ALU.mult)
                if a == 0:
                    step(ins)
            vector_done(ins)
            dve.sem_inc(final_ready, 1)


OUT_SHAPE = (1, S, D)


def kernel(**inputs):
    import concourse.bacc as _bacc
    from concourse.bass_utils import run_bass_kernel_spmd as _run

    nc = _bacc.Bacc("TRN2", target_bir_lowering=False, num_devices=1)
    arrays, args = {}, {}
    for name, a in {**inputs, **constants()}.items():
        a = np.ascontiguousarray(a)
        arrays[f"in_{name}"] = a
        args[name] = nc.dram_tensor(f"in_{name}", a.shape, F32, kind="ExternalInput").ap()
    out = nc.dram_tensor("out_0", OUT_SHAPE, F32, kind="ExternalOutput").ap()
    rel_scratch = nc.dram_tensor("rel_scratch", (8, BANK), F32, kind="Internal").ap()
    build(nc, args, out, rel_scratch)
    r = _run(nc, [arrays], core_ids=[0])
    return r.results[0]["out_0"]
```

```python
from contextlib import ExitStack

import numpy as np

import concourse.bass as bass
from concourse import mybir

F32 = mybir.dt.float32
ALU = mybir.AluOpType
ACT = mybir.ActivationFunctionType
AX = mybir.AxisListType

P = 128
S = 256
NT = S // P
D = 1024
KT = D // P
E1, F1 = 32, 1024
TOP1 = 4
E3, F3, G3, PG3 = 32, 256, 4, 8
TOP3 = 2
NCMP = 15
CONVW = 31
FF2 = 4096
SLOTS = 3
SLAB = 4096
BANK = 512
PBANKS = 3
NEG = -1.0e30
FLOOR = -1.0e20
C1 = 64
PASSES = E1 + TOP1 * S // C1
C = 96
ROUNDS = -(-S // C)
SUBS = C // 32
JOBS = 4
TURNS = PG3 * SUBS // JOBS
GROUP_STEPS = 4
EXPERT_STEPS = 7
THROUGH, OF_PASS = 1, 1 + E1
ROUNDS3 = OF_PASS + PASSES
FOUR_OF = ROUNDS3 + 1
BLK, PART = 16, 4
NBLK, NPART = S // BLK, BLK // PART

STAGES = [
    ("ada1a", [2] * 4, 0), ("rel", [], 1), ("h1T", [], 4), ("in1", [2, 3, 2, 2, 2], 0), ("gate1", [], 1), ("flip", [], 5),
    ("ada1b", [2] * 8, 0), ("mix1T", [], 4), ("out1", [2, 2], 0), ("h2T", [], 4), ("route1", [], 1), ("gates1T", [], 1), ("rank1", [], 1),
    ("x1T", [], 4), ("convw", [], 1), ("in2", [4, 3, 2, 2, 2, 2], 0), ("cmp2", [1, 1], 3), ("ada3", [2] * 12, 0), ("convT", [], 1),
    ("convback", [], 1), ("pw2", [], 1), ("mix2T", [], 4), ("out2", [2, 2], 0), ("y2T", [], 4), ("ff1", [2] * 8, 0),
    ("ff2", [1] * 8, 0),
    ("u1T", [], 4), ("in3", [2] * 10, 0), ("gates3", [2] * 4, 0),
    ("retT", [], 4), ("reto", [2, 2], 0), ("cqT", [], 3), ("uq", [4, 4], 0), ("ukv", [8], 0),
    ("mlaT", [], 4), ("mlao", [2, 2], 0), ("mergeT", [], 4), ("out3", [2, 2], 0),
    ("u2T", [], 4), ("route3", [], 1), ("rank3", [], 1),
]


def product_plan():
    first, end, first_slab, release, product, slab = {}, {}, {}, [], 0, 0
    for name, per_slab, extra in STAGES:
        first[name], first_slab[name] = product, slab
        for n in per_slab:
            product += n
            release.append(product)
            slab += 1
        product += extra
        end[name] = product
    return first, end, first_slab, release


def constants():
    p, j = np.arange(P)[:, None], np.arange(2 * P)[None, :]
    rel = p + P - j
    window = np.where((rel >= 0) & (rel < P), 0.0, NEG)
    causal = np.where(rel >= 0, 0.0, NEG)
    dist = 255 - np.arange(BANK)
    nf = np.maximum(dist, 1).astype(np.float32)
    large = 16 + (np.log(nf / np.float32(16)) / np.float32(np.log(8.0)) * 16).astype(np.int32)
    n = np.maximum(dist, 0)
    bucket = np.where(n < 16, n, np.minimum(large, 31))
    onehot = np.zeros((33, BANK))
    onehot[bucket, np.arange(BANK)] = (dist >= 0)
    onehot[32] = np.where(dist >= 0, 0.0, NEG)
    s = np.arange(P)[:, None, None]
    b = np.arange(P // PART)[None, :, None]
    i = np.arange(PART)[None, None, :]
    diag = ((s // PART == b) & (i >= s % PART)).reshape(P, P)
    same = np.arange(P)[:, None] // BLK == np.arange(P // BLK)[None, :]
    heads2 = np.stack([np.arange(P) < 64, np.arange(P) >= 64], 1)
    e = np.arange(32)
    before = np.broadcast_to((e[None, :] < e[:, None]).reshape(1, -1), (P, 1024))
    log_gamma = np.log1p(-np.exp2(-5.0 - np.arange(4)))
    relT = np.arange(2 * P)[None, :] - np.arange(P)[:, None]
    decay = np.where(relT[:, None, :] >= 0, np.exp(log_gamma[None, :, None] * np.maximum(relT, 0)[:, None, :]), 0.0) / 16.0

    def rope(dim):
        inv = np.float32(10000.0) ** (-np.arange(0, dim, 2, dtype=np.float32) / np.float32(dim))
        ang = inv[:, None].astype(np.float32) * np.arange(S, dtype=np.float32)[None, :]
        return np.cos(ang), np.sin(ang)

    cr, sr = rope(256)
    cm, sm = rope(64)
    ropes = np.stack([cr, sr, np.concatenate([cm, cm, cm, cm]), np.concatenate([-sm, sm, -sm, sm])], 1)
    c = {
        "c_ident": np.eye(P), "c_flip": np.eye(P)[::-1], "c_window": window, "c_causal": causal, "c_onehot": onehot, "c_diag": diag, "c_same": same,
        "c_heads2": heads2, "c_before": before, "c_tri": np.arange(P)[:, None] < np.arange(P)[None, :],
        "c_iota": np.broadcast_to(np.arange(C), (P, C)), "c_decay": decay.reshape(P, -1), "c_ropes": ropes.reshape(P, -1),
    }
    return {k: np.ascontiguousarray(v, dtype=np.float32) for k, v in c.items()}


PARTS = {("in3", 9): 3, ("uq", 0): 7, ("uq", 1): 7}
VECTORS = ["g_pre_mix", "g_post_mix", "g_pre_ffn", "g_post_ffn", "ln1_g_2", "ln1_b_2", "norm1_3", "ln2_g_2",
           "ln2_b_2", "norm2_3", "final_norm_3"]
GVSLOTS = 3


def landed_plan():
    at, out = [0] * SLOTS, []
    for name, per_slab, _ in STAGES:
        for i in range(len(per_slab)):
            at[len(out) % SLOTS] += 16 * PARTS.get((name, i), 1)
            out.append(at[len(out) % SLOTS])
    return out


def build(nc, I, out, rel_scratch):
    first, end, first_slab, release = product_plan()
    landed = landed_plan()
    with ExitStack() as ctx:
        def sb(name, shape):
            return ctx.enter_context(nc.sbuf_tensor(name, shape, F32))

        def sem(name):
            return ctx.enter_context(nc.semaphore(name))

        ring = sb("ring", [P, SLOTS, SLAB])
        X = sb("X", [P, NT, D])
        H = sb("H", [P, NT, D])
        HTY = sb("HTY", [P, SLAB])
        HT = HTY[:, 0:KT * S].rearrange("p (k s) -> p k s", k=KT)
        Y = HTY[:, KT * S:].rearrange("p (a d) -> p a d", a=NT)
        MOD = sb("MOD", [P, 6, D])
        GV = sb("GV", [P, GVSLOTS, D])
        BD = sb("BD", [P, 4, 2, S])
        QD = sb("QD", [P, 2, NBLK, 2, BLK])
        KC = sb("KC", [P, 2, NCMP])
        BIAS = sb("BIAS", [P, 8, S])
        BIASC = sb("BIASC", [P, NT, 4, NCMP])
        decay = BIAS[:, 0:4, :]
        ropes = BIAS[:, 4:8, :]
        ident = sb("ident", [P, P])
        window = sb("window", [P, S])
        causal = sb("causal", [P, S])
        diag, same = sb("diag", [P, P]), sb("same", [P, P // BLK])
        heads2 = sb("heads2", [P, 2])
        ones = sb("ones", [P, S])
        tri = sb("tri", [P, P])
        work = ctx.enter_context(nc.sbuf_tensor("work", [P, FOUR_OF + ROUNDS * E3 // 4], mybir.dt.int32))
        wr1 = sb("wr1", [P, KT, E1])
        wr3 = sb("wr3", [P, KT, G3 + E3])
        wgu = sb("wgu", [16, S])
        rows = sb("rows", [P, 1920])
        cols = sb("cols", [P, 128])
        stat = sb("stat", [P, 256])
        scr = sb("scr", [P, 13312])
        ps = ctx.enter_context(nc.psum_tensor("ps", [P, 8, BANK], F32))

        def shaped(v, shape):
            names = "abcd"[:len(shape)]
            if len(shape) == 1:
                return v
            return v.rearrange(f"p ({' '.join(names)}) -> p {' '.join(names)}",
                               **{k: s for k, s in zip(names, shape)})

        def carve(base, *shape):
            n = int(np.prod(shape))
            assert base + n <= 13312, (base, shape)
            return shaped(scr[:, base:base + n], shape)

        b_router, b_route3 = rows[:, 0:32], rows[:, 32:68]
        qn_row, kvn_row = rows[:, 128:512], rows[:, 512:768]
        gla_norm, sinks = rows[:, 768:896], rows[:, 896:904]
        conv_g, conv_b, hgrn_g = rows[:, 1024:1280], rows[:, 1280:1536], rows[:, 1536:1792]
        iota = rows[:, 1792:1792 + C]
        cvec = shaped(cols[:, 0:16], (2, KT))
        b_gate = cols[:, 16:18]
        conv_bias = cols[:, 18:20]
        tab = cols[0:33, 24:32]
        cmp_pe = shaped(cols[:, 32:64], (2, 16))
        csil = shaped(cols[:, 64:80], (2, KT))
        var, std, rstd = stat[:, 64:80], stat[:, 80:96], stat[:, 96:112]
        moment = stat[:, 0:64]
        bnst = stat[:, 128:140]
        att_stat = [{n: stat[:, 144 + 32 * b + 4 * i:148 + 32 * b + 4 * i]
                     for i, n in enumerate(("max", "shift", "sum", "inv", "sink"))} for b in range(2)]
        relv = Y[0:8, 1, 0:BANK]
        onehot = Y[0:33, 1, BANK:2 * BANK]

        slab_landed = [sem(f"slab_landed{i}") for i in range(SLOTS)]
        product_ready, product_free = sem("product_ready"), sem("product_free")
        consts_landed, first_landed = sem("consts_landed"), sem("first_landed")
        vec_landed = [sem(f"vec_landed{i}") for i in range(GVSLOTS)]
        vec_used = sem("vec_used")
        zeros_ready = sem("zeros_ready")
        rel_stored, rel_landed = sem("rel_stored"), sem("rel_landed")
        moe1_params_landed = sem("moe1_params_landed")
        block2_params_landed, tables_landed, before_landed = sem("block2_params"), sem("tables"), sem("before_landed")
        x_landed, stored = sem("x_landed"), sem("stored")
        dve_step, act_step = sem("dve_step"), sem("act_step")
        var_ready, std_ready = sem("var_ready"), sem("std_ready")
        cond_ready, h1_ready, loglog_ready = (sem(n) for n in ("cond_ready", "h1_ready", "loglog_ready"))
        mix_ready, h2_ready, route_shift, route_exp, gates_ready = (sem(n) for n in (
            "mix_ready", "h2_ready", "route_shift", "route_exp", "gates_ready"))
        m1 = {n: sem("m1_" + n) for n in (
            "counted", "listed", "pick", "pick_back", "gather", "slots_read", "turn_tokens", "gather_read", "back", "back_read",
            "up_read", "glu", "sig", "hidden", "turn",
            "turn_read", "down", "down_read", "scatter", "sum", "sum_read", "step")}
        m1_up = [sem(f"m1_up{b}") for b in range(2)]
        m1_landed = [sem(f"m1_landed{i}") for i in range(6)]
        m3 = {n: sem("m3_" + n) for n in (
            "rounds", "pick", "pick_back", "gather", "gather_read", "gates", "up", "sil", "hidden", "turn", "turn_read",
            "used", "down_read", "back", "back_read", "scatter", "sum", "sum_read", "zero", "step")}
        m3_landed = [sem(f"m3_landed{i}") for i in range(6)]
        x1_ready, blocks_ready, conv_gated, conv_ready, convln_ready, keep_ready, log_ready = (sem(n) for n in (
            "x1_ready", "blocks_ready", "conv_gated", "conv_ready", "convln_ready", "keep_ready", "log_ready"))
        y2_ready, relu_ready, x2_ready, u1_ready, cq_ready, rope_ready = (sem(n) for n in (
            "y2_ready", "relu_ready", "x2_ready", "u1_ready", "cq_ready", "rope_ready"))
        ret_scores, ret_decayed, ret_out, ret_copied, ret_ready, mlarope_ready = (sem(n) for n in (
            "ret_scores", "ret_decayed", "ret_out", "ret_copied", "ret_ready", "mlarope_ready"))
        ret_gated, merge_ready, u2_ready, final_ready, mla_ready, convsilu_ready = (sem(n) for n in (
            "ret_gated", "merge_ready", "u2_ready", "final_ready", "mla_ready", "convsilu_ready"))
        att = {n: sem("att_" + n) for n in (
            "scores", "scores_read", "shift", "probs", "turned", "turned_copied", "out", "out_read", "sink")}
        lin = {n: sem("lin_" + n) for n in (
            "cum", "qdiff", "qexp", "queries", "kexp", "keys", "keys_used", "ddiff", "dexp", "sub", "diag", "diag_used", "tiles",
            "merged", "out", "read")}

        sS, sP, sPT = carve(6400, 4, S), carve(7424, 4, S), carve(8448, 2, 4, P)
        BIASR, BIASCR, flip = carve(6400, 8, S), carve(8448, NT, 4, NCMP), carve(8704, P)
        ada_bias = [scr[0:6 * D // P, col:col + P] for col in (6144, 5120)]
        ada_quarters = carve(6272, P), carve(5248, P)
        Q1, AV = carve(0, 4, S), carve(1024, NT, P)
        GQ, GK = carve(1280, 2, S), carve(1792, 2, S)
        GVV, GG = carve(2304, NT, BANK), carve(3328, NT, BANK)
        GA, GZ, GL, CUM = carve(4352, S), carve(4608, 2, S), carve(5120, 2, S), carve(5632, 2, S)
        b1row = scr[:, 0:BANK]
        b2row = scr[0:E1, 2560:3584]
        RANK, GATE = carve(2048, NT, PASSES + 1), carve(2146, NT, PASSES + 1)
        MASK = carve(2244, NT, E1)
        MASKED = carve(2308, 3 * E1)
        gcur, rcur, rcur2 = carve(2404, NT), carve(2406, NT), carve(9120, NT)
        WORK = carve(2408, ROUNDS3)
        EPASS, ESTART = carve(2492, E1), carve(9024, E1)
        EPLACE = carve(9056, NT, E1)
        LG, GT, LX = carve(3584, NT, E1), carve(3648, NT, E1), carve(3712, NT, E1)
        gatesT = scr[0:E1, 3776:4032]
        XG, GPT, XS = carve(4032, KT, C1), carve(4544, S), carve(4800, BANK)
        PICK, PICKG = carve(5568, NT, C1), carve(5696, NT, 2, C1)
        glu, lin1 = carve(5952, 2, 256), carve(6464, 2, 256)
        sig, aS = carve(6976, 2, 256), carve(7488, 2, 256)
        aT, YS = carve(8000, 4, P), carve(8512, BANK)
        cmp1, cmp2, before = carve(9664, 32, 32), carve(10688, 32, 32), carve(11776, 32, 32)
        SEL, PROD = carve(512, PASSES, E1), shaped(MOD[:, 0, 0:PASSES // 2 * E1], (PASSES // 2, E1))
        m1_slabs = [shaped(ring[:, j, :], (KT, BANK)) for j in range(3)] + [
            MOD[:, 1:5, :].rearrange("p m (h n) -> p (m h) n", h=2), shaped(HTY[:, :], (KT, BANK)), carve(9216, KT, BANK)]
        GLA_KD = carve(10496, 2, 2, S)
        LQ = carve(6400, 2, NBLK, BLK)
        GLA_AT = carve(12032, 4, S), carve(4608, 4, P)
        GLA_LD, HG_LD = carve(10496, 2, PART, S), carve(5376, 2, PART, S)
        flat_h = H.rearrange("p a d -> p (a d)")
        QS, LQS = shaped(flat_h[:, 0:768], (2, 3, 2, NBLK * PART)), shaped(flat_h[:, 768:1152], (2, 3, NBLK, PART))
        OFFS = shaped(flat_h[:, 1152:1280], (4, P // BLK, PART))
        KS = shaped(HTY[:, 0:1536], (3, 2, S))
        Q2, QM = carve(0, 2, S), carve(512, 2, S)
        VS, VW, VM = carve(1024, NT, 64), carve(1152, NT, 64), carve(1280, NT, S)
        GN = carve(1792, NT, 12)
        KCT, BLOCKS, CHID = carve(1824, 2, S), carve(2336, 2, 16, NCMP), carve(2816, 2, 2, NCMP)
        VC = carve(2880, 64)
        CMID = carve(12032, 2, P)
        cmp_b1 = [scr[32 * (kv + 1):32 * (kv + 1) + 1, 13056:13312] for kv in range(2)]
        cw2, pww = carve(12288, 2, 2, 64), carve(12544, 2, S)
        convrow = scr[0:CONVW, 13056:13312]
        convw = carve(2944, 2, 32)
        CA, CG, CACC = carve(3520, 2, CONVW - 1 + S), carve(4096, 2, S), carve(4608, 2, S)
        CTOK, CSIL = carve(3520, NT, S), carve(4608, 2, S)
        QH, FH, IH, GH = carve(9472, 2, S), carve(9984, 2, S), carve(10496, NT, S), carve(11008, NT, S)
        HCUM, HLOG = carve(11520, 2, S), carve(4096, 2, S)
        ONSA = carve(12032, 4, 64)
        HG_KD, LQ2 = carve(0, 2, 2, S), carve(1024, 2, NBLK, BLK)
        HG_AT = carve(1824, 4, S), carve(3520, 4, P)
        FFT = carve(0, 32, S)
        RQ, RK = carve(0, 8, S), carve(2048, 8, S)
        RV, RG = carve(4096, NT, D), carve(6144, NT, D)
        RTMP = carve(8192, 2, 4, S)
        RT = carve(8192, 4, 2, S)
        CQ, CKV, KPE = carve(10240, NT, 384), carve(11008, NT, S), carve(11520, 2, S)
        CQT, CKVT = carve(12032, 3, S), carve(12800, 2, S)
        MG1, MG2 = carve(0, NT, D), MOD[:, 0:2, :]
        QNT, QPE, KNT, VV = carve(0, 8, S), carve(2048, 2, 4, S), carve(4096, 8, S), carve(9472, NT, D)
        YM = carve(0, NT, D)
        LR, GE, LE = carve(0, NT, 36), carve(128, NT, E3), carve(256, NT, G3 + E3)
        cmp3, cmp4 = carve(512, 4, 8, 8), carve(768, 4, 8, 8)
        PICKB, RANK3 = carve(1024, NT, C), carve(1216, NT, 16)
        MASK3, MASKED3 = carve(1248, NT, G3), carve(1256, 3 * G3)
        rcur3, rcurb = carve(1268, NT), carve(1270, NT)
        PT3, GSUB, GJOB = scr[0:C, 1280:1536], carve(1536, SUBS, PG3), carve(1560, TURNS)
        GE3 = carve(1600, NT, (ROUNDS * G3 + 1) * PG3)
        zero_row = scr[0:1, 1824:2336]
        XG3, hT3 = carve(5120, KT, C), carve(5888, 2, 4 * C)
        sil3, aS3 = carve(6656, 2, F3), carve(7168, 2, F3)
        YS3, PICK3 = scr[0:C, 7680:8704], carve(8704, NT, 2 * C)
        m3_slabs = [shaped(v.rearrange("p k n -> p (k n)"), (2, KT, F3)) for v in m1_slabs[0:4]] + [
            shaped(v.rearrange("p k n -> p (k n)"), (4, D)) for v in m1_slabs[4:]]
        before3 = carve(4096, 32, 32)

        units = []

        def unit(kind, tile, group, nk, width):
            units.append((kind, tile, group, nk, width))

        for t in range(NT):
            for grp in range(2):
                unit("window", t, grp, P * (t + 1), 64)
        for t in range(NT):
            for kind in ("cmp", "sel", "win", "moba"):
                unit(kind, t, 0, NCMP if kind == "cmp" else P * (t + 1), 64)
        for t in range(NT):
            for grp in range(2):
                unit("mla", t, grp, P * (t + 1), P)
        n_window, n_nsa = 4, 8

        def bias_of(u, pair):
            kind, t, grp, nk, _ = units[u]
            if kind == "cmp":
                return BIASC[:, t, 2 * pair:2 * pair + 2, :]
            k0 = S - nk
            if kind in ("sel", "win", "moba"):
                h = (4 if kind == "moba" else 0) + 2 * pair
                return BIAS[:, h:h + 2, k0:S]
            m = window if kind == "window" else causal
            return m[:, k0:S].unsqueeze(1).to_broadcast([P, 2, nk])

        def values_of(u, kt, h):
            kind, _, grp, _, _ = units[u]
            if kind == "window":
                return AV[:, kt, 64 * grp:64 * grp + 64]
            if kind == "cmp":
                return VC[0:NCMP, :]
            if kind == "sel":
                return VS[:, kt, :]
            if kind == "win":
                return VW[:, kt, :]
            if kind == "moba":
                return VM[:, kt, 64 * h:64 * h + 64]
            return VV[:, kt, (4 * grp + h) * P:(4 * grp + h + 1) * P]

        def lin_off(b, tile):
            c = S * ((b - 1) % 2) + P * tile
            return ps[:, 3 if b < 3 else 7, c:c + P]

        lin_diag = ps[:, 7, S:S + 8 * PART].rearrange("p (t h i) -> p t h i", t=NT, h=4)

        block = ctx.enter_context(nc.Block())

        def kpn(ap):
            return ap.rearrange("(k p) n -> p k n", p=P)

        def slot(s, k, n, off=0):
            return shaped(ring[:, s % SLOTS, off:off + k * n], (k, n))

        n_first, n_consts = 4, 27

        @block.sync
        def _(sp):
            at = [0]

            def slab():
                s = at[0]
                at[0] += 1
                if s >= SLOTS:
                    sp.wait_ge(product_ready, release[s - SLOTS])
                return s

            def load(s, dst, src):
                sp.dma_start(dst, src).then_inc(slab_landed[s % SLOTS], 16)

            def column_slabs(w, bounds, view=kpn):
                for lo, hi in zip(bounds, bounds[1:]):
                    s = slab()
                    load(s, slot(s, KT, hi - lo), view(w[:, lo:hi]))

            with nc.allow_non_contiguous_dma("short vectors"):
                for dst, src in ((cvec[:, 0, :], I["c"][0].rearrange("(p k) -> p k", k=KT)),
                                 (cvec[:, 1, :], I["c_3"][0].rearrange("(p k) -> p k", k=KT)),
                                 (ada_bias[0], I["b_ada"][0].rearrange("(n c) -> n c", c=P)), (ident[:, :], I["c_ident"])):
                    sp.dma_start(dst, src).then_inc(first_landed, 16)
            sp.dma_start(X[:, :, :], I["x"][0].rearrange("(a p) n -> p a n", p=P)).then_inc(x_landed, 16)

            def ada_view(ap):
                return ap.rearrange("(p k) n -> p k n", k=KT)

            wide = list(range(0, 6 * D + 1, BANK))
            column_slabs(I["w_ada"][0], wide[:5], ada_view)
            column_slabs(I["w_in"][0], [0, 512, 1024, 1536, 2048, 2320])
            column_slabs(I["w_ada"][0], wide[4:], ada_view)
            column_slabs(I["w_out"][0], [0, 512, 1024])
            def expert_slab(e, j):
                cols_ = slice(BANK * j, BANK * (j + 1))
                sp.dma_start(b1row[32 * j:32 * j + 1, :], I["b_mlp1"][0][e:e + 1, cols_] if isinstance(e, int)
                             else I["b_mlp1"][0][bass.ds(e, 1), cols_]).then_inc(m1_landed[j], 16)
                sp.dma_start(m1_slabs[j], kpn(I["w_mlp1"][0][e][:, cols_])).then_inc(m1_landed[j], 16)

            sp.wait_ge(product_ready, end["out1"])
            for j in range(3):
                expert_slab(0, j)
            sp.wait_ge(h2_ready, NT)
            expert_slab(0, 3)
            sp.wait_ge(m1["counted"], 1)
            with sp.Fori(1, E1) as e:
                through = sp.value_load(work[0:1, bass.ds(e + (THROUGH - 1), 1)], min_val=1, max_val=PASSES)
                for j in range(4):
                    sp.wait_ge(m1_up[j // 2], through)
                    expert_slab(e, j)
            n_passes = sp.value_load(work[0:1, 0:1], min_val=E1, max_val=PASSES)
            sp.wait_ge(m1_up[1], n_passes)
            column_slabs(I["w_in_2"][0], [0, 512, 908, 1420, 1932, 2444, 2956])
            for kv in range(2):
                s = slab()
                load(s, slot(s, 16, S), kpn(I["nsa_cmp_w1_2"][0, kv]))
            column_slabs(I["w_ada_3"][0], wide, ada_view)
            column_slabs(I["w_out_2"][0], [0, 512, 1024])
            column_slabs(I["w_ff1_2"][0], list(range(0, FF2 + 1, BANK)))
            for n in range(8):
                s = slab()
                load(s, slot(s, 32, P), kpn(I["w_ff2_2"][0][:, P * n:P * (n + 1)]))
            w3 = I["w_in_3"][0]
            column_slabs(w3, list(range(0, 4097, BANK)) + [4480])
            s = slab()
            load(s, slot(s, KT, 320), kpn(w3[:, 4480:4800]))
            for half in range(2):
                load(s, slot(s, KT, 64, 2560)[:, :, 32 * half:32 * half + 32],
                     kpn(w3[:, 4736 + 32 * (1 - half):4768 + 32 * (1 - half)]))
            column_slabs(w3, [4800, 5312, 5824, 6336, 6848])
            column_slabs(I["w_ret_o_3"][0], [0, 512, 1024])
            for grp in range(2):
                s = slab()
                load(s, slot(s, 3, 768), kpn(I["w_uq_3"][0][:, 768 * grp:768 * (grp + 1)]))
                pe_cols = kpn(I["w_uq_3"][0]).rearrange("p k (h c) -> p k h c", h=8)
                for half in range(2):
                    dst = shaped(ring[:, s % SLOTS, 2304:3072], (3, 4, 64))[:, :, :, 32 * half:32 * half + 32]
                    c = P + 32 * (1 - half)
                    for k in range(3):
                        load(s, dst[:, k], pe_cols[:, k, 4 * grp:4 * grp + 4, c:c + 32])
            s = slab()
            load(s, slot(s, 2, 2048), kpn(I["w_ukv_3"][0]))
            column_slabs(I["w_mla_o_3"][0], [0, 512, 1024])
            column_slabs(I["w_out_3"][0], [0, 512, 1024])
            w1 = I["w1_3"][0].rearrange("g e d f -> (g e) d f")
            w3e = I["w3_3"][0].rearrange("g e d f -> (g e) d f")
            w2 = I["w2_3"][0].rearrange("g e f d -> (g e) f d")

            def expert_slab(e, j):
                if j < 4:
                    sp.dma_start(m3_slabs[j][:, 0], kpn(w1[e + j])).then_inc(m3_landed[j], 16)
                    sp.dma_start(m3_slabs[j][:, 1], kpn(w3e[e + j])).then_inc(m3_landed[j], 16)
                else:
                    sp.dma_start(m3_slabs[j], w2[bass.ds(e + 2 * (j - 4), 2)].rearrange("e (k p) n -> p (e k) n", p=P))\
                        .then_inc(m3_landed[j], 16)

            sp.wait_ge(product_ready, end["out3"])
            for j in range(3):
                expert_slab(0, j)
            sp.wait_ge(u2_ready, NT)
            expert_slab(0, 3)
            sp.wait_ge(product_ready, end["route3"])
            expert_slab(0, 4)
            expert_slab(0, 5)
            sp.wait_ge(m3["rounds"], 1)
            n_fours = E3 // 4 * sp.value_load(work[0:1, ROUNDS3:ROUNDS3 + 1], min_val=1, max_val=ROUNDS)
            with sp.Fori(1, n_fours) as n:
                q = sp.value_load(work[0:1, bass.ds(n + FOUR_OF, 1)], min_val=0, max_val=E3 // 4 - 1)
                for j in range(4):
                    sp.wait_ge(m3["up"], SUBS * n + min(j, 2) + 1)
                    expert_slab(4 * q, j)
                for j in (4, 5):
                    sp.wait_ge(m3["used"], 2 * n + j - 3)
                    expert_slab(4 * q, j)
            sp.wait_ge(final_ready, 1)
            sp.dma_start(out[0].rearrange("(a p) n -> p a n", p=P), H[:, :, :]).then_inc(stored, 16)
            sp.wait_ge(stored, 16)

        @block.gpsimd
        def _(pool):
            n = [0]

            def const(dst, src):
                n[0] += 1
                pool.dma_start(dst, src).then_inc(consts_landed, 16)

            def row(ap):
                return ap.partition_broadcast(P)

            def vector(v):
                if v >= GVSLOTS:
                    pool.wait_ge(vec_used, v - GVSLOTS + 1)
                name = VECTORS[v]
                src = I[name] if name == "final_norm_3" else I[name][0]
                pool.dma_start(GV[:, v % GVSLOTS, :], row(src)).then_inc(vec_landed[v % GVSLOTS], 16)

            with nc.allow_non_contiguous_dma("short vectors"):
                vector(0)
                const(flip, I["c_flip"])
                const(onehot, I["c_onehot"])
                const(tab[0:32, :], I["rel_bias_2"].rearrange("h b -> b h"))
                vector(1)
                vector(2)
                const(window[:, :], I["c_window"])
                const(causal[:, :], I["c_causal"])
                const(diag[:, :], I["c_diag"])
                const(same[:, :], I["c_same"])
                const(heads2[:, :], I["c_heads2"])
                const(tri[:, :], I["c_tri"])
                const(iota, I["c_iota"])
                const(wr1[:, :, :], kpn(I["w_router"][0]))
                const(wr3[:, :, 0:G3], kpn(I["w_grp_3"][0]))
                const(wr3[:, :, G3:], kpn(I["w_exp_3"][0]))
                const(wgu[:, :], I["w_gla_gate_up"][0])
                const(b_gate, I["b_gla_gate"][0].rearrange("(c p) -> p c", p=P))
                const(conv_bias, I["conv_dw_b_2"][0].rearrange("(c p) -> p c", p=P))
                const(cmp_pe, I["nsa_cmp_pe_2"][0].rearrange("a (j r) d -> (r d) a j", r=2))
                const(b_router, row(I["b_router"][0]))
                const(b_route3[:, 0:G3], row(I["b_grp_3"][0]))
                const(b_route3[:, G3:], row(I["b_exp_3"][0]))
                const(qn_row, row(I["q_norm_3"][0]))
                const(kvn_row, row(I["kv_norm_3"][0]))
                const(gla_norm, row(I["g_gla_norm"][0]))
                const(sinks, row(I["sinks"][0]))
                const(conv_g, row(I["conv_ln_g_2"][0]))
                const(conv_b, row(I["conv_ln_b_2"][0]))
                const(hgrn_g, row(I["hgrn_norm_g_2"][0]))
            assert n[0] == n_consts
            for i, (area, value) in enumerate(((tab[32:33, :], 1.0), (ones[:, :], 1.0), (BD[:, :, :, :], 0.0),
                                               (QD[:, :, :, :, :], 0.0), (KC[:, :, :], 0.0))):
                pool.memset(area, value).then_inc(zeros_ready, 1)
                pool.wait_ge(zeros_ready, i + 1)
            pool.wait_ge(rel_stored, 16)
            rs = rel_scratch
            pool.dma_start(BIASR, bass.AP(rs.tensor, 0, [[1, P], [BANK, 8], [1, S]])).then_inc(rel_landed, 16)
            with nc.allow_non_contiguous_dma("every sixteenth distance"):
                for t in range(NT):
                    for h in range(4):
                        pool.dma_start(BIASCR[:, t, h, :], bass.AP(rs.tensor, 159 - P * t + BANK * h, [[1, P], [16, NCMP]]))\
                            .then_inc(rel_landed, 16)
            vector(3)
            pool.wait_ge(h2_ready, NT)
            pool.dma_start(b2row, I["b_mlp2"][0]).then_inc(moe1_params_landed, 16)
            pool.dma_start(before, I["c_before"].rearrange("p (a b) -> p a b", a=32)).then_inc(moe1_params_landed, 16)
            vector(4)
            vector(5)
            def expert_slab(e, j):
                pool.dma_start(m1_slabs[j], kpn(I["w_mlp2"][0][e][:, BANK * (j - 4):BANK * (j - 3)])).then_inc(m1_landed[j], 16)

            pool.wait_ge(product_ready, end["route1"])
            expert_slab(0, 4)
            pool.wait_ge(gates_ready, 1)
            expert_slab(0, 5)
            pool.wait_ge(m1["counted"], 1)
            with pool.Fori(1, E1) as e:
                through = pool.value_load(work[0:1, bass.ds(e + (THROUGH - 1), 1)], min_val=1, max_val=PASSES)
                pool.wait_ge(m1["down"], through)
                for j in (4, 5):
                    expert_slab(e, j)
            pool.wait_ge(m1["sum"], 1)
            pool.dma_start(cw2, I["nsa_cmp_w2_2"][0].rearrange("a (c p) n -> p a c n", p=P)).then_inc(block2_params_landed, 16)
            pool.dma_start(pww, kpn(I["conv_pw_w_2"][0])).then_inc(block2_params_landed, 16)
            pool.dma_start(convrow, I["conv_dw_w_2"][0]).then_inc(block2_params_landed, 16)
            for kv in range(2):
                pool.dma_start(cmp_b1[kv], I["nsa_cmp_b1_2"][0][kv:kv + 1, :]).then_inc(block2_params_landed, 16)
            pool.dma_start(ada_bias[1], I["b_ada_3"][0].rearrange("(n c) -> n c", c=P)).then_inc(block2_params_landed, 16)
            vector(6)
            vector(7)
            pool.wait_ge(mix_ready, 2)
            pool.dma_start(decay, I["c_decay"].rearrange("p (h s) -> p h s", h=4)).then_inc(tables_landed, 16)
            pool.dma_start(ropes, I["c_ropes"].rearrange("p (h s) -> p h s", h=4)).then_inc(tables_landed, 16)
            for v in range(8, 11):
                vector(v)
            pool.wait_ge(u2_ready, NT)
            pool.dma_start(before3, I["c_before"].rearrange("p (a b) -> p a b", a=32)).then_inc(before_landed, 16)

        @block.tensor
        def _(pe):
            done = [0]

            def bank():
                if done[0] >= PBANKS:
                    pe.wait_ge(product_free, done[0] - PBANKS + 1)
                return ps[:, done[0] % PBANKS, :]

            def close(mm):
                mm.then_inc(product_ready, 1)
                done[0] += 1

            def weights(s):
                pe.wait_ge(slab_landed[s % SLOTS], landed[s])

            def mm_k(o, lhs, rhs, nk, begin=True, end=True):
                for k in range(nk):
                    mm = pe.matmul(o, lhs(k), rhs(k), start=begin and k == 0, stop=end and k == nk - 1)
                return mm

            def turn(src, ready=None):
                for a in range(NT):
                    if ready is not None:
                        pe.wait_ge(ready, a + 1)
                    for half in range(2):
                        b = bank()
                        for k in range(4):
                            mm = pe.transpose(b[:, P * k:P * (k + 1)], src[:, a, P * (4 * half + k):P * (4 * half + k + 1)],
                                              ident[:, :])
                        close(mm)

            def tokens(rhs, width, lhs=HT, nk=KT, tiles=range(NT)):
                if width * NT <= BANK:
                    b = bank()
                    for a in range(NT):
                        mm = mm_k(b[:, a * width:(a + 1) * width], lambda k: lhs[:, k, P * a:P * (a + 1)], rhs, nk)
                    close(mm)
                else:
                    for a in range(NT):
                        b = bank()
                        close(mm_k(b[:, 0:width], lambda k: lhs[:, k, P * a:P * (a + 1)], rhs, nk))

            def features(cols_of, rhs=HT, nk=KT, m=P):
                b = bank()
                for i, c in enumerate(cols_of):
                    if isinstance(c, tuple):
                        for half in range(2):
                            mm = mm_k(b[64 * half:64 * half + 64, S * i:S * (i + 1)], c[half], lambda k: rhs[:, k, :], nk)
                    else:
                        mm = mm_k(b[0:m, S * i:S * (i + 1)], c, lambda k: rhs[:, k, :], nk)
                close(mm)

            def col(w, c, n=P):
                return lambda k: w[:, k, c:c + n]

            def twice(w, c):
                return col(w, c, 64), col(w, c, 64)

            def wide_stage(name, lhs=HT, width=BANK):
                n_slabs = next(len(per_slab) for stage, per_slab, _ in STAGES if stage == name)
                for i in range(n_slabs):
                    s = first_slab[name] + i
                    weights(s)
                    w = slot(s, KT, BANK)
                    tokens(lambda k: w[:, k, :], BANK, lhs)

            def modulation(name, j, i):
                at = i - (4 if name == "ada1b" else 0)
                s = first_slab[name] + at
                weights(s)
                w = slot(s, KT, BANK)
                b = bank()
                for k in range(KT):
                    for t in range(4):
                        pe.matmul(b[32 * t:32 * (t + 1), 0:P], csil[:, j, k:k + 1].to_broadcast([P, 32]), w[:, k, P * t:P * (t + 1)],
                                  start=k == 0, stop=False)
                n = ada_bias[j].shape[0]
                for t in range(4):
                    mm = pe.matmul(b[32 * t:32 * (t + 1), 0:P], ident[0:n, 4 * i + t:4 * i + t + 1].to_broadcast([n, 32]), ada_bias[j],
                                   start=False, stop=True)
                close(mm)
                pe.wait_ge(product_free, done[0])
                b = bank()
                for t in range(4):
                    mm = pe.matmul(b[:, P * t:P * (t + 1)], ident[:, 32 * t:32 * t + 1].to_broadcast([P, P]), ada_quarters[j],
                                   start=True, stop=True)
                close(mm)

            def queries_of(u, pair):
                kind, t, grp, _, _ = units[u]
                q = {"window": Q1[:, 2 * grp + pair, :] if kind == "window" else None, "cmp": Q2[:, pair, :],
                     "sel": Q2[:, pair, :], "win": Q2[:, pair, :], "moba": QM[:, pair, :],
                     "mla": QPE[:, 0, 2 * grp + pair, :] if kind == "mla" else None}[kind]
                return q[:, P * t:P * (t + 1)]

            def keys_of(u, pair):
                kind, t, grp, nk, _ = units[u]
                if kind == "cmp":
                    return KC[:, :, :]
                return BD[:, {"window": grp, "sel": 0, "win": 1, "moba": 2 + pair, "mla": 0}[kind], :, 0:nk]

            def scores(u):
                kind, t, grp, nk, _ = units[u]
                if u >= 1:
                    pe.wait_ge(att["scores_read"], u)
                for pair in range(2):
                    o = ps[:, 4 + pair, 0:2 * nk].rearrange("p (h n) -> p h n", h=2)
                    if kind != "mla":
                        mm = pe.matmul(o, queries_of(u, pair), keys_of(u, pair), start=True, stop=True)
                        continue
                    for j in range(2):
                        h = 4 * grp + 2 * pair + j
                        pe.matmul(o[:, j, :], QNT[:, h, P * t:P * (t + 1)], KNT[:, h, 0:nk], start=True, stop=False)
                        mm = pe.matmul(o[:, j, :], queries_of(u, pair), keys_of(u, pair)[:, j, :], start=False, stop=True)
                mm.then_inc(att["scores"], 1)

            def attend(u):
                kind, t, grp, nk, width = units[u]
                pe.wait_ge(att["probs"], u + 1)
                if u >= 1:
                    pe.wait_ge(att["turned_copied"], u)
                for kt in range(-(-nk // P)):
                    n = min(P, nk - P * kt)
                    for h in range(4):
                        mm = pe.transpose(ps[0:n, 6 + kt, P * h:P * (h + 1)], sP[:, h, P * kt:P * kt + n], ident[:, :])
                mm.then_inc(att["turned"], 1)
                pe.wait_ge(att["turned_copied"], u + 1)
                if u >= 1:
                    pe.wait_ge(att["out_read"], u)
                kts = range(-(-nk // P))
                for h in range(4):
                    for kt in kts:
                        n = min(P, nk - P * kt)
                        mm = pe.matmul(ps[:, 3, h * width:(h + 1) * width], sPT[0:n, kt, h, :], values_of(u, kt, h),
                                       start=kt == 0, stop=kt == kts[-1])
                mm.then_inc(att["out"], 1)

            def attention(u0, u1, between=lambda i: None):
                scores(u0)
                for u in range(u0, u1):
                    if u + 1 < u1:
                        scores(u + 1)
                    between(u - u0)
                    attend(u)

            def linear_attention(n, KDb, LDb, AT, v, dv):
                pe.wait_ge(att["out_read"], n_window + n_nsa * n)
                pe.wait_ge(lin["sub"], n + 1)
                for b in range(1, NPART):
                    for tile in range(NT):
                        for pair in range(2):
                            o = lin_off(b, tile)[:, 64 * pair:64 * (pair + 1)].rearrange("p (h t) -> p h t", h=2)
                            pe.matmul(o, KS[:, b - 1, pair, P * tile:P * (tile + 1)], QS[:, pair, b - 1, :, 32 * tile:32 * (tile + 1)],
                                      start=True, stop=True)
                pe.wait_ge(lin["diag"], n + 1)
                for tile in range(NT):
                    for pair in range(2):
                        for i in range(PART):
                            mm = pe.matmul(lin_diag[:, tile, 2 * pair:2 * pair + 2, i], LDb[:, pair, i, P * tile:P * (tile + 1)],
                                           heads2[:, :], start=True, stop=True)
                mm.then_inc(lin["diag_used"], 1)
                pe.wait_ge(lin["queries"], n + 1)
                for i in range(NBLK):
                    pe.wait_ge(lin["keys"], NBLK * n + i + 1)
                    for tile in range(1 if i < P // BLK else 2):
                        for pair in range(2):
                            if tile == 0:
                                o = ps[:, 4 + pair, :].rearrange("p (h t) -> p h t", h=2)[:, :, BLK * i:BLK * (i + 1)]
                            else:
                                o = ps[:, 6, :].rearrange("p (h t) -> p h t", h=4)[
                                    :, 2 * pair:2 * pair + 2, BLK * i - P:BLK * (i + 1) - P]
                            mm = pe.matmul(o, KDb[:, i % 2, pair, P * tile:P * (tile + 1)], QD[:, pair, i, :, :],
                                           start=True, stop=True)
                    mm.then_inc(lin["keys_used"], 1)
                pe.wait_ge(lin["merged"], n + 1)
                for a in range(NT):
                    for h in range(4):
                        for kt in range(a + 1):
                            w = AT[0][:, h, P * a:P * (a + 1)] if kt == 0 else AT[1][:, h, :]
                            mm = pe.matmul(ps[:, 4 + a, h * dv:(h + 1) * dv], w, v[:, kt, h * dv:(h + 1) * dv],
                                           start=kt == 0, stop=kt == a)
                mm.then_inc(lin["out"], 1)

            pe.wait_ge(first_landed, 16 * n_first)
            pe.wait_ge(cond_ready, 1)
            for i in range(4):
                modulation("ada1a", 0, i)
            pe.wait_ge(consts_landed, 16 * n_consts)
            pe.wait_ge(zeros_ready, 5)
            b = bank()
            close(pe.matmul(b[0:8, :], tab, onehot, start=True, stop=True))
            turn(H, h1_ready)
            pe.wait_ge(product_free, end["h1T"])
            s = first_slab["in1"]
            weights(s)
            w = slot(s, KT, BANK)
            features([col(w, 0), col(w, P)])
            features([col(w, 2 * P), col(w, 3 * P)])
            weights(s + 1)
            w = slot(s + 1, KT, BANK)
            features([twice(w, 0), twice(w, 64)])
            tokens(lambda k: w[:, k, P:2 * P], P)
            features([col(w, S), col(w, S + P)])
            weights(s + 2)
            w2 = slot(s + 2, KT, BANK)
            features([col(w2, 0), col(w2, P)])
            tokens(lambda k: w2[:, k, S:2 * S], S)
            weights(s + 3)
            w3 = slot(s + 3, KT, BANK)
            tokens(lambda k: w3[:, k, 0:S], S)
            tokens(lambda k: w3[:, k, S:2 * S], S)
            weights(s + 4)
            w4 = slot(s + 4, KT, 272)
            tokens(lambda k: w4[:, k, 0:S], S)
            features([col(w4, S, 16)], m=16)
            b = bank()
            pe.wait_ge(product_free, end["in1"])
            for c in range(2):
                mm = pe.matmul(b[:, S * c:S * (c + 1)], wgu[:, P * c:P * (c + 1)], GA[0:16, :], start=True, stop=True)
            close(mm)
            pe.wait_ge(rel_landed, 16 * (1 + 4 * NT))
            for i in range(4):
                b = bank()
                close(pe.matmul(b, flip, BIASR[:, 2 * i:2 * i + 2, :], start=True, stop=True))
            b = bank()
            close(pe.matmul(b[:, 0:NT * 4 * NCMP], flip, BIASCR, start=True, stop=True))

            def rest_of_modulation(i):
                for x in range(2):
                    modulation("ada1b", 0, 4 + 2 * i + x)

            attention(0, n_window, rest_of_modulation)
            linear_attention(0, GLA_KD, GLA_LD, GLA_AT, GVV, P)
            pe.wait_ge(mix_ready, 1)
            turn(Y)
            pe.wait_ge(product_free, end["mix1T"])
            wide_stage("out1")
            turn(H, h2_ready)
            pe.wait_ge(product_free, end["h2T"])
            tokens(lambda k: wr1[:, k, :], E1)
            pe.wait_ge(gates_ready, 1)
            b = bank()
            for a in range(NT):
                mm = pe.transpose(b[0:E1, P * a:P * (a + 1)], GT[:, a, :], ident[:, :])
            close(mm)
            pe.wait_ge(moe1_params_landed, 32)
            b = bank()
            for a in range(NT):
                pe.matmul(b[:, E1 * a:E1 * (a + 1)], tri[:, :], MASK[:, a, :], start=True, stop=a == 0)
                if a == 1:
                    pe.matmul(b[:, E1:2 * E1], ones[:, 0:P], MASK[:, 0, :], start=False, stop=True)
            for a in range(NT):
                mm = pe.matmul(b[:, 2 * E1:3 * E1], ones[:, 0:P], MASK[:, a, :], start=a == 0, stop=a == 1)
            close(mm)
            pe.wait_ge(product_free, end["gates1T"])

            def sum_bank(a, half):
                return ps[:, 4 + 2 * a + half, :]

            for a in range(NT):
                for half in range(2):
                    pe.matmul(sum_bank(a, half), gatesT[:, P * a:P * (a + 1)], b2row[:, BANK * half:BANK * (half + 1)],
                              start=True, stop=False, skip_group_check=True)

            def gather(n):
                pe.wait_ge(m1["pick"], n + 1)
                if not (isinstance(n, int) and n == 0):
                    pe.wait_ge(m1["gather_read"], n)
                for a in range(NT):
                    for half in range(2):
                        mm = pe.matmul(ps[C1 * half:C1 * (half + 1), 3, :], PICK[:, a, :], H[:, a, BANK * half:BANK * (half + 1)],
                                       start=a == 0, stop=a == NT - 1)
                mm.then_inc(m1["gather"], 1)

            def turn_tokens(n):
                pe.wait_ge(m1["slots_read"], n + 1)
                for k in range(4):
                    mm = pe.transpose(ps[:, 3, P * k:P * (k + 1)], XS[:, P * k:P * (k + 1)], ident[:, :])
                mm.then_inc(m1["turn_tokens"], 1)

            def back(n):
                pe.wait_ge(m1["pick_back"], n + 1)
                for a in range(NT):
                    mm = pe.transpose(ps[:, 2, S + P * a:S + P * (a + 1)], PICKG[:, a, :, :].rearrange("p t c -> p (t c)"),
                                      ident[:, :])
                mm.then_inc(m1["back"], 1)

            def up(n, b, e):
                for j in (2 * b, 2 * b + 1):
                    pe.wait_ge(m1_landed[j], 32 * e + 32)
                if not (isinstance(n, int) and n == 0):
                    pe.wait_ge(*((m1["up_read"], 2 * n - 1) if b == 0 else (m1["turn_read"], 2 * n)))
                for k in range(KT):
                    for s in range(2):
                        pe.matmul(ps[C1 * s:C1 * (s + 1), b, :], XG[:, k, :], m1_slabs[2 * b + s][:, k, :],
                                  start=k == 0, stop=False)
                for s in range(2):
                    r = 32 * (2 * b + s)
                    mm = pe.matmul(ps[C1 * s:C1 * (s + 1), b, :], ones[r:r + 1, 0:C1], b1row[r:r + 1, :], start=False, stop=True)
                mm.then_inc(m1_up[b], 1)

            def turn_hidden(n, b):
                pe.wait_ge(m1["hidden"], 2 * n + b + 1)
                for c in range(2):
                    mm = pe.transpose(ps[:, 2 - b, P * c:P * (c + 1)], aS[:, b, P * c:P * (c + 1)], ident[:, :])
                mm.then_inc(m1["turn"], 1)

            def down(n, e):
                pe.wait_ge(m1["turn_read"], 2 * n + 2)
                pe.wait_ge(m1["back_read"], n + 1)
                for j in (4, 5):
                    pe.wait_ge(m1_landed[j], 16 * e + 16)
                for k in range(KT):
                    b, s_, c = k // 4, k // 2 % 2, k % 2
                    for s in range(2):
                        mm = pe.matmul(ps[C1 * s:C1 * (s + 1), 2, :], aT[:, 2 * b + c, C1 * s_:C1 * (s_ + 1)],
                                       m1_slabs[4 + s][:, k, :], start=k == 0, stop=k == KT - 1)
                mm.then_inc(m1["down"], 1)

            def scatter(n, last=False):
                pe.wait_ge(m1["down_read"], n + 1)
                for a in range(NT):
                    for half in range(2):
                        mm = pe.matmul(sum_bank(a, half), GPT[C1 * half:C1 * (half + 1), P * a:P * (a + 1)],
                                       YS[C1 * half:C1 * (half + 1), :], start=False, stop=last, skip_group_check=True)
                mm.then_inc(m1["sum" if last else "scatter"], 1)

            def expert_of(n):
                return pe.value_load(work[0:1, bass.ds(n + OF_PASS, 1)], min_val=0, max_val=E1 - 1)

            def expert_pass(n, e, e_before):
                pe.wait_ge(m1["gather_read"], n + 1)
                up(n, 0, e)
                if e_before is not None:
                    turn_hidden(n - 1, 1)
                    gather(n + 1)
                    down(n - 1, e_before)
                    turn_tokens(n + 1)
                    up(n, 1, e)
                    scatter(n - 1)
                else:
                    up(n, 1, e)
                    gather(n + 1)
                    turn_tokens(n + 1)
                turn_hidden(n, 0)
                back(n)

            pe.sem_inc(m1["scatter"], 1)
            pe.wait_ge(product_free, end["rank1"])
            gather(0)
            turn_tokens(0)
            expert_pass(0, 0, None)
            pe.wait_ge(m1["listed"], 1)
            n_passes = pe.value_load(work[0:1, 0:1], min_val=E1, max_val=PASSES)
            with pe.Fori(1, n_passes) as n:
                expert_pass(n, expert_of(n), expert_of(n - 1))
            turn_hidden(n_passes - 1, 1)
            down(n_passes - 1, expert_of(n_passes - 1))
            scatter(n_passes - 1, last=True)
            pe.wait_ge(x1_ready, 1)
            pe.wait_ge(block2_params_landed, 96)
            turn(X)
            b = bank()
            for c in range(2):
                mm = pe.transpose(b[:, 32 * c:32 * c + CONVW], convrow[:, P * c:P * (c + 1)], ident[0:CONVW, 0:CONVW])
            close(mm)
            pe.wait_ge(product_free, end["x1T"])
            s = first_slab["in2"]
            weights(s)
            w = slot(s, KT, BANK)
            features([col(w, 0), col(w, P)])
            features([twice(w, 256), twice(w, 320)])
            features([twice(w, 384)])
            tokens(lambda k: w[:, k, 448:512], 64)
            weights(s + 1)
            w1 = slot(s + 1, KT, 396)
            features([twice(w1, 0)])
            tokens(lambda k: w1[:, k, 64:140], 76)
            features([col(w1, 140), col(w1, 268)])
            for i in range(4):
                weights(s + 2 + i)
                wi = slot(s + 2 + i, KT, BANK)
                if i < 3:
                    features([col(wi, 0), col(wi, P)])
                if i in (1, 2):
                    features([col(wi, S), col(wi, S + P)])
                if i == 3:
                    tokens(lambda k: wi[:, k, 0:S], S)
                if i in (0, 3):
                    tokens(lambda k: wi[:, k, S:2 * S], S)
            pe.wait_ge(blocks_ready, 1)
            for kv in range(2):
                s = first_slab["cmp2"] + kv
                weights(s)
                w = slot(s, 16, S)
                b = bank()
                for k in range(16):
                    for c in range(2):
                        pe.matmul(b[64 * c:64 * c + NCMP, 0:P], BLOCKS[:, kv, k, :], w[:, k, P * c:P * (c + 1)], start=k == 0, stop=False)
                r = 32 * (kv + 1)
                for c in range(2):
                    mm = pe.matmul(b[64 * c:64 * c + NCMP, 0:P], ones[r:r + 1, 0:NCMP], cmp_b1[kv][:, P * c:P * (c + 1)],
                                   start=False, stop=True)
                close(mm)
            pe.wait_ge(product_free, end["cmp2"] - 3)
            b = bank()
            for kv in range(2):
                mm = pe.transpose(b[:, P * kv:P * (kv + 1)], CMID[:, kv, :], ident[:, :])
            close(mm)
            pe.wait_ge(product_free, end["cmp2"] - 2)
            b = bank()
            for half in range(2):
                mm = mm_k(b[64 * half:64 * half + 64, 0:NCMP], lambda k: cw2[:, 0, k, :], lambda k: CHID[:, 0, k, :], 2)
            close(mm)
            b = bank()
            close(mm_k(b[0:NCMP, 0:64], lambda k: CHID[:, 1, k, :], lambda k: cw2[:, 1, k, :], 2))
            pe.wait_ge(product_free, end["cmp2"])
            attention(n_window, n_window + n_nsa, lambda i: modulation("ada3", 1, i))
            for i in range(n_nsa, 12):
                modulation("ada3", 1, i)
            pe.wait_ge(conv_ready, 1)
            b = bank()
            for a in range(NT):
                for c in range(2):
                    mm = pe.transpose(b[:, S * a + P * c:S * a + P * (c + 1)], CACC[:, c, P * a:P * (a + 1)], ident[:, :])
            close(mm)
            pe.wait_ge(convsilu_ready, 1)
            b = bank()
            for c in range(2):
                for a in range(NT):
                    mm = pe.transpose(b[:, S * c + P * a:S * c + P * (a + 1)], CTOK[:, a, P * c:P * (c + 1)], ident[:, :])
            close(mm)
            pe.wait_ge(product_free, end["convback"])
            tokens(lambda k: pww[:, k, :], S, lhs=CSIL, nk=2)
            linear_attention(1, HG_KD, HG_LD, HG_AT, IH, 64)
            pe.wait_ge(mix_ready, 2)
            turn(Y)
            pe.wait_ge(product_free, end["mix2T"])
            wide_stage("out2")
            pe.wait_ge(y2_ready, 1)
            turn(X)
            pe.wait_ge(product_free, end["y2T"])
            for i in range(8):
                s = first_slab["ff1"] + i
                weights(s)
                w = slot(s, KT, BANK)
                features([col(w, 0), col(w, P)])
                features([col(w, 2 * P), col(w, 3 * P)])
            pe.wait_ge(relu_ready, 16)
            for i in range(8):
                s = first_slab["ff2"] + i
                weights(s)
                w = slot(s, 32, P)
                tokens(lambda k: w[:, k, :], P, lhs=FFT, nk=32)
            turn(H, u1_ready)
            pe.wait_ge(product_free, end["u1T"])
            s = first_slab["in3"]
            for i in range(9):
                weights(s + i)
                w = slot(s + i, KT, BANK if i < 8 else 384)
                if i < 4:
                    features([col(w, 0), col(w, P)])
                    features([col(w, 2 * P), col(w, 3 * P)])
                else:
                    tokens(lambda k: w[:, k, :], BANK if i < 8 else 384)
            weights(s + 9)
            w = slot(s + 9, KT, 320)
            wx = slot(s + 9, KT, 64, 2560)
            tokens(lambda k: w[:, k, 0:S], S)
            features([twice(w, S), twice(wx, 0)])
            pe.wait_ge(rope_ready, 1)
            pe.wait_ge(product_free, end["in3"])

            def ret_out_of(h):
                pe.wait_ge(ret_decayed, h + 1)
                if h >= 2:
                    pe.wait_ge(ret_copied, h - 1)
                for a in range(NT):
                    for kt in range(a + 1):
                        mm = pe.matmul(ps[:, 6 + h % 2, S * a:S * (a + 1)], RT[:, h, kt, P * a:P * (a + 1)],
                                       RV[:, kt, S * h:S * (h + 1)], start=kt == 0, stop=kt == a)
                mm.then_inc(ret_out, 1)

            for h in range(4):
                if h >= 2:
                    pe.wait_ge(ret_decayed, h - 1)
                for kt in range(NT):
                    o = ps[:, 4 + h % 2, 0:S] if kt == 0 else ps[:, 4 + h % 2, S:S + P]
                    mm = mm_k(o, lambda c: RK[:, 2 * h + c, P * kt:P * (kt + 1)], lambda c: RQ[:, 2 * h + c, P * kt:S], 2)
                mm.then_inc(ret_scores, 1)
                if h >= 1:
                    ret_out_of(h - 1)
            ret_out_of(3)
            wide_stage("gates3")
            pe.wait_ge(ret_ready, 1)
            turn(Y)
            pe.wait_ge(product_free, end["retT"])
            wide_stage("reto")
            pe.wait_ge(cq_ready, 1)
            for a in range(NT):
                b = bank()
                for c in range(3):
                    mm = pe.transpose(b[:, P * c:P * (c + 1)], CQ[:, a, P * c:P * (c + 1)], ident[:, :])
                close(mm)
            b = bank()
            for c in range(2):
                for a in range(NT):
                    mm = pe.transpose(b[:, S * c + P * a:S * c + P * (a + 1)], CKV[:, a, P * c:P * (c + 1)], ident[:, :])
            close(mm)
            pe.wait_ge(product_free, end["cqT"])
            for grp in range(2):
                s = first_slab["uq"] + grp
                weights(s)
                w = slot(s, 3, 768).rearrange("p k (h c) -> p k h c", h=4)
                wx = shaped(ring[:, s % SLOTS, 2304:3072], (3, 4, 64))
                for j in range(2):
                    features([lambda k, h=2 * j + i: w[:, k, h, 0:P] for i in range(2)], rhs=CQT, nk=3)
                features([tuple(lambda k, h=2 * i + x: w[:, k, h, P:] for x in range(2)) for i in range(2)], rhs=CQT, nk=3)
                features([tuple(lambda k, h=2 * i + x: wx[:, k, h, :] for x in range(2)) for i in range(2)], rhs=CQT, nk=3)
            s = first_slab["ukv"]
            weights(s)
            w = slot(s, 2, 2048).rearrange("p k (h c) -> p k h c", h=8)
            for j in range(4):
                features([lambda k, h=2 * j + i: w[:, k, h, 0:P] for i in range(2)], rhs=CKVT, nk=2)
            for half in range(2):
                tokens(lambda k: w[:, k, 4 * half:4 * half + 4, P:], BANK, lhs=CKVT, nk=2)
            pe.wait_ge(mlarope_ready, 1)
            pe.wait_ge(product_free, end["ukv"])
            attention(n_window + n_nsa, len(units))
            pe.wait_ge(mla_ready, 1)
            turn(Y)
            pe.wait_ge(product_free, end["mlaT"])
            wide_stage("mlao")
            pe.wait_ge(merge_ready, 1)
            turn(H)
            pe.wait_ge(product_free, end["mergeT"])
            wide_stage("out3")
            turn(H, u2_ready)
            pe.wait_ge(product_free, end["u2T"])
            tokens(lambda k: wr3[:, k, :], G3 + E3)
            pe.wait_ge(product_free, end["route3"])
            pe.wait_ge(m3["zero"], 1)
            for a in range(NT):
                for half in range(2):
                    pe.matmul(sum_bank(a, half), ones[0:1, 0:P], zero_row, start=True, stop=False, skip_group_check=True)
            b = bank()
            for a in range(NT):
                pe.matmul(b[:, G3 * a:G3 * (a + 1)], tri[:, :], MASK3[:, a, :], start=True, stop=a == 0)
                if a == 1:
                    pe.matmul(b[:, G3:2 * G3], ones[:, 0:P], MASK3[:, 0, :], start=False, stop=True)
            for a in range(NT):
                mm = pe.matmul(b[:, 2 * G3:3 * G3], ones[:, 0:P], MASK3[:, a, :], start=a == 0, stop=a == 1)
            close(mm)
            pe.sem_inc(m3["up"], SUBS)
            pe.sem_inc(m3["used"], 2)

            def gather(n):
                pe.wait_ge(m3["pick"], n + 1)
                if not (isinstance(n, int) and n == 0):
                    pe.wait_ge(m3["turn_read"], TURNS * n)
                for half in range(2):
                    for k in range(4):
                        mm = mm_k(ps[:, half, C * k:C * (k + 1)], lambda a: H[:, a, P * (4 * half + k):P * (4 * half + k + 1)],
                                  lambda a: PICK3[:, a, 0:C], NT)
                    if half == 0:
                        for s in range(SUBS):
                            mm = mm_k(ps[:, 0, 4 * C + PG3 * s:4 * C + PG3 * (s + 1)], lambda a: PICK3[:, a, 32 * s:32 * s + P],
                                      lambda a: GE3[:, a, bass.ds(PG3 * n, PG3)], NT)
                    mm.then_inc(m3["gather"], 1)

            def back(n):
                pe.wait_ge(m3["pick_back"], n + 1)
                pe.wait_ge(m3["down_read"], n + 1)
                for a in range(NT):
                    mm = pe.transpose(ps[0:C, 2, P * a:P * (a + 1)], PICKB[:, a, :], ident[:, :])
                mm.then_inc(m3["back"], 1)

            def scatter(n):
                pe.wait_ge(m3["back_read"], n + 1)
                for a in range(NT):
                    for half in range(2):
                        mm = pe.matmul(sum_bank(a, half), PT3[:, P * a:P * (a + 1)], YS3[:, BANK * half:BANK * (half + 1)],
                                       start=False, stop=False, skip_group_check=True)
                mm.then_inc(m3["scatter"], 1)

            def jobs(n, i):
                m = 2 * n + i // SUBS
                mine = [(JOBS * (i % SUBS) + t) // SUBS for t in range(JOBS)]
                for j in sorted(set(mine)):
                    pe.wait_ge(m3_landed[j], 32 * m + 32)
                if i >= 2:
                    pe.wait_ge(m3["turn_read"], TURNS * n + i - 1)
                for k in range(KT):
                    for t in range(JOBS):
                        s = (i + t) % SUBS
                        mm = pe.matmul(ps[32 * t:32 * (t + 1), i % 2, :].rearrange("p (x f) -> p x f", x=2),
                                       XG3[:, k, 32 * s:32 * (s + 1)], m3_slabs[mine[t]][:, :, k, :], start=k == 0, stop=k == KT - 1)
                mm.then_inc(m3["up"], 1)

            def turn_jobs(n, i):
                pe.wait_ge(m3["hidden"], TURNS * n + i + 1)
                for c in range(2):
                    mm = pe.transpose(ps[:, i % 2, P * c:P * (c + 1)], aS3[:, i % 2, P * c:P * (c + 1)], ident[:, :])
                mm.then_inc(m3["turn"], 1)

            def down(n, x):
                m, j = 2 * n + x // 4, 4 + x % 4 // 2
                pe.wait_ge(m3["turn_read"], TURNS * n + (SUBS * x + SUBS - 1) // JOBS + 1)
                pe.wait_ge(m3_landed[j], 16 * m + 16)
                for half in range(2):
                    for c in range(2):
                        mm = pe.matmul(ps[0:C, 2 + half, :], hT3[:, c, C * (x % 4):C * (x % 4 + 1)],
                                       m3_slabs[j][:, 2 * (x % 2) + c, BANK * half:BANK * (half + 1)],
                                       start=x == 0 and c == 0, stop=x == PG3 - 1 and c == 1)
                if x % 2:
                    mm.then_inc(m3["used"], 1)

            def group_pass(n, first=False):
                pe.wait_ge(m3["gather_read"], 2 * n + 2)
                jobs(n, 0)
                jobs(n, 1)
                if not first:
                    back(n - 1)
                turn_jobs(n, 0)
                jobs(n, 2)
                turn_jobs(n, 1)
                if not first:
                    scatter(n - 1)
                down(n, 0)
                jobs(n, 3)
                turn_jobs(n, 2)
                down(n, 1)
                jobs(n, 4)
                turn_jobs(n, 3)
                down(n, 2)
                down(n, 3)
                jobs(n, 5)
                turn_jobs(n, 4)
                down(n, 4)
                turn_jobs(n, 5)
                down(n, 5)
                gather(n + 1)
                down(n, 6)
                down(n, 7)

            pe.wait_ge(m3["rounds"], 1)
            n_groups = G3 * pe.value_load(work[0:1, ROUNDS3:ROUNDS3 + 1], min_val=1, max_val=ROUNDS)
            pe.wait_ge(product_free, end["rank3"])
            gather(0)
            group_pass(0, first=True)
            with pe.Fori(1, n_groups) as n:
                group_pass(n)
            back(n_groups - 1)
            scatter(n_groups - 1)
            for a in range(NT):
                for half in range(2):
                    mm = pe.matmul(sum_bank(a, half), ones[0:1, 0:P], zero_row, start=False, stop=True, skip_group_check=True)
            mm.then_inc(m3["sum"], 1)

        @block.scalar
        def _(act):
            done = [0]
            steps = [0]
            roots = [0]

            def step(ins):
                ins.then_inc(act_step, 1)
                steps[0] += 1
                act.wait_ge(act_step, steps[0])

            def product():
                g = done[0]
                act.wait_ge(product_ready, g + 1)
                done[0] += 1
                return ps[:, g % PBANKS, :]

            def read(dst, src, func=ACT.Copy, **kw):
                act.activation(dst, src, func, **kw).then_inc(product_free, 1)

            def two(b, n=S):
                return b[:, 0:2 * n].rearrange("p (c n) -> p c n", c=2)

            def root(n):
                roots[0] += 1
                act.wait_ge(var_ready, roots[0])
                act.activation(std[:, 0:n], var[:, 0:n], ACT.Sqrt).then_inc(std_ready, 1)

            def turned():
                for a in range(NT):
                    for half in range(2):
                        b = product()
                        read(HT[:, 4 * half:4 * half + 4, P * a:P * (a + 1)], b.rearrange("p (k n) -> p k n", k=4))

            def wide(dst, func=ACT.Copy):
                for i in range(2):
                    for a in range(NT):
                        b = product()
                        read(dst[:, a, BANK * i:BANK * (i + 1)], b, func)

            def diagonal(b, first_slot, n):
                v = b[:, 0:S * n].rearrange("p (c n) -> p c n", c=n)
                act.activation(BD[0:64, first_slot:first_slot + n, 0, :], v[0:64], ACT.Copy)
                read(BD[64:P, first_slot:first_slot + n, 1, :], v[64:P])

            def modulation(j, i):
                read(ada_quarters[j], product()[:, 0:P])
                read(MOD.rearrange("p m d -> p (m d)")[:, BANK * i:BANK * (i + 1)], product())

            def attention(u0, u1, between=lambda i: None):
                for u in range(u0, u1):
                    kind, t, grp, nk, _ = units[u]
                    st = att_stat[u % 2]
                    act.wait_ge(att["shift"], u + 1)
                    if u >= 1:
                        act.wait_ge(att["turned"], u)
                    if kind == "window":
                        act.activation(st["sink"], st["sink"], ACT.Exp)
                    for h in range(4):
                        ins = act.activation(sP[:, h, 0:nk], sS[:, h, 0:nk], ACT.Exp, bias=st["shift"][:, h:h + 1],
                                             accum_out=st["sum"][:, h:h + 1])
                    ins.then_inc(att["probs"], 1)
                    between(u - u0)
                    act.wait_ge(att["turned"], u + 1)
                    if u >= 1:
                        act.wait_ge(att["out"], u)
                    kts = -(-nk // P)
                    n = min(nk, P)
                    act.activation(sPT[0:n, 0:kts, :, :].rearrange("p k h q -> p k (h q)"), ps[0:n, 6:6 + kts, :], ACT.Copy)\
                        .then_inc(att["turned_copied"], 1)

            def queries_decay(n, LQb):
                act.wait_ge(lin["qdiff"], n + 1)
                act.activation(LQb, LQb, ACT.Exp).then_inc(lin["qexp"], 1)

            def within_blocks(n, LDb):
                act.wait_ge(lin["ddiff"], n + 1)
                act.activation(LQS, LQS, ACT.Exp)
                for b in range(1, NPART):
                    kb = KS[:, b - 1].rearrange("p c (b i) -> p c b i", i=BLK)[:, :, :, 0:PART * b]
                    act.activation(kb, kb, ACT.Exp)
                act.activation(LDb, LDb, ACT.Exp).then_inc(lin["dexp"], 1)

            def linear_attention(n, cum, KDb, dst, dv):
                act.wait_ge(lin["queries"], n + 1)
                for i in range(1, NBLK):
                    if i >= 2:
                        act.wait_ge(lin["keys_used"], NBLK * n + i - 1)
                    for pair in range(2):
                        ins = act.activation(KDb[:, i % 2, pair, 0:BLK * i], cum[:, pair, 0:BLK * i], ACT.Exp,
                                             bias=cum[:, pair, BLK * i - 1:BLK * i], scale=-1.0)
                    ins.then_inc(lin["kexp"], 1)
                act.wait_ge(lin["out"], n + 1)
                for a in range(NT):
                    act.activation(dst[:, a, :], ps[:, 4 + a, 0:4 * dv], ACT.Copy).then_inc(lin["read"], 1)

            def log_sigmoid_part(dst, src):
                step(act.activation(dst, src, ACT.Abs))
                step(act.activation(dst, dst, ACT.Exp, scale=-1.0))
                act.activation(dst, dst, ACT.Ln, bias=1.0).then_inc(loglog_ready, 1)

            act.wait_ge(first_landed, 16 * n_first)
            act.activation(csil[:, :, :], cvec[:, :, :], ACT.Silu).then_inc(cond_ready, 1)
            root(2)
            for i in range(4):
                modulation(0, i)
            act.wait_ge(consts_landed, 16 * n_consts)
            b = product()
            read(relv, b[0:8, :])
            act.wait_ge(product_free, end["rel"])
            act.dma_start(rel_scratch, relv).then_inc(rel_stored, 16)
            turned()
            for i in range(2):
                b = product()
                read(Q1[:, 2 * i:2 * i + 2, :], two(b))
            diagonal(product(), 0, 2)
            read(AV[:, :, :], two(product(), P))
            read(GQ[:, :, :], two(product()), scale=0.125)
            read(GK[:, :, :], two(product()))
            for i in range(2):
                read(GVV[:, :, S * i:S * (i + 1)], two(product()))
            for i in range(2):
                read(GG[:, :, S * i:S * (i + 1)], two(product()), ACT.Silu)
            read(GA[0:16, :], product()[0:16, 0:S])
            b = product()
            act.activation(GZ[:, 0, :], b[:, 0:S], ACT.Identity, bias=b_gate[:, 0:1])
            read(GZ[:, 1, :], b[:, S:2 * S], ACT.Identity, bias=b_gate[:, 1:2])
            act.wait_ge(product_free, end["gate1"])
            log_sigmoid_part(GL[:, :, :], GZ[:, :, :])
            for i in range(4):
                read(BIAS[:, 2 * i:2 * i + 2, :], two(product()))
            read(BIASC[:, :, :, :].rearrange("p t h n -> p (t h n)"), product()[:, 0:NT * 4 * NCMP])

            def rest_of_modulation(i):
                modulation(0, 4 + 2 * i)
                modulation(0, 5 + 2 * i)
                if i == 1:
                    within_blocks(0, GLA_LD)

            attention(0, n_window, rest_of_modulation)
            queries_decay(0, LQ[:, :, :, :])
            linear_attention(0, CUM, GLA_KD, Y[:, :, BANK:], P)
            root(8)
            turned()
            wide(H)
            root(2)
            root(2)
            turned()
            read(LG[:, :, :], two(product(), E1))
            act.wait_ge(route_shift, 1)
            act.activation(LX[:, :, :], LX[:, :, :], ACT.Exp).then_inc(route_exp, 1)
            read(gatesT, product()[0:E1, 0:S])
            read(MASKED[:, :], product()[:, 0:3 * E1])

            def slots(n):
                act.wait_ge(m1["gather"], n + 1)
                act.activation(XS, ps[:, 3, :], ACT.Copy).then_inc(m1["slots_read"], 1)

            def gathered(n):
                if not (isinstance(n, int) and n == 0):
                    act.wait_ge(m1_up[1], n)
                act.wait_ge(m1["turn_tokens"], n + 1)
                act.activation(XG.rearrange("p (h k) c -> p k h c", h=2), ps[:, 3, :].rearrange("p (k h c) -> p k h c", k=4, h=2),
                               ACT.Copy).then_inc(m1["gather_read"], 1)

            def way_back(n):
                act.wait_ge(m1["back"], n + 1)
                act.activation(GPT, ps[:, 2, S:2 * S], ACT.Copy).then_inc(m1["back_read"], 1)

            def gate(n, b):
                act.wait_ge(m1["glu"], 2 * n + b + 1)
                act.activation(sig[:, b, :], glu[:, b, :], ACT.Sigmoid, scale=1.702).then_inc(m1["sig"], 1)

            def turned_hidden(n, b):
                act.wait_ge(m1["turn"], 2 * n + b + 1)
                act.activation(aT[:, 2 * b:2 * b + 2, :], two(ps[:, 2 - b, :], P), ACT.Copy).then_inc(m1["turn_read"], 1)

            def outputs(n):
                act.wait_ge(m1["scatter"], n + 1)
                act.wait_ge(m1["down"], n + 1)
                act.activation(YS, ps[:, 2, :], ACT.Copy).then_inc(m1["down_read"], 1)

            def expert_pass(n, first=False):
                gate(n, 0)
                if not first:
                    turned_hidden(n - 1, 1)
                slots(n + 1)
                if not first:
                    outputs(n - 1)
                gathered(n + 1)
                gate(n, 1)
                way_back(n)
                turned_hidden(n, 0)

            slots(0)
            gathered(0)
            expert_pass(0, first=True)
            act.wait_ge(m1["listed"], 1)
            n_passes = act.value_load(work[0:1, 0:1], min_val=E1, max_val=PASSES)
            with act.Fori(1, n_passes) as n:
                expert_pass(n)
            turned_hidden(n_passes - 1, 1)
            outputs(n_passes - 1)
            act.wait_ge(m1["sum"], 1)
            for a in range(NT):
                act.activation(Y[:, a, :].rearrange("p (c n) -> p c n", c=2), ps[:, 4 + 2 * a:6 + 2 * a, :], ACT.Copy)\
                    .then_inc(m1["sum_read"], 1)
            root(2)
            turned()
            read(convw[:, :, 0:CONVW], two(product(), 32)[:, :, 0:CONVW])
            read(Q2[:, :, :], two(product()))
            read(KCT[:, :, :], two(product()))
            diagonal(product(), 0, 1)
            read(VS[:, :, :], two(product(), 64))
            diagonal(product(), 1, 1)
            b = two(product(), 76)
            act.activation(GN[:, :, :], b[:, :, 64:76], ACT.Sigmoid)
            read(VW[:, :, :], b[:, :, 0:64])
            read(QM[:, :, :], two(product()))
            diagonal(product(), 2, 2)
            read(VM[:, :, :], two(product()))
            read(CA[:, :, CONVW - 1:], two(product()))
            read(CG[:, :, :], two(product()), ACT.Sigmoid)
            read(QH[:, :, :], two(product()))
            read(FH[:, :, :], two(product()))
            read(IH[:, :, :], two(product()))
            read(GH[:, :, :], two(product()), ACT.Sigmoid)
            act.wait_ge(conv_gated, 1)
            act.wait_ge(product_free, end["in2"])
            log_sigmoid_part(HLOG[:, :, :], FH[:, :, :])
            act.wait_ge(log_ready, 1)
            act.activation(FH[:, :, :], FH[:, :, :], ACT.Sigmoid, scale=-1.0).then_inc(keep_ready, 1)
            for kv in range(2):
                b = product()
                act.activation(CMID[0:NCMP, kv, :], b[0:NCMP, 0:P], ACT.Gelu_apprx_tanh)
                read(CMID[64:64 + NCMP, kv, :], b[64:64 + NCMP, 0:P], ACT.Gelu_apprx_tanh)
            read(CHID[:, :, :, :], product()[:, 0:2 * P].rearrange("p (a c n) -> p a c n", a=2, c=2)[:, :, :, 0:NCMP])
            b = product()
            act.activation(KC[0:64, 0, :], b[0:64, 0:NCMP], ACT.Copy)
            read(KC[64:P, 1, :], b[64:P, 0:NCMP])
            read(VC[0:NCMP, :], product()[0:NCMP, 0:64])
            attention(n_window, n_window + n_nsa, lambda i: modulation(1, i))
            for i in range(n_nsa, 12):
                modulation(1, i)
                if i == 10:
                    within_blocks(1, HG_LD)
                    queries_decay(1, LQ2[:, :, :, :])
            read(CTOK[:, :, :], two(product()))
            root(2)
            act.wait_ge(convln_ready, 1)
            act.activation(CTOK[:, :, :], CTOK[:, :, :], ACT.Silu).then_inc(convsilu_ready, 1)
            read(CSIL[:, :, :], two(product()))
            read(Y[:, :, 512:768], two(product()))
            linear_attention(1, HCUM, HG_KD, Y[:, :, 768:], 64)
            root(8)
            turned()
            wide(H)
            root(2)
            turned()
            for i in range(16):
                read(FFT[:, 2 * i:2 * i + 2, :], two(product()), ACT.Relu)
            for i in range(8):
                read(H[:, :, P * i:P * (i + 1)], two(product(), P))
            root(2)
            root(2)
            turned()
            for i in range(4):
                read(RQ[:, 2 * i:2 * i + 2, :], two(product()))
            for i in range(4):
                read(RK[:, 2 * i:2 * i + 2, :], two(product()))
            wide(RV)
            wide(RG, ACT.Silu)
            for a in range(NT):
                read(CQ[:, a, :], product()[:, 0:384])
            read(CKV[:, :, :], two(product()))
            read(KPE[:, :, :], two(product()))
            root(4)
            for h in range(4):
                act.wait_ge(ret_out, h + 1)
                act.activation(Y[:, :, S * h:S * (h + 1)], two(ps[:, 6 + h % 2, :]), ACT.Copy).then_inc(ret_copied, 1)
            root(8)
            wide(MG1, ACT.Sigmoid)
            wide(MG2, ACT.Sigmoid)
            turned()
            wide(H)
            for a in range(NT):
                read(CQT[:, :, P * a:P * (a + 1)], product()[:, 0:384].rearrange("p (c n) -> p c n", c=3))
            read(CKVT[:, :, :], two(product()))
            act.wait_ge(ret_gated, 1)
            for grp in range(2):
                for j in range(2):
                    read(QNT[:, 4 * grp + 2 * j:4 * grp + 2 * j + 2, :], two(product()))
                for j in range(2):
                    read(QPE[:, j, 2 * grp:2 * grp + 2, :], two(product()))
            for j in range(4):
                read(KNT[:, 2 * j:2 * j + 2, :], two(product()))
            wide(VV)
            attention(n_window + n_nsa, len(units))
            turned()
            wide(YM)
            turned()
            wide(H)
            root(2)
            turned()
            read(LR[:, :, :], two(product(), G3 + E3))
            act.wait_ge(route_shift, 2)
            act.activation(LE[:, :, :], LE[:, :, :], ACT.Exp).then_inc(route_exp, 1)
            read(MASKED3[:, :], product()[:, 0:3 * G3])
            act.wait_ge(m3["rounds"], 1)
            n_groups = G3 * act.value_load(work[0:1, ROUNDS3:ROUNDS3 + 1], min_val=1, max_val=ROUNDS)

            def gathered(n):
                for half in range(2):
                    act.wait_ge(m3["gather"], 2 * n + half + 1)
                    if half == 0:
                        act.activation(GSUB, ps[:, 0, 4 * C:4 * C + SUBS * PG3].rearrange("p (s e) -> p s e", s=SUBS), ACT.Copy)
                    act.activation(XG3[:, 4 * half:4 * half + 4, :], ps[:, half, 0:4 * C].rearrange("p (k c) -> p k c", k=4),
                                   ACT.Copy).then_inc(m3["gather_read"], 1)

            def gate(n, i):
                act.wait_ge(m3["up"], TURNS * n + i + 1 + SUBS)
                act.activation(sil3[:, i % 2, :], ps[:, i % 2, 0:F3], ACT.Silu).then_inc(m3["sil"], 1)

            def turned_jobs(n, i):
                act.wait_ge(m3["turn"], TURNS * n + i + 1)
                at = P * (i % SUBS)
                act.activation(hT3[:, :, at:at + P], two(ps[:, i % 2, :], P), ACT.Copy).then_inc(m3["turn_read"], 1)

            def way_back(n):
                act.wait_ge(m3["back"], n + 1)
                act.activation(PT3, ps[0:C, 2, 0:S], ACT.Copy).then_inc(m3["back_read"], 1)

            def group_pass(n, first=False):
                gate(n, 0)
                gate(n, 1)
                if not first:
                    way_back(n - 1)
                turned_jobs(n, 0)
                gate(n, 2)
                turned_jobs(n, 1)
                for i in range(3, TURNS):
                    gate(n, i)
                    turned_jobs(n, i - 1)
                turned_jobs(n, TURNS - 1)
                gathered(n + 1)
                act.wait_ge(m3["used"], PG3 // 2 * (n + 1) + 2)
                act.activation(YS3.rearrange("p (c n) -> p c n", c=2), ps[0:C, 2:4, :], ACT.Copy).then_inc(m3["down_read"], 1)

            gathered(0)
            group_pass(0, first=True)
            with act.Fori(1, n_groups) as n:
                group_pass(n)
            way_back(n_groups - 1)
            act.wait_ge(m3["sum"], 1)
            for a in range(NT):
                act.activation(Y[:, a, :].rearrange("p (c n) -> p c n", c=2), ps[:, 4 + 2 * a:6 + 2 * a, :], ACT.Copy)\
                    .then_inc(m3["sum_read"], 1)
            root(2)

        @block.vector
        def _(dve):
            steps = [0]
            roots = [0]
            vectors = [0]

            def step(ins):
                ins.then_inc(dve_step, 1)
                steps[0] += 1
                dve.wait_ge(dve_step, steps[0])

            def tell(ins, signal, value):
                ins.then_inc(signal, 1)
                dve.wait_ge(signal, value)

            def vector():
                v = vectors[0]
                dve.wait_ge(vec_landed[v % GVSLOTS], 16 * (v // GVSLOTS + 1))
                return GV[:, v % GVSLOTS, :]

            def vector_done(ins):
                vectors[0] += 1
                tell(ins, vec_used, vectors[0])

            def moments(src, i):
                n = src.shape[-1]
                parts = -(-n // BANK)
                for c in range(parts):
                    step(dve.bn_stats(bnst[:, 6 * c:6 * c + 6], src[:, BANK * c:min(n, BANK * (c + 1))]))
                step(dve.bn_aggr(moment[:, 2 * i:2 * i + 2], bnst[:, 0:6 * parts]))

            def inverse_roots(n, eps, square=False):
                mean, variance = moment[:, 0:2 * n:2], moment[:, 1:2 * n:2]
                if square:
                    step(dve.tensor_tensor(var[:, 0:n], mean, mean, ALU.mult))
                    step(dve.tensor_tensor(var[:, 0:n], var[:, 0:n], variance, ALU.add))
                    variance = var[:, 0:n]
                roots[0] += 1
                tell(dve.tensor_scalar(var[:, 0:n], variance, eps, None, ALU.add), var_ready, roots[0])
                dve.wait_ge(std_ready, roots[0])
                step(dve.reciprocal(rstd[:, 0:n], std[:, 0:n]))

            def both(v):
                return v.unsqueeze(1).to_broadcast([P, NT, v.shape[-1]])

            def gain_scale(scale):
                m = MOD[:, scale, :]
                vector_done(dve.scalar_tensor_tensor(m, m, 1.0, vector(), ALU.add, ALU.mult))

            def gain_gate(gate):
                vector_done(dve.tensor_tensor(MOD[:, gate, :], MOD[:, gate, :], vector(), ALU.mult))

            def rms_modulate(src, shift, scale, ready, before=lambda: None):
                for a in range(NT):
                    moments(src[:, a, :], a)
                inverse_roots(NT, 1e-6, square=True)
                before()
                for a in range(NT):
                    step(dve.scalar_tensor_tensor(H[:, a, :], src[:, a, :], rstd[:, a:a + 1], MOD[:, scale, :], ALU.mult, ALU.mult))
                    tell(dve.tensor_tensor(H[:, a, :], H[:, a, :], MOD[:, shift, :], ALU.add), ready, a + 1)

            def add_gated_norm(src, gate, semaphore, value):
                for a in range(NT):
                    dve.wait_ge(semaphore, value - (NT - 1 - a))
                    moments(src[:, a, :], a)
                inverse_roots(NT, 1e-6, square=True)
                for a in range(NT):
                    step(dve.scalar_tensor_tensor(src[:, a, :], src[:, a, :], rstd[:, a:a + 1], MOD[:, gate, :], ALU.mult, ALU.mult))
                    step(dve.tensor_tensor(X[:, a, :], X[:, a, :], src[:, a, :], ALU.add))

            def add_gated(src, gate):
                step(dve.tensor_tensor(src[:, :, :], src[:, :, :], both(MOD[:, gate, :]), ALU.mult))
                step(dve.tensor_tensor(X[:, :, :], X[:, :, :], src[:, :, :], ALU.add))

            def center_scale(dst, src, i):
                step(dve.tensor_scalar(dst, src, moment[:, 2 * i:2 * i + 1], rstd[:, i:i + 1], ALU.subtract, ALU.mult))

            def add_layer_norm(src, ready):
                for a in range(NT):
                    dve.wait_ge(product_free, ready[a])
                    step(dve.scalar_tensor_tensor(X[:, a, :], X[:, a, :], 2.0 ** 0.25, src[:, a, :], ALU.mult, ALU.add))
                    moments(X[:, a, :], a)
                inverse_roots(NT, 1e-5)
                g = vector()
                for a in range(NT):
                    ins = dve.scalar_tensor_tensor(X[:, a, :], X[:, a, :], moment[:, 2 * a:2 * a + 1], g, ALU.subtract, ALU.mult)
                    step(ins) if a == 0 else vector_done(ins)
                g = vector()
                for a in range(NT):
                    ins = dve.scalar_tensor_tensor(X[:, a, :], X[:, a, :], rstd[:, a:a + 1], g, ALU.mult, ALU.add)
                    step(ins) if a == 0 else vector_done(ins)

            scale_of = {"window": 0.125, "cmp": 0.125, "sel": 0.125, "win": 0.125, "moba": 0.125, "mla": 192.0 ** -0.5}

            def shift(u):
                kind, t, grp, nk, _ = units[u]
                st = att_stat[u % 2]
                dve.wait_ge(att["scores"], u + 1)
                if u >= 1:
                    dve.wait_ge(att["probs"], u)
                for pair in range(2):
                    ins = dve.scalar_tensor_tensor(
                        sS[:, 2 * pair:2 * pair + 2, 0:nk], ps[:, 4 + pair, 0:2 * nk].rearrange("p (h n) -> p h n", h=2),
                        scale_of[kind], bias_of(u, pair), ALU.mult, ALU.add)
                    if pair == 0:
                        step(ins)
                tell(ins, att["scores_read"], u + 1)
                step(dve.tensor_reduce(st["max"], sS[:, :, 0:nk], AX.X, ALU.max))
                if kind == "window":
                    sink = sinks[:, 4 * grp:4 * grp + 4]
                    step(dve.tensor_tensor(st["max"], st["max"], sink, ALU.max))
                    step(dve.tensor_tensor(st["sink"], sink, st["max"], ALU.subtract))
                tell(dve.tensor_scalar(st["shift"], st["max"], FLOOR, -1.0, ALU.max, ALU.mult), att["shift"], u + 1)

            def finish(u):
                kind, t, grp, nk, width = units[u]
                st = att_stat[u % 2]
                dve.wait_ge(att["probs"], u + 1)
                if kind == "window":
                    step(dve.tensor_tensor(st["sum"], st["sum"], st["sink"], ALU.add))
                else:
                    step(dve.tensor_scalar(st["sum"], st["sum"], 1e-30, None, ALU.max))
                step(dve.reciprocal(st["inv"], st["sum"]))
                if kind in ("cmp", "sel", "win"):
                    branch = ("cmp", "sel", "win").index(kind)
                    step(dve.tensor_tensor(st["inv"], st["inv"], GN[:, t, branch:12:3], ALU.mult))
                dve.wait_ge(att["out"], u + 1)
                o = ps[:, 3, 0:4 * width].rearrange("p (h d) -> p h d", h=4)
                at = {"window": 256 * grp, "moba": 256, "mla": 512 * grp}.get(kind, 0)
                dst = Y[:, t, at:at + 4 * width].rearrange("p (h d) -> p h d", h=4)
                add = kind in ("sel", "win")
                tell(dve.tensor_tensor(ONSA if add else dst, o, st["inv"].unsqueeze(2).to_broadcast([P, 4, width]), ALU.mult),
                     att["out_read"], u + 1)
                if add:
                    step(dve.tensor_tensor(dst, dst, ONSA, ALU.add))

            def attention(u0, u1, between=lambda i: None):
                shift(u0)
                for u in range(u0, u1):
                    if u + 1 < u1:
                        shift(u + 1)
                    between(u - u0)
                    finish(u)

            def within_blocks(n, q, k, cum, LDb):
                c5 = cum.rearrange("p c (b t j) -> p c b t j", t=NPART, j=PART)
                q4, k4 = (x.rearrange("p c (b i) -> p c b i", i=BLK) for x in (q, k))
                before_part = [KS[:, b - 1].rearrange("p c (b i) -> p c b i", i=BLK)[:, :, :, 0:PART * b] for b in range(1, NPART)]
                c4 = cum.rearrange("p c (b i) -> p c b i", i=BLK)
                shape = [P, PART, S // PART, PART]

                def later(x, pair):
                    return x[:, pair, :].rearrange("p (g i) -> p i g", i=PART).unsqueeze(3).to_broadcast(shape)

                def earlier(x, pair):
                    return x[:, pair, :].unsqueeze(1).to_broadcast([P, PART, S])

                ld4 = [LDb[:, pair].rearrange("p i (g s) -> p i g s", s=PART) for pair in range(2)]

                def parts_before():
                    for pair in range(2):
                        v = c5[:, pair].rearrange("p b t j -> p t b j")
                        step(dve.tensor_tensor(LQS[:, pair], v[:, 1:], v[:, 0:NPART - 1, :, PART - 1:].to_broadcast([P, 3, NBLK, PART]),
                                               ALU.subtract))
                    step(dve.memset(KS, 0.0))
                    for b in range(1, NPART):
                        step(dve.tensor_tensor(before_part[b - 1], c4[:, :, :, PART * b - 1:PART * b].to_broadcast([P, 2, NBLK, PART * b]),
                                               c4[:, :, :, 0:PART * b], ALU.subtract))

                def within_part():
                    for pair in range(2):
                        step(dve.tensor_tensor(ld4[pair], later(cum, pair), earlier(cum, pair).rearrange("p i (g s) -> p i g s", s=PART),
                                               ALU.subtract))
                    tell(dve.tensor_scalar(LDb, LDb, 0.0, None, ALU.min), lin["ddiff"], n + 1)

                def weigh_parts_before():
                    step(dve.memset(QS, 0.0))
                    dve.wait_ge(lin["dexp"], n + 1)
                    for h in range(2):
                        for pair in range(2):
                            rows_ = slice(64 * h, 64 * h + 64)
                            qs = QS[rows_, pair, :, h, :].rearrange("p t (b j) -> p t b j", j=PART)
                            qb = q4[rows_, pair].rearrange("p b (t j) -> p t b j", j=PART)[:, 1:]
                            step(dve.tensor_tensor(qs, qb, LQS[rows_, pair], ALU.mult))
                    for b in range(1, NPART):
                        ins = dve.tensor_tensor(before_part[b - 1], before_part[b - 1], k4[:, :, :, 0:PART * b], ALU.mult)
                        step(ins) if b < NPART - 1 else tell(ins, lin["sub"], n + 1)

                def weigh_within_part():
                    for pair in range(2):
                        step(dve.tensor_tensor(ld4[pair], ld4[pair], later(q, pair), ALU.mult))
                        ins = dve.tensor_tensor(LDb[:, pair], LDb[:, pair], earlier(k, pair), ALU.mult)
                        step(ins) if pair == 0 else tell(ins, lin["diag"], n + 1)

                return parts_before, within_part, weigh_parts_before, weigh_within_part

            def queries_decay(n, cum, LQb):
                c4 = cum.rearrange("p c (b i) -> p c b i", i=BLK)
                step(dve.tensor_copy(LQb[:, :, 0, :], c4[:, :, 0, :]))
                for pair in range(2):
                    ins = dve.tensor_tensor(LQb[:, pair, 1:, :], c4[:, pair, 1:, :],
                                            c4[:, pair, 0:NBLK - 1, BLK - 1:BLK].to_broadcast([P, NBLK - 1, BLK]), ALU.subtract)
                    if pair == 0:
                        step(ins)
                tell(ins, lin["qdiff"], n + 1)

            def linear_attention(n, q, k, LQb, KDb, AT):
                q4 = q.rearrange("p c (b i) -> p c b i", i=BLK)
                if n == 0:
                    dve.wait_ge(lin["diag_used"], n + 1)
                for i in range(2):
                    step(dve.memset(KDb[:, i, :, :], 0.0))
                dve.wait_ge(lin["qexp"], n + 1)
                for h in range(2):
                    for pair in range(2):
                        rows_ = slice(64 * h, 64 * h + 64)
                        ins = dve.tensor_tensor(QD[rows_, pair, :, h, :], q4[rows_, pair, :, :], LQb[rows_, pair, :, :], ALU.mult)
                        if h + pair < 2:
                            step(ins)
                tell(ins, lin["queries"], n + 1)
                dve.sem_inc(lin["keys"], 1)
                for i in range(1, NBLK):
                    dve.wait_ge(lin["kexp"], (NBLK - 1) * n + i)
                    kd = KDb[:, i % 2, :, 0:BLK * i]
                    dve.tensor_tensor(kd, kd, k[:, :, 0:BLK * i], ALU.mult).then_inc(lin["keys"], 1)
                dve.wait_ge(lin["keys_used"], NBLK * (n + 1))
                dve.wait_ge(lin["diag_used"], n + 1)
                for tile in range(NT):
                    a = AT[tile][:, :, 0:P]
                    shape = [P, 4, P // PART, PART]
                    step(dve.tensor_tensor(a.rearrange("p h (g j) -> p h g j", j=PART), lin_diag[:, tile].unsqueeze(2).to_broadcast(shape),
                                           diag.rearrange("p (g j) -> p g j", j=PART).unsqueeze(1).to_broadcast(shape), ALU.mult))
                    a5 = a.rearrange("p h (b t j) -> p t h b j", t=NPART, j=PART)
                    for b in range(1, NPART):
                        step(dve.tensor_tensor(OFFS, lin_off(b, tile).rearrange("p (h b j) -> p h b j", h=4, j=PART),
                                               same[:, :].unsqueeze(1).unsqueeze(3).to_broadcast([P, 4, P // BLK, PART]), ALU.mult))
                        step(dve.tensor_tensor(a5[:, b], a5[:, b], OFFS, ALU.add))
                for pair in range(2):
                    o = ps[:, 4 + pair, :].rearrange("p (h t) -> p h t", h=2)
                    a = AT[0][:, 2 * pair:2 * pair + 2, :]
                    step(dve.tensor_tensor(a[:, :, 0:P], a[:, :, 0:P], o[:, :, 0:P], ALU.add))
                    step(dve.tensor_copy(a[:, :, P:S], o[:, :, P:S]))
                tell(dve.tensor_tensor(AT[1], AT[1], ps[:, 6, :].rearrange("p (h t) -> p h t", h=4), ALU.add),
                     lin["merged"], n + 1)

            def log_sigmoid_sums(n, z, part, cum, factor):
                dve.wait_ge(loglog_ready, n)
                for c in range(2):
                    ins = dve.scalar_tensor_tensor(part[:, c, :], z[:, c, :], 0.0, part[:, c, :], ALU.min, ALU.subtract)
                    if c == 0:
                        step(ins)
                tell(ins, log_ready, 1) if n == 2 else step(ins)
                if factor != 1.0:
                    step(dve.tensor_scalar(part, part, factor, None, ALU.mult))
                for c in range(2):
                    step(dve.tensor_tensor_scan(cum[:, c, :], ones[:, :], part[:, c, :], 0.0, ALU.mult, ALU.add))

            def head_rms(o, width, n0=0):
                for a in range(NT):
                    for h in range(4):
                        moments(o[:, a, width * h:width * (h + 1)], 4 * a + h)
                inverse_roots(8, 1e-6, square=True)

            def ranks(dst, v, groups, n, c1, c2, order):
                shape = [P, groups, n, n] if groups > 1 else [P, n, n]
                ax = 2 if groups > 1 else 1
                other, own = v.unsqueeze(ax).to_broadcast(shape), v.unsqueeze(ax + 1).to_broadcast(shape)
                o = order[:, 0:n, 0:n]
                if groups > 1:
                    o = o.unsqueeze(1).to_broadcast(shape)
                step(dve.tensor_tensor(c1, other, own, ALU.is_gt))
                step(dve.tensor_tensor(c2, other, own, ALU.is_equal))
                step(dve.tensor_tensor(c2, c2, o, ALU.mult))
                step(dve.tensor_tensor(c1, c1, c2, ALU.add))
                step(dve.tensor_reduce(dst, c1, AX.X, ALU.add))

            dve.wait_ge(x_landed, 16)

            def first_scale():
                dve.wait_ge(product_free, end["ada1a"])
                gain_scale(1)

            rms_modulate(X, 0, 1, h1_ready, first_scale)
            dve.wait_ge(consts_landed, 16 * n_consts)
            dve.wait_ge(zeros_ready, 5)
            log_sigmoid_sums(1, GZ, GL[:, :, :], CUM, 1.0 / 16.0)
            pieces = within_blocks(0, GQ[:, :, :], GK[:, :, :], CUM[:, :, :], GLA_LD)
            attention(0, n_window, lambda i: pieces[i]())
            queries_decay(0, CUM[:, :, :], LQ)
            linear_attention(0, GQ[:, :, :], GK[:, :, :], LQ, GLA_KD, GLA_AT)
            dve.wait_ge(lin["read"], 2)
            o = Y[:, :, BANK:]
            head_rms(o, P)
            for a in range(NT):
                for h in range(4):
                    oh = o[:, a, P * h:P * (h + 1)]
                    step(dve.scalar_tensor_tensor(oh, oh, rstd[:, 4 * a + h:4 * a + h + 1], gla_norm, ALU.mult, ALU.mult))
            tell(dve.tensor_tensor(o, o, GG[:, :, :], ALU.mult), mix_ready, 1)
            dve.wait_ge(product_free, end["ada1b"])
            gain_gate(2)
            gain_scale(4)
            add_gated_norm(H, 2, product_free, end["out1"])
            rms_modulate(X, 3, 4, h2_ready)
            dve.wait_ge(moe1_params_landed, 32)
            dve.wait_ge(product_free, end["route1"])
            step(dve.tensor_tensor(LG[:, :, :], LG[:, :, :], both(b_router), ALU.add))
            for a in range(NT):
                ranks(GT[:, a, :], LG[:, a, :], 1, E1, cmp1, cmp2, before)
                step(dve.tensor_reduce(moment[:, a:a + 1], LG[:, a, :], AX.X, ALU.max))
                step(dve.tensor_scalar(LX[:, a, :], LG[:, a, :], moment[:, a:a + 1], None, ALU.subtract))
            tell(dve.tensor_scalar(MASK[:, :, :], GT[:, :, :], float(TOP1), None, ALU.is_lt), route_shift, 1)
            dve.wait_ge(route_exp, 1)
            step(dve.tensor_tensor(GT[:, :, :], MASK[:, :, :], LX[:, :, :], ALU.mult))
            step(dve.tensor_reduce(moment[:, 0:NT], GT[:, :, :], AX.X, ALU.add))
            step(dve.reciprocal(moment[:, 2:2 + NT], moment[:, 0:NT]))
            tell(dve.tensor_tensor(GT[:, :, :], GT[:, :, :], moment[:, 2:2 + NT].unsqueeze(2).to_broadcast([P, NT, E1]),
                                   ALU.mult), gates_ready, 1)

            slots = iota[:, 0:C1]

            def pick(n, astep):
                astep(dve.tensor_copy(rcur, RANK[:, :, n]))
                astep(dve.tensor_scalar(PICK[:, 0, :], slots, rcur[:, 0:1], None, ALU.is_equal))
                tell(dve.tensor_scalar(PICK[:, 1, :], slots, rcur[:, 1:2], None, ALU.is_equal), m1["pick"], n + 1)

            def pick_back(n, astep):
                astep(dve.tensor_copy(rcur2, RANK[:, :, n]))
                astep(dve.tensor_copy(gcur, GATE[:, :, n]))
                for a in range(NT):
                    ins = dve.tensor_scalar(PICKG[:, a, :, :], slots.unsqueeze(1).to_broadcast([P, 2, C1]), rcur2[:, a:a + 1],
                                            gcur[:, a:a + 1], ALU.is_equal, ALU.mult)
                    if a == 0:
                        astep(ins)
                tell(ins, m1["pick_back"], n + 1)

            far = 65536.0
            dve.wait_ge(product_free, end["rank1"])
            place = MASKED[:, 0:NT * E1].rearrange("p (a e) -> p a e", a=NT)
            count = MASKED[:, NT * E1:]
            step(dve.memset(RANK[:, :, :], -1.0))
            step(dve.memset(GATE[:, :, :], 0.0))
            step(dve.tensor_copy(GATE[:, :, 0:1], GT[:, :, 0:1]))
            step(dve.scalar_tensor_tensor(EPLACE, place, far, MASK[:, :, :], ALU.add, ALU.mult))
            step(dve.tensor_scalar(RANK[:, :, 0:1], EPLACE[:, :, 0:1], -far, None, ALU.add))
            pick(0, step)
            step(dve.tensor_scalar(EPASS, count, float(C1), 1.0, ALU.is_gt, ALU.add))
            for r in range(2, -(-S // C1)):
                step(dve.scalar_tensor_tensor(EPASS, count, float(C1 * r), EPASS, ALU.is_gt, ALU.add))
            through = WORK[:, THROUGH:THROUGH + E1]
            step(dve.tensor_tensor_scan(through, ones[:, 0:E1], EPASS, 0.0, ALU.mult, ALU.add))
            step(dve.tensor_copy(WORK[:, 0:1], through[:, E1 - 1:]))
            tell(dve.tensor_copy(work[:, 0:OF_PASS], WORK[:, 0:OF_PASS]), m1["counted"], 1)
            step(dve.tensor_tensor(ESTART, through, EPASS, ALU.subtract))
            shape = [P, PASSES // 2, E1]
            halves = [slice(0, PASSES // 2), slice(PASSES // 2, PASSES)]
            for half in halves:
                number = iota[:, half].unsqueeze(2).to_broadcast(shape)
                step(dve.tensor_tensor(SEL[:, half], number, ESTART.unsqueeze(1).to_broadcast(shape), ALU.is_ge))
                step(dve.tensor_tensor(PROD, number, through.unsqueeze(1).to_broadcast(shape), ALU.is_lt))
                step(dve.tensor_tensor(SEL[:, half], SEL[:, half], PROD, ALU.mult))

            def selected(dst, v):
                for half in halves:
                    step(dve.tensor_tensor(PROD, SEL[:, half], v.unsqueeze(1).to_broadcast(shape), ALU.mult))
                    step(dve.tensor_reduce(dst[:, half], PROD, AX.X, ALU.add))

            selected(WORK[:, OF_PASS:OF_PASS + PASSES], iota[:, 0:E1])
            step(dve.tensor_scalar(EPLACE, EPLACE, -far, None, ALU.add))
            for a in range(NT):
                step(dve.scalar_tensor_tensor(EPLACE[:, a, :], ESTART, float(C1), EPLACE[:, a, :], ALU.mult, ALU.add))
                selected(RANK[:, a, 0:PASSES], EPLACE[:, a, :])
                step(dve.scalar_tensor_tensor(RANK[:, a, 0:PASSES], iota[:, 0:PASSES], -float(C1), RANK[:, a, 0:PASSES],
                                              ALU.mult, ALU.add))
                selected(GATE[:, a, 0:PASSES], GT[:, a, :])
            tell(dve.tensor_copy(work[:, OF_PASS:ROUNDS3], WORK[:, OF_PASS:]), m1["listed"], 1)

            def expert_pass(n):
                own = [0]

                def astep(ins):
                    own[0] += 1
                    ins.then_inc(m1["step"], 1)
                    dve.wait_ge(m1["step"], EXPERT_STEPS * n + own[0])

                dve.wait_ge(m1["gather"], n + 1)
                pick(n + 1, astep)
                if not (isinstance(n, int) and n == 0):
                    dve.wait_ge(m1["back"], n)
                pick_back(n, astep)
                for b in range(2):
                    dve.wait_ge(m1_up[b], n + 1)
                    tell(dve.tensor_scalar(glu[:, b, :], ps[:, b, 0:BANK:2], 7.0, None, ALU.min), m1["glu"], 2 * n + b + 1)
                    tell(dve.tensor_scalar(lin1[:, b, :], ps[:, b, 1:BANK:2], 7.0, -7.0, ALU.min, ALU.max), m1["up_read"],
                         2 * n + b + 1)
                    dve.wait_ge(m1["sig"], 2 * n + b + 1)
                    astep(dve.tensor_tensor(sig[:, b, :], sig[:, b, :], glu[:, b, :], ALU.mult))
                    tell(dve.scalar_tensor_tensor(aS[:, b, :], lin1[:, b, :], 1.0, sig[:, b, :], ALU.add, ALU.mult),
                         m1["hidden"], 2 * n + b + 1)
                assert own[0] == EXPERT_STEPS, own[0]

            expert_pass(0)
            n_passes = dve.value_load(work[0:1, 0:1], min_val=E1, max_val=PASSES)
            with dve.Fori(1, n_passes) as n:
                expert_pass(n)
            gain_gate(5)
            add_gated_norm(Y, 5, m1["sum_read"], NT)
            dve.sem_inc(x1_ready, 1)
            dve.wait_ge(product_free, end["in2"])
            step(dve.memset(CMID, 0.0))
            kct = KCT.rearrange("p a (m q r) -> p a q m r", q=8, r=2)
            for kv in range(2):
                for r in range(2):
                    for jh in range(2):
                        hs = slice(64 * r, 64 * r + 64)
                        ins = dve.tensor_tensor(
                            BLOCKS[hs, kv, 8 * jh:8 * jh + 8, :], kct[hs, kv, :, jh:jh + NCMP, r],
                            cmp_pe[hs, kv, 8 * jh:8 * jh + 8].unsqueeze(2).to_broadcast([64, 8, NCMP]), ALU.add)
                        if kv + r + jh < 3:
                            step(ins)
            tell(ins, blocks_ready, 1)
            step(dve.memset(CA[:, :, 0:CONVW - 1], 0.0))
            tell(dve.tensor_tensor(CA[:, :, CONVW - 1:], CA[:, :, CONVW - 1:], CG[:, :, :], ALU.mult), conv_gated, 1)
            for c in range(2):
                step(dve.tensor_scalar(CACC[:, c, :], CA[:, c, 0:S], convw[:, c, 0:1], conv_bias[:, c:c + 1], ALU.mult, ALU.add))

            log_sigmoid_sums(2, FH, HLOG[:, :, :], HCUM, 1.0)

            def taps(i):
                each = -(-(CONVW - 1) // n_nsa)
                for k in range(1 + each * i, min(CONVW, 1 + each * (i + 1))):
                    for c in range(2):
                        ins = dve.scalar_tensor_tensor(CACC[:, c, :], CA[:, c, k:k + S], convw[:, c, k:k + 1], CACC[:, c, :],
                                                       ALU.mult, ALU.add)
                        if k + c < CONVW:
                            step(ins)
                        else:
                            tell(ins, conv_ready, 1)

            attention(n_window, n_window + n_nsa, taps)
            parts_before, within_part, weigh_parts_before, weigh_within_part = within_blocks(
                1, QH[:, :, :], FH[:, :, :], HCUM[:, :, :], HG_LD)
            parts_before()
            within_part()
            queries_decay(1, HCUM[:, :, :], LQ2)
            dve.wait_ge(product_free, end["convT"])
            for a in range(NT):
                moments(CTOK[:, a, :], a)
            inverse_roots(NT, 1e-5)
            for a in range(NT):
                center_scale(CTOK[:, a, :], CTOK[:, a, :], a)
            step(dve.tensor_tensor(CTOK[:, :, :], CTOK[:, :, :], both(conv_g), ALU.mult))
            tell(dve.tensor_tensor(CTOK[:, :, :], CTOK[:, :, :], both(conv_b), ALU.add), convln_ready, 1)
            dve.wait_ge(keep_ready, 1)
            weigh_parts_before()
            weigh_within_part()
            linear_attention(1, QH[:, :, :], FH[:, :, :], LQ2, HG_KD, HG_AT)
            dve.wait_ge(lin["read"], 4)
            o = Y[:, :, 768:]
            head_rms(o, 64)
            for a in range(NT):
                oa = o[:, a, :].rearrange("p (h d) -> p h d", h=4)
                step(dve.tensor_tensor(oa, oa, rstd[:, 4 * a:4 * a + 4].unsqueeze(2).to_broadcast([P, 4, 64]), ALU.mult))
            step(dve.tensor_tensor(o, o, both(hgrn_g), ALU.mult))
            tell(dve.tensor_tensor(o, o, GH[:, :, :], ALU.mult), mix_ready, 2)
            add_layer_norm(H, (end["out2"] - 1, end["out2"]))
            dve.sem_inc(y2_ready, 1)
            for i in range(16):
                dve.wait_ge(product_free, end["y2T"] + i + 1)
                f = FFT[:, 2 * i:2 * i + 2, :]
                dve.tensor_tensor(f, f, f, ALU.mult).then_inc(relu_ready, 1)
            dve.wait_ge(product_free, end["ada3"])
            gain_scale(1)
            add_layer_norm(H, (end["ff2"], end["ff2"]))
            rms_modulate(X, 0, 1, u1_ready)
            dve.wait_ge(tables_landed, 32)
            for i, r in enumerate((RQ, RK)):
                dve.wait_ge(product_free, end["u1T"] + 4 * (i + 1))
                x1, x2 = r[:, 0:8:2, :], r[:, 1:8:2, :]
                cos, sin = (ropes[:, i, :].unsqueeze(1).to_broadcast([P, 4, S]) for i in range(2))
                step(dve.tensor_tensor(RTMP[:, 0], x1, sin, ALU.mult))
                step(dve.tensor_tensor(RTMP[:, 1], x2, sin, ALU.mult))
                step(dve.tensor_tensor(x1, x1, cos, ALU.mult))
                step(dve.tensor_tensor(x2, x2, cos, ALU.mult))
                step(dve.tensor_tensor(x1, x1, RTMP[:, 1], ALU.subtract))
                ins = dve.tensor_tensor(x2, x2, RTMP[:, 0], ALU.add)
                step(ins) if r is RQ else tell(ins, rope_ready, 1)
            dve.wait_ge(product_free, end["in3"])
            step(dve.tensor_tensor(KPE[:, 0, :], KPE[:, 0, :], ropes[:, 2, :], ALU.mult))
            step(dve.tensor_tensor(KPE[:, 1, :], KPE[:, 1, :], ropes[:, 3, :], ALU.mult))
            for h in range(2):
                hs = slice(64 * h, 64 * h + 64)
                step(dve.tensor_tensor(BD[hs, 0, h, :], KPE[hs, 0, :], KPE[hs, 1, :], ALU.add))
            for a in range(NT):
                moments(CQ[:, a, :], 2 * a)
                moments(CKV[:, a, :], 2 * a + 1)
            inverse_roots(4, 1e-6, square=True)
            for a in range(NT):
                step(dve.scalar_tensor_tensor(CQ[:, a, :], CQ[:, a, :], rstd[:, 2 * a:2 * a + 1], qn_row, ALU.mult, ALU.mult))
                ins = dve.scalar_tensor_tensor(CKV[:, a, :], CKV[:, a, :], rstd[:, 2 * a + 1:2 * a + 2], kvn_row, ALU.mult, ALU.mult)
                if a == 0:
                    step(ins)
            tell(ins, cq_ready, 1)
            for h in range(4):
                dve.wait_ge(ret_scores, h + 1)
                b = ps[:, 4 + h % 2, :]
                step(dve.tensor_tensor(RT[:, h, 0, :], b[:, 0:S], decay[:, h, :], ALU.mult))
                tell(dve.tensor_tensor(RT[:, h, 1, P:S], b[:, S:S + P], decay[:, h, 0:P], ALU.mult), ret_decayed, h + 1)
            dve.wait_ge(ret_copied, 4)
            for a in range(NT):
                for h in range(4):
                    moments(Y[:, a, S * h:S * (h + 1)], 4 * a + h)
            inverse_roots(8, 1e-6)
            for a in range(NT):
                for h in range(4):
                    yh = Y[:, a, S * h:S * (h + 1)]
                    center_scale(yh, yh, 4 * a + h)
            tell(dve.tensor_tensor(Y[:, :, :], Y[:, :, :], RG[:, :, :], ALU.mult), ret_ready, 1)
            dve.wait_ge(product_free, end["reto"])
            tell(dve.tensor_tensor(H[:, :, :], H[:, :, :], MG1[:, :, :], ALU.mult), ret_gated, 1)
            dve.wait_ge(product_free, end["uq"])
            for j in range(2):
                step(dve.tensor_tensor(QPE[:, j, :, :], QPE[:, j, :, :],
                                       ropes[:, 2 + j, :].unsqueeze(1).to_broadcast([P, 4, S]), ALU.mult))
            tell(dve.tensor_tensor(QPE[:, 0, :, :], QPE[:, 0, :, :], QPE[:, 1, :, :], ALU.add), mlarope_ready, 1)
            attention(n_window + n_nsa, len(units))
            dve.sem_inc(mla_ready, 1)
            dve.wait_ge(product_free, end["mlao"])
            step(dve.tensor_tensor(YM[:, :, :], YM[:, :, :], MG2[:, :, :], ALU.mult))
            tell(dve.tensor_tensor(H[:, :, :], H[:, :, :], YM[:, :, :], ALU.add), merge_ready, 1)
            gain_scale(4)
            dve.wait_ge(product_free, end["out3"])
            add_gated(H, 2)
            rms_modulate(X, 3, 4, u2_ready)
            dve.wait_ge(before_landed, 16)
            dve.wait_ge(product_free, end["route3"])
            step(dve.tensor_tensor(LR[:, :, :], LR[:, :, :], both(b_route3), ALU.add))
            GSEL, ESEL, GMAX = moment[:, 0:8], GE, moment[:, 8:24]
            for a in range(NT):
                grp, exp = LR[:, a, 0:G3], LR[:, a, G3:].rearrange("p (g e) -> p g e", g=G3)
                ranks(GSEL[:, G3 * a:G3 * (a + 1)], grp, 1, G3, cmp3[:, 0, 0:G3, 0:G3], cmp4[:, 0, 0:G3, 0:G3], before3)
                ranks(GE[:, a, :].rearrange("p (g e) -> p g e", g=G3), exp, G3, PG3, cmp3, cmp4, before3)
                step(dve.tensor_reduce(GMAX[:, 8 * a:8 * a + 1], grp, AX.X, ALU.max))
                step(dve.tensor_reduce(GMAX[:, 8 * a + 4:8 * a + 8], exp, AX.X, ALU.max))
                step(dve.tensor_scalar(LE[:, a, 0:G3], grp, GMAX[:, 8 * a:8 * a + 1], None, ALU.subtract))
                step(dve.tensor_tensor(LE[:, a, G3:].rearrange("p (g e) -> p g e", g=G3), exp,
                                       GMAX[:, 8 * a + 4:8 * a + 8].unsqueeze(2).to_broadcast([P, G3, PG3]), ALU.subtract))
            step(dve.tensor_scalar(GSEL, GSEL, 1.0, None, ALU.is_lt))
            tell(dve.tensor_scalar(GE[:, :, :], GE[:, :, :], float(TOP3), None, ALU.is_lt), route_shift, 2)
            dve.wait_ge(route_exp, 2)
            for a in range(NT):
                e8 = GE[:, a, :].rearrange("p (g e) -> p g e", g=G3)
                step(dve.tensor_reduce(GMAX[:, 0:1], LE[:, a, 0:G3], AX.X, ALU.add))
                step(dve.reciprocal(GMAX[:, 1:2], GMAX[:, 0:1]))
                step(dve.scalar_tensor_tensor(GMAX[:, 4:8], LE[:, a, 0:G3], GMAX[:, 1:2], GSEL[:, G3 * a:G3 * (a + 1)],
                                              ALU.mult, ALU.mult))
                step(dve.tensor_tensor(GE[:, a, :], GE[:, a, :], LE[:, a, G3:], ALU.mult))
                step(dve.tensor_reduce(GMAX[:, 8:12], e8, AX.X, ALU.add))
                step(dve.reciprocal(GMAX[:, 12:16], GMAX[:, 8:12]))
                step(dve.tensor_tensor(GMAX[:, 4:8], GMAX[:, 4:8], GMAX[:, 12:16], ALU.mult))
                step(dve.tensor_tensor(e8, e8, GMAX[:, 4:8].unsqueeze(2).to_broadcast([P, G3, PG3]), ALU.mult))
            def passes(rank, mask, counted, groups, column, ready):
                step(dve.memset(rank, -1.0))
                r0 = counted[:, 0:NT * groups].rearrange("p (a e) -> p a e", a=NT)
                step(dve.scalar_tensor_tensor(r0, r0, 1.0, mask, ALU.add, ALU.mult))
                for r in range(ROUNDS):
                    step(dve.tensor_scalar(rank[:, :, groups * r:groups * (r + 1)], r0, -1.0 - C * r, None, ALU.add))
                step(dve.tensor_reduce(moment[:, 0:1], counted[:, NT * groups:(NT + 1) * groups], AX.X, ALU.max))
                step(dve.tensor_scalar(moment[:, 1:2], moment[:, 0:1], float(C), 1.0, ALU.is_gt, ALU.add))
                for r in range(2, ROUNDS):
                    step(dve.tensor_scalar(moment[:, 2:3], moment[:, 0:1], float(C * r), None, ALU.is_gt))
                    step(dve.tensor_tensor(moment[:, 1:2], moment[:, 1:2], moment[:, 2:3], ALU.add))
                step(dve.tensor_copy(work[:, column:column + 1], moment[:, 1:2]))
                dve.sem_inc(ready, 1)
                return dve.value_load(work[0:1, column:column + 1], min_val=1, max_val=ROUNDS)

            step(dve.memset(zero_row, 0.0))
            step(dve.memset(GE3, 0.0))
            for r in range(ROUNDS):
                step(dve.tensor_copy(GE3[:, :, E3 * r:E3 * (r + 1)], GE[:, :, :]))
            tell(dve.tensor_copy(MASK3[:, :, :], GSEL.rearrange("p (a g) -> p a g", a=NT)), m3["zero"], 1)
            dve.wait_ge(product_free, end["rank3"])
            for r in range(ROUNDS):
                step(dve.tensor_copy(work[:, FOUR_OF + E3 // 4 * r:FOUR_OF + E3 // 4 * (r + 1)], iota[:, 0:E3 // 4]))
            n_rounds = passes(RANK3[:, :, :], MASK3[:, :, :], MASKED3, G3, ROUNDS3, m3["rounds"])
            n_groups = G3 * n_rounds

            def group_step(n, i, ins):
                ins.then_inc(m3["step"], 1)
                dve.wait_ge(m3["step"], GROUP_STEPS * n + i)

            def pick(n, before, own):
                group_step(before, own, dve.tensor_copy(rcur3, RANK3[:, :, n]))
                for a in range(NT):
                    ins = dve.tensor_scalar(PICK3[:, a, :].rearrange("p (x c) -> p x c", x=2),
                                            iota.unsqueeze(1).to_broadcast([P, 2, C]), rcur3[:, a:a + 1], None, ALU.is_equal)
                    group_step(before, own + 1, ins) if a == 0 else tell(ins, m3["pick"], n + 1)

            def pick_back(n, before, own):
                group_step(before, own, dve.tensor_copy(rcurb, RANK3[:, :, n]))
                for a in range(NT):
                    ins = dve.tensor_scalar(PICKB[:, a, :], iota, rcurb[:, a:a + 1], None, ALU.is_equal)
                    group_step(before, own + 1, ins) if a == 0 else tell(ins, m3["pick_back"], n + 1)

            def group_pass(n, first=False):
                dve.wait_ge(m3["gather_read"], 2 * n + 1)
                for t in range(JOBS):
                    for s in range(SUBS):
                        rows_, e = slice(32 * t, 32 * (t + 1)), (JOBS * s + t) // SUBS
                        ins = dve.tensor_copy(GJOB[rows_, s:TURNS:SUBS], GSUB[rows_, s, e:PG3:4])
                tell(ins, m3["gates"], n + 1)
                dve.wait_ge(m3["gather"], 2 * n + 2)
                pick(n + 1, n, 3)
                for i in range(TURNS):
                    dve.wait_ge(m3["sil"], TURNS * n + i + 1)
                    tell(dve.scalar_tensor_tensor(aS3[:, i % 2, :], ps[:, i % 2, F3:2 * F3], GJOB[:, i:i + 1], sil3[:, i % 2, :],
                                                  ALU.mult, ALU.mult), m3["hidden"], TURNS * n + i + 1)
                    if i == 1:
                        if not first:
                            dve.wait_ge(m3["back"], n)
                        pick_back(n, n, 5)

            pick(0, 0, 1)
            group_pass(0, first=True)
            with dve.Fori(1, n_groups) as n:
                group_pass(n)
            dve.wait_ge(m3["sum_read"], NT)
            add_gated(Y, 5)
            for a in range(NT):
                moments(X[:, a, :], a)
            inverse_roots(NT, 1e-6, square=True)
            g = vector()
            for a in range(NT):
                ins = dve.scalar_tensor_tensor(H[:, a, :], X[:, a, :], rstd[:, a:a + 1], g, ALU.mult, ALU.mult)
                if a == 0:
                    step(ins)
            vector_done(ins)
            dve.sem_inc(final_ready, 1)


OUT_SHAPE = (1, S, D)


def kernel(**inputs):
    import concourse.bacc as _bacc
    from concourse.bass_utils import run_bass_kernel_spmd as _run

    nc = _bacc.Bacc("TRN2", target_bir_lowering=False, num_devices=1)
    arrays, args = {}, {}
    for name, a in {**inputs, **constants()}.items():
        a = np.ascontiguousarray(a)
        arrays[f"in_{name}"] = a
        args[name] = nc.dram_tensor(f"in_{name}", a.shape, F32, kind="ExternalInput").ap()
    out = nc.dram_tensor("out_0", OUT_SHAPE, F32, kind="ExternalOutput").ap()
    rel_scratch = nc.dram_tensor("rel_scratch", (8, BANK), F32, kind="Internal").ap()
    build(nc, args, out, rel_scratch)
    r = _run(nc, [arrays], core_ids=[0])
    return r.results[0]["out_0"]
```
